# Optimizing a Trainium2 kernel written in Bass

```python
import jax, jax.numpy as jnp
from jax import lax
import numpy as np

D_MODEL = 1024
BATCH = 1
SEQ = 256
DEPTH = 2

HEAD_DIM = 64
A_HEADS = D_MODEL // 256
B_HEADS = D_MODEL // 256
C_HEADS = D_MODEL // 128
A_WIDTH = A_HEADS * HEAD_DIM
B_WIDTH = B_HEADS * HEAD_DIM
C_WIDTH = C_HEADS * HEAD_DIM
D_MIX = A_WIDTH + B_WIDTH + C_WIDTH
CHUNK = 128
LN_EPS = 1e-5
RW_DECAY_LORA = 64
RW_A_LORA = 64
RW_GATE_LORA = 128
GN_EPS = 64e-5
C_KV_GROUPS = 2
C_Q_PER_GROUP = C_HEADS // C_KV_GROUPS
C_KV_WIDTH = C_KV_GROUPS * HEAD_DIM
CMP_BLOCK = 32
CMP_STRIDE = 16
CMP_HIDDEN = 2 * HEAD_DIM
SLC_BLOCK = 64
SLC_TOPK = 16
WINDOW = 512
Q_BLOCK = 128
NEG_INF = -1e30
FORCE = 1e4
ROPE_THETA = 500000.0
ROPE_DIM = HEAD_DIM // 4
D_FF = 2816
N_EXPERTS = 8
TOP_K = 2
PLE_DIM = 256
RMS_EPS = 1e-6
N_DENSE = (DEPTH + 1) // 2
N_MOE = DEPTH // 2
A_SIZES = (A_WIDTH, A_WIDTH)
B_SIZES = (B_WIDTH, B_WIDTH, B_WIDTH, RW_DECAY_LORA, RW_A_LORA, RW_GATE_LORA)
C_SIZES = (C_WIDTH,) + (C_KV_WIDTH,) * 6 + (3 * C_HEADS,)
A_COLS = 2 * A_WIDTH
B_COLS = 3 * B_WIDTH + RW_DECAY_LORA + RW_A_LORA + RW_GATE_LORA
C_COLS = C_WIDTH + 6 * C_KV_WIDTH + 3 * C_HEADS
D_IN = A_COLS + B_COLS + C_COLS


def split_cols(z, sizes):
    out, off = [], 0
    for s in sizes:
        out.append(z[..., off:off + s])
        off += s
    return out

def rms_norm(x, g):
    xf = x.astype(jnp.float32)
    y = xf * lax.rsqrt(jnp.mean(xf * xf, axis=-1, keepdims=True) + RMS_EPS)
    return (y * g.astype(jnp.float32)).astype(x.dtype)

def layer_norm(x, g, b, eps):
    xf = x.astype(jnp.float32)
    mu = jnp.mean(xf, axis=-1, keepdims=True)
    var = jnp.mean(jnp.square(xf - mu), axis=-1, keepdims=True)
    return ((xf - mu) * lax.rsqrt(var + eps) * g.astype(jnp.float32) + b.astype(jnp.float32)).astype(x.dtype)

def rope_tables(positions):
    inv = 1.0 / (ROPE_THETA ** (jnp.arange(0, ROPE_DIM, 2, dtype=jnp.float32) / ROPE_DIM))
    ang = positions.astype(jnp.float32)[..., None] * inv
    return jnp.cos(ang), jnp.sin(ang)

def apply_partial_rope(x, cos, sin):
    bshape = cos.shape[:2] + (1,) * (x.ndim - 3) + cos.shape[-1:]
    c = cos.reshape(bshape).astype(x.dtype)
    s = sin.reshape(bshape).astype(x.dtype)
    half = ROPE_DIM // 2
    x1, x2, xp = x[..., :half], x[..., half:ROPE_DIM], x[..., ROPE_DIM:]
    return jnp.concatenate([x1 * c - x2 * s, x1 * s + x2 * c, xp], axis=-1)

def masked_softmax(s, mask):
    s32 = jnp.where(mask, s.astype(jnp.float32), NEG_INF)
    pr = jax.nn.softmax(s32, axis=-1)
    return jnp.where(mask, pr, 0.0).astype(s.dtype)

def swiglu(x, w1, w3, w2):
    return (jax.nn.silu(x @ w1) * (x @ w3)) @ w2

def chunked_spatial_gating(z_a, ln_g, ln_b, w_s, b_s):
    Bn, S, _ = z_a.shape
    nc = S // CHUNK
    u, v = split_cols(jax.nn.gelu(z_a), A_SIZES)
    u = u.reshape(Bn, nc, CHUNK, A_HEADS, HEAD_DIM)
    v = layer_norm(v.reshape(Bn, nc, CHUNK, A_HEADS, HEAD_DIM), ln_g, ln_b, LN_EPS)
    causal = jnp.tril(jnp.ones((CHUNK, CHUNK), dtype=bool))
    w = jnp.where(causal[None], w_s, 0.0).astype(v.dtype)
    mixed = jnp.einsum('hts,bnshd->bnthd', w, v) + b_s.T[None, None, :, :, None]
    return (u * mixed).reshape(Bn, S, A_WIDTH)

def rwkv7_time_mix(z_b, mu, w0, w_up, a0, a_up, g_up, k_k, k_a, r_k, gn_g, gn_b):
    Bn, S, _ = z_b.shape
    f32 = jnp.float32
    z_prev = jnp.pad(z_b[:, :-1], ((0, 0), (1, 0), (0, 0)))
    z = z_b + (z_prev - z_b) * mu
    r, k, v, wd, ad, gd = split_cols(z, B_SIZES)
    w_logit = -jax.nn.softplus(-(w0 + jnp.tanh(wd) @ w_up).astype(f32)) - 0.5
    decay = jnp.exp(-jnp.exp(w_logit))
    a = jax.nn.sigmoid((a0 + ad @ a_up).astype(f32))
    g = jax.nn.sigmoid(gd) @ g_up
    hs = lambda t: t.astype(f32).reshape(Bn, S, B_HEADS, HEAD_DIM)
    kk = hs(k * k_k)
    kk = kk * lax.rsqrt(jnp.maximum(jnp.sum(kk * kk, axis=-1, keepdims=True), 1e-24))
    k_a_h = k_a.astype(f32).reshape(B_HEADS, HEAD_DIM)
    k = hs(k) * (1.0 + (hs(a) - 1.0) * k_a_h)
    r_h, v_h, a_h, w_h = hs(r), hs(v), hs(a), hs(decay)

    def step(state, inp):
        r_t, w_t, k_t, v_t, kk_t, a_t = inp
        sa = jnp.einsum('bhvk,bhk->bhv', state, -kk_t)
        state = (state * w_t[:, :, None, :] + sa[..., None] * (kk_t * a_t)[:, :, None, :]
                 + v_t[..., None] * k_t[:, :, None, :])
        return state, jnp.einsum('bhvk,bhk->bhv', state, r_t)

    xs = tuple(jnp.moveaxis(t, 1, 0) for t in (r_h, w_h, k, v_h, kk, a_h))
    s0 = jnp.zeros((Bn, B_HEADS, HEAD_DIM, HEAD_DIM), f32)
    _, ys = lax.scan(step, s0, xs)
    y = jnp.moveaxis(ys, 0, 1)
    mu_y = jnp.mean(y, axis=-1, keepdims=True)
    var_y = jnp.mean(jnp.square(y - mu_y), axis=-1, keepdims=True)
    y = ((y - mu_y) * lax.rsqrt(var_y + GN_EPS)).reshape(Bn, S, B_WIDTH)
    y = y * gn_g.astype(f32) + gn_b.astype(f32)
    bonus = jnp.sum(r_h * k * r_k.astype(f32), axis=-1, keepdims=True) * v_h
    y = y + bonus.reshape(Bn, S, B_WIDTH)
    return (y * g.astype(f32)).astype(z_b.dtype)

def nsa_attention(z_c, cos, sin, cmp_pos, kc_w1, kc_w2, vc_w1, vc_w2):
    Bn, S, _ = z_c.shape
    G, J, Dh = C_KV_GROUPS, C_Q_PER_GROUP, HEAD_DIM
    scale = HEAD_DIM ** -0.5
    q, kc, vc, ks, vs, kw, vw, gates = split_cols(z_c, C_SIZES)
    q = q.reshape(Bn, S, G, J, Dh)
    kv = lambda t: t.reshape(Bn, S, G, Dh)
    kc, vc, ks, vs, kw, vw = map(kv, (kc, vc, ks, vs, kw, vw))
    gates = jax.nn.sigmoid(gates.astype(jnp.float32)).astype(z_c.dtype).reshape(Bn, S, G, J, 3)
    q_rot = apply_partial_rope(q, cos, sin)
    ks = apply_partial_rope(ks, cos, sin)
    kw = apply_partial_rope(kw, cos, sin)

    n_cmp = (S - CMP_BLOCK) // CMP_STRIDE + 1
    cmp_idx = np.arange(n_cmp)[:, None] * CMP_STRIDE + np.arange(CMP_BLOCK)[None, :]
    cmp_end = jnp.asarray(cmp_idx[:, -1])

    def compress(t, w1, w2):
        blk = t[:, cmp_idx] + cmp_pos[None, None, :, None, :]
        blk = blk.transpose(0, 1, 3, 2, 4).reshape(Bn, n_cmp, G, CMP_BLOCK * Dh)
        return jax.nn.gelu(blk @ w1) @ w2

    k_cmp = compress(kc, kc_w1, kc_w2)
    v_cmp = compress(vc, vc_w1, vc_w2)

    n_slc = S // SLC_BLOCK
    n_sel = min(SLC_TOPK, n_slc)
    slc_start = np.arange(n_slc) * SLC_BLOCK
    overlap = jnp.asarray(((cmp_idx[:, :1] < slc_start[None, :] + SLC_BLOCK)
                           & (cmp_idx[:, -1:] >= slc_start[None, :])).astype(np.float32))
    ks_blk = ks.reshape(Bn, n_slc, SLC_BLOCK, G, Dh).transpose(0, 3, 1, 2, 4)
    vs_blk = vs.reshape(Bn, n_slc, SLC_BLOCK, G, Dh).transpose(0, 3, 1, 2, 4)
    kw_pad = jnp.pad(kw, ((0, 0), (WINDOW, 0), (0, 0), (0, 0)))
    vw_pad = jnp.pad(vw, ((0, 0), (WINDOW, 0), (0, 0), (0, 0)))
    bi = jnp.arange(Bn)[:, None, None, None]
    gi = jnp.arange(G)[None, :, None, None]
    m_ids = jnp.arange(n_slc)

    def query_block(qb):
        start = qb * Q_BLOCK
        t = start + jnp.arange(Q_BLOCK)
        q_raw = lax.dynamic_slice_in_dim(q, start, Q_BLOCK, axis=1)
        q_r = lax.dynamic_slice_in_dim(q_rot, start, Q_BLOCK, axis=1)
        g_t = lax.dynamic_slice_in_dim(gates, start, Q_BLOCK, axis=1)
        s_c = jnp.einsum('btgjd,bngd->bgjtn', q_raw, k_cmp) * scale
        p_c = masked_softmax(s_c, cmp_end[None, :] <= t[:, None])
        o_c = jnp.einsum('bgjtn,bngd->btgjd', p_c, v_cmp)
        imp = jnp.einsum('bgjtn,nm->bgtm', p_c.astype(jnp.float32), overlap)
        blk_t = (t // SLC_BLOCK)[:, None]
        valid = m_ids[None, :] <= blk_t
        forced = (m_ids[None, :] == 0) | (m_ids[None, :] == blk_t) | (m_ids[None, :] == blk_t - 1)
        imp = jnp.where(valid, imp + FORCE * forced.astype(jnp.float32), -FORCE)
        top_v, top_i = lax.top_k(imp, n_sel)
        sel_ok = top_v > -0.5 * FORCE
        k_sel = ks_blk[bi, gi, top_i]
        v_sel = vs_blk[bi, gi, top_i]
        kpos = top_i[..., None] * SLC_BLOCK + jnp.arange(SLC_BLOCK)
        m_s = (sel_ok[..., None] & (kpos <= t[None, None, :, None, None]))
        m_s = m_s.reshape(Bn, G, 1, Q_BLOCK, n_sel * SLC_BLOCK)
        s_s = jnp.einsum('btgjd,bgtksd->bgjtks', q_r, k_sel) * scale
        p_s = masked_softmax(s_s.reshape(Bn, G, J, Q_BLOCK, n_sel * SLC_BLOCK), m_s)
        p_s = p_s.reshape(Bn, G, J, Q_BLOCK, n_sel, SLC_BLOCK)
        o_s = jnp.einsum('bgjtks,bgtksd->btgjd', p_s, v_sel)
        k_win = lax.dynamic_slice_in_dim(kw_pad, start, WINDOW + Q_BLOCK, axis=1)
        v_win = lax.dynamic_slice_in_dim(vw_pad, start, WINDOW + Q_BLOCK, axis=1)
        kpos_w = start - WINDOW + jnp.arange(WINDOW + Q_BLOCK)
        m_w = ((kpos_w[None, :] <= t[:, None]) & (kpos_w[None, :] > t[:, None] - WINDOW)
               & (kpos_w[None, :] >= 0))
        s_w = jnp.einsum('btgjd,bkgd->bgjtk', q_r, k_win) * scale
        p_w = masked_softmax(s_w, m_w)
        o_w = jnp.einsum('bgjtk,bkgd->btgjd', p_w, v_win)
        o = g_t[..., 0:1] * o_c + g_t[..., 1:2] * o_s + g_t[..., 2:3] * o_w
        return o.reshape(Bn, Q_BLOCK, C_WIDTH)

    out = lax.map(query_block, jnp.arange(S // Q_BLOCK))
    return out.transpose(1, 0, 2, 3).reshape(Bn, S, C_WIDTH)

def moe_swiglu(x, router_w, router_b, w1, w3, w2):
    logits = (x @ router_w + router_b).astype(jnp.float32)
    top_v, top_i = lax.top_k(logits, TOP_K)
    top_p = jax.nn.softmax(top_v, axis=-1)
    gate = jnp.sum(jax.nn.one_hot(top_i, N_EXPERTS, dtype=jnp.float32) * top_p[..., None], axis=-2)
    gate = gate.astype(x.dtype)
    out = jnp.zeros_like(x)
    for e in range(N_EXPERTS):
        out = out + gate[..., e:e + 1] * swiglu(x, w1[e], w3[e], w2[e])
    return out

def first_inputs(seed: int = 0) -> dict:
    key = jax.random.key(seed)
    ks = iter(jax.random.split(key, 64))
    f32 = jnp.float32

    def nrm(shape, scale):
        return scale * jax.random.normal(next(ks), shape, f32)

    def gain(shape):
        return 1.0 + 0.1 * jax.random.normal(next(ks), shape, f32)

    L = DEPTH
    x = nrm((BATCH, SEQ, D_MODEL), 1.0)
    p = nrm((DEPTH, BATCH, SEQ, PLE_DIM), 1.0)
    offset = jax.random.randint(next(ks), (BATCH, 1), 0, 1024, dtype=jnp.int32)
    positions = offset + jnp.arange(SEQ, dtype=jnp.int32)[None, :]
    return {
        "x": x, "p": p, "positions": positions,
        "g_mix": gain((L, D_MODEL)),
        "w_in": nrm((L, D_MODEL, D_IN), D_MODEL ** -0.5),
        "w_out": nrm((L, D_MIX, D_MODEL), D_MIX ** -0.5),
        "gm_ln_g": gain((L, A_HEADS, HEAD_DIM)),
        "gm_ln_b": nrm((L, A_HEADS, HEAD_DIM), 0.1),
        "gm_ws": nrm((L, A_HEADS, CHUNK, CHUNK), CHUNK ** -0.5),
        "gm_bs": gain((L, A_HEADS, CHUNK)),
        "rw_mu": jax.random.uniform(next(ks), (L, B_COLS), f32),
        "rw_w0": nrm((L, B_WIDTH), 0.5),
        "rw_w_up": nrm((L, RW_DECAY_LORA, B_WIDTH), 0.1),
        "rw_a0": nrm((L, B_WIDTH), 0.5),
        "rw_a_up": nrm((L, RW_A_LORA, B_WIDTH), RW_A_LORA ** -0.5),
        "rw_g_up": nrm((L, RW_GATE_LORA, B_WIDTH), RW_GATE_LORA ** -0.5),
        "rw_k_k": 0.85 + nrm((L, B_WIDTH), 0.1),
        "rw_k_a": gain((L, B_WIDTH)),
        "rw_r_k": nrm((L, B_HEADS, HEAD_DIM), 0.1),
        "rw_gn_g": gain((L, B_WIDTH)),
        "rw_gn_b": nrm((L, B_WIDTH), 0.1),
        "nsa_cmp_pos": nrm((L, CMP_BLOCK, HEAD_DIM), 0.1),
        "nsa_kc_w1": nrm((L, CMP_BLOCK * HEAD_DIM, CMP_HIDDEN), (CMP_BLOCK * HEAD_DIM) ** -0.5),
        "nsa_kc_w2": nrm((L, CMP_HIDDEN, HEAD_DIM), CMP_HIDDEN ** -0.5),
        "nsa_vc_w1": nrm((L, CMP_BLOCK * HEAD_DIM, CMP_HIDDEN), (CMP_BLOCK * HEAD_DIM) ** -0.5),
        "nsa_vc_w2": nrm((L, CMP_HIDDEN, HEAD_DIM), CMP_HIDDEN ** -0.5),
        "g_ffn": gain((L, D_MODEL)),
        "ffn_w1": nrm((N_DENSE, D_MODEL, D_FF), D_MODEL ** -0.5),
        "ffn_w3": nrm((N_DENSE, D_MODEL, D_FF), D_MODEL ** -0.5),
        "ffn_w2": nrm((N_DENSE, D_FF, D_MODEL), D_FF ** -0.5),
        "router_w": nrm((N_MOE, D_MODEL, N_EXPERTS), D_MODEL ** -0.5),
        "router_b": nrm((N_MOE, N_EXPERTS), 0.01),
        "moe_w1": nrm((N_MOE, N_EXPERTS, D_MODEL, D_FF), D_MODEL ** -0.5),
        "moe_w3": nrm((N_MOE, N_EXPERTS, D_MODEL, D_FF), D_MODEL ** -0.5),
        "moe_w2": nrm((N_MOE, N_EXPERTS, D_FF, D_MODEL), D_FF ** -0.5),
        "g_ple": gain((L, D_MODEL)),
        "ple_gate_w": nrm((L, D_MODEL, D_MODEL), D_MODEL ** -0.5),
        "ple_proj_w": nrm((L, PLE_DIM, D_MODEL), PLE_DIM ** -0.5),
        "g_final": gain((D_MODEL,)),
    }

def first_block(x, p, positions, g_mix, w_in, w_out, gm_ln_g, gm_ln_b, gm_ws, gm_bs,
              rw_mu, rw_w0, rw_w_up, rw_a0, rw_a_up, rw_g_up, rw_k_k, rw_k_a, rw_r_k, rw_gn_g, rw_gn_b,
              nsa_cmp_pos, nsa_kc_w1, nsa_kc_w2, nsa_vc_w1, nsa_vc_w2,
              g_ffn, ffn_w1, ffn_w3, ffn_w2, router_w, router_b, moe_w1, moe_w3, moe_w2,
              g_ple, ple_gate_w, ple_proj_w, g_final):
    cos, sin = rope_tables(positions)
    h = x
    for i in range(DEPTH):
        hn = rms_norm(h, g_mix[i])
        z = hn @ w_in[i]
        z_a, z_b, z_c = split_cols(z, (A_COLS, B_COLS, C_COLS))
        y_a = chunked_spatial_gating(z_a, gm_ln_g[i], gm_ln_b[i], gm_ws[i], gm_bs[i])
        y_b = rwkv7_time_mix(z_b, rw_mu[i], rw_w0[i], rw_w_up[i], rw_a0[i], rw_a_up[i], rw_g_up[i],
                             rw_k_k[i], rw_k_a[i], rw_r_k[i], rw_gn_g[i], rw_gn_b[i])
        y_c = nsa_attention(z_c, cos, sin, nsa_cmp_pos[i], nsa_kc_w1[i], nsa_kc_w2[i],
                            nsa_vc_w1[i], nsa_vc_w2[i])
        h = h + jnp.concatenate([y_a, y_b, y_c], axis=-1) @ w_out[i]
        hn = rms_norm(h, g_ffn[i])
        if i % 2 == 0:
            j = i // 2
            f = swiglu(hn, ffn_w1[j], ffn_w3[j], ffn_w2[j])
        else:
            j = i // 2
            f = moe_swiglu(hn, router_w[j], router_b[j], moe_w1[j], moe_w3[j], moe_w2[j])
        h = h + f
        gate = jax.nn.sigmoid(rms_norm(h, g_ple[i]) @ ple_gate_w[i])
        h = h + (p[i] @ ple_proj_w[i]) * gate
    return rms_norm(h, g_final)


N_MIXERS = 4
GROUP_WIDTH = D_MODEL // N_MIXERS
FOX_HEADS = GROUP_WIDTH // HEAD_DIM
RET_HEADS = GROUP_WIDTH // HEAD_DIM
POOL_WINDOWS = (2, 4, 8, 16)
POOL_GROUPS = len(POOL_WINDOWS)
POOL_GROUP_DIM = GROUP_WIDTH // POOL_GROUPS
CONV_WIDTH = 31
CONV_CH = GROUP_WIDTH
N_IN = 3 * GROUP_WIDTH + FOX_HEADS + GROUP_WIDTH + 4 * GROUP_WIDTH + 2 * CONV_CH
D_FF_2 = ((8 * D_MODEL + 3 * 256 - 1) // (3 * 256)) * 256
RET_CHUNK = 128
ROPE_BASE = 10000.0
EPS = 1e-6


def rmsnorm(x, g):
    xf = x.astype(jnp.float32)
    y = xf * lax.rsqrt(jnp.mean(xf * xf, axis=-1, keepdims=True) + EPS)
    return (y * g.astype(jnp.float32)).astype(x.dtype)

def layernorm(x, g, b):
    xf = x.astype(jnp.float32)
    mu = jnp.mean(xf, axis=-1, keepdims=True)
    var = jnp.mean(jnp.square(xf - mu), axis=-1, keepdims=True)
    y = (xf - mu) * lax.rsqrt(var + EPS)
    return (y * g.astype(jnp.float32) + b.astype(jnp.float32)).astype(x.dtype)

def rope(x, positions):
    half = x.shape[-1] // 2
    inv = ROPE_BASE ** (-jnp.arange(half, dtype=jnp.float32) / half)
    ang = positions.astype(jnp.float32)[..., None] * inv
    cos = jnp.cos(ang)[:, :, None, :]
    sin = jnp.sin(ang)[:, :, None, :]
    x1, x2 = x[..., :half], x[..., half:]
    return jnp.concatenate([x1 * cos - x2 * sin, x1 * sin + x2 * cos], axis=-1).astype(x.dtype)

def fox_attention(q, k, v, f_logit, f_bias):
    B, S, H, Dh = q.shape
    log_f = jax.nn.log_sigmoid((f_logit + f_bias).astype(jnp.float32))
    cum = jnp.cumsum(log_f, axis=1).transpose(0, 2, 1)
    key_pos = jnp.arange(S)
    scale = Dh ** -0.5

    def block(i):
        start = i * Q_BLOCK
        qb = lax.dynamic_slice_in_dim(q, start, Q_BLOCK, axis=1)
        cq = lax.dynamic_slice_in_dim(cum, start, Q_BLOCK, axis=2)
        s = jnp.einsum('bqhd,bkhd->bhqk', qb, k).astype(jnp.float32) * scale
        s = s + cq[..., :, None] - cum[:, :, None, :]
        q_pos = start + jnp.arange(Q_BLOCK)
        causal = key_pos[None, :] <= q_pos[:, None]
        s = jnp.where(causal, s, -jnp.inf)
        p = jax.nn.softmax(s, axis=-1).astype(v.dtype)
        return jnp.einsum('bhqk,bkhd->bqhd', p, v)

    out = lax.map(block, jnp.arange(S // Q_BLOCK))
    return out.transpose(1, 0, 2, 3, 4).reshape(B, S, H * Dh)

def pool_mixer(u, pool_w, pool_scale):
    B, S, _ = u.shape
    ug = u.reshape(B, S, POOL_GROUPS, POOL_GROUP_DIM)
    cs = jnp.cumsum(ug.astype(jnp.float32), axis=1)
    pos = jnp.arange(S)
    means = []
    for gi, w in enumerate(POOL_WINDOWS):
        c_g = cs[:, :, gi]
        shifted = jnp.pad(c_g, ((0, 0), (w, 0), (0, 0)))[:, :S]
        count = jnp.minimum(pos + 1, w).astype(jnp.float32)[None, :, None]
        means.append((c_g - shifted) / count)
    pooled = jnp.stack(means, axis=2)
    delta = (pooled - ug.astype(jnp.float32)).astype(u.dtype)
    mixed = jnp.einsum('bsgc,gcd->bsgd', delta, pool_w).reshape(B, S, GROUP_WIDTH)
    return mixed * pool_scale

def retention(q, k, v, g, positions, gn_g):
    B, S, H, Dh = q.shape
    q = rope(q, positions)
    k = rope(k, positions) * (Dh ** -0.5)
    log_gamma = jnp.log(1.0 - 2.0 ** (-5.0 - jnp.arange(H, dtype=jnp.float32)))
    C = RET_CHUNK
    NC = S // C
    idx = jnp.arange(C, dtype=jnp.float32)
    diff = idx[:, None] - idx[None, :]
    dmask = jnp.where(diff >= 0, jnp.exp(log_gamma[:, None, None] * jnp.maximum(diff, 0.0)), 0.0)
    zeta = jnp.exp(log_gamma[:, None] * (C - 1 - idx))
    xi = jnp.exp(log_gamma[:, None] * (idx + 1))
    chunk_decay = jnp.exp(log_gamma * C)

    qc = q.reshape(B, NC, C, H, Dh)
    kc = k.reshape(B, NC, C, H, Dh)
    vc = v.reshape(B, NC, C, H, Dh)
    intra_s = jnp.einsum('bnqhd,bnkhd->bnhqk', qc, kc) * dmask
    intra = jnp.einsum('bnhqk,bnkhe->bnqhe', intra_s, vc)
    kv = jnp.einsum('bnkhd,hk,bnkhe->bnhde', kc, zeta, vc)

    def step(state, xs):
        q_n, kv_n = xs
        cross = jnp.einsum('bqhd,bhde->bqhe', q_n, state)
        new = (state * chunk_decay[None, :, None, None] + kv_n).astype(state.dtype)
        return new, cross

    state0 = jnp.zeros((B, H, Dh, Dh), dtype=kv.dtype)
    _, cross = lax.scan(step, state0, (qc.transpose(1, 0, 2, 3, 4), kv.transpose(1, 0, 2, 3, 4)))
    cross = cross.transpose(1, 0, 2, 3, 4) * xi.T[None, None, :, :, None]
    o = (intra + cross).reshape(B, S, H, Dh).astype(jnp.float32)
    mu = jnp.mean(o, axis=-1, keepdims=True)
    var = jnp.mean(jnp.square(o - mu), axis=-1, keepdims=True)
    o = (o - mu) * lax.rsqrt(var + EPS) * gn_g.reshape(H, Dh).astype(jnp.float32)
    o = o.reshape(B, S, H * Dh).astype(g.dtype)
    return jax.nn.silu(g) * o

def conformer_conv(u, conv_w, conv_b, ln_g, ln_b):
    a, gate = jnp.split(u, 2, axis=-1)
    h = a * jax.nn.sigmoid(gate)
    h = lax.conv_general_dilated(
        h, conv_w[:, None, :], window_strides=(1,), padding=[(CONV_WIDTH - 1, 0)],
        dimension_numbers=('NWC', 'WIO', 'NWC'), feature_group_count=CONV_CH) + conv_b
    return jax.nn.silu(layernorm(h, ln_g, ln_b))

def second_inputs(seed: int = 0) -> dict:
    key = jax.random.key(seed)
    ks = jax.random.split(key, 24)
    f32 = jnp.float32
    D, G = D_MODEL, GROUP_WIDTH
    nrm = lambda k, shape, s: jax.random.normal(k, shape, f32) * s
    return {
        "x": jax.random.normal(ks[0], (BATCH, SEQ, D), f32),
        "c": jax.random.normal(ks[1], (BATCH, D), f32),
        "positions": jnp.broadcast_to(jnp.arange(SEQ, dtype=jnp.int32)[None, :], (BATCH, SEQ)),
        "ada_w": nrm(ks[2], (DEPTH, D, 6 * D), 0.5 * D ** -0.5),
        "ada_b": nrm(ks[3], (DEPTH, 6 * D), 0.01),
        "norm_mix_g": 1.0 + nrm(ks[4], (DEPTH, D), 0.1),
        "norm_ffn_g": 1.0 + nrm(ks[5], (DEPTH, D), 0.1),
        "w_in": nrm(ks[6], (DEPTH, D, N_IN), D ** -0.5),
        "fox_fb": jax.random.uniform(ks[7], (DEPTH, FOX_HEADS), f32, 2.0, 5.0),
        "pool_w": nrm(ks[8], (DEPTH, POOL_GROUPS, POOL_GROUP_DIM, POOL_GROUP_DIM), POOL_GROUP_DIM ** -0.5),
        "pool_scale": 1.0 + nrm(ks[9], (DEPTH, G), 0.1),
        "ret_gn_g": 1.0 + nrm(ks[10], (DEPTH, G), 0.1),
        "conv_w": nrm(ks[11], (DEPTH, CONV_WIDTH, CONV_CH), CONV_WIDTH ** -0.5),
        "conv_b": nrm(ks[12], (DEPTH, CONV_CH), 0.01),
        "conv_ln_g": 1.0 + nrm(ks[13], (DEPTH, CONV_CH), 0.1),
        "conv_ln_b": nrm(ks[14], (DEPTH, CONV_CH), 0.01),
        "w_out": nrm(ks[15], (DEPTH, D, D), D ** -0.5),
        "ffn_w1": nrm(ks[16], (DEPTH, D, D_FF_2), D ** -0.5),
        "ffn_w3": nrm(ks[17], (DEPTH, D, D_FF_2), D ** -0.5),
        "ffn_w2": nrm(ks[18], (DEPTH, D_FF_2, D), D_FF_2 ** -0.5),
        "final_g": 1.0 + nrm(ks[19], (D,), 0.1),
    }

def second_block(x, c, positions, ada_w, ada_b, norm_mix_g, norm_ffn_g, w_in, fox_fb,
              pool_w, pool_scale, ret_gn_g, conv_w, conv_b, conv_ln_g, conv_ln_b,
              w_out, ffn_w1, ffn_w3, ffn_w2, final_g):
    B, S, _ = x.shape
    G, H, Dh = GROUP_WIDTH, FOX_HEADS, HEAD_DIM
    bounds = [G, 2 * G, 3 * G, 3 * G + H,
              4 * G + H,
              5 * G + H, 6 * G + H, 7 * G + H, 8 * G + H]
    c_act = jax.nn.silu(c)
    for l in range(DEPTH):
        mod = (c_act @ ada_w[l] + ada_b[l])[:, None, :]
        sh1, sc1, g1, sh2, sc2, g2 = jnp.split(mod, 6, axis=-1)

        h = rmsnorm(x, norm_mix_g[l]) * (1.0 + sc1) + sh1
        u = h @ w_in[l]
        fq, fk, fv, ff, pu, rq, rk, rv, rg, cu = jnp.split(u, bounds, axis=-1)
        y_fox = fox_attention(fq.reshape(B, S, H, Dh), fk.reshape(B, S, H, Dh),
                              fv.reshape(B, S, H, Dh), ff, fox_fb[l])
        y_pool = pool_mixer(pu, pool_w[l], pool_scale[l])
        y_ret = retention(rq.reshape(B, S, RET_HEADS, Dh), rk.reshape(B, S, RET_HEADS, Dh),
                          rv.reshape(B, S, RET_HEADS, Dh), rg, positions, ret_gn_g[l])
        y_conv = conformer_conv(cu, conv_w[l], conv_b[l], conv_ln_g[l], conv_ln_b[l])
        mix = jnp.concatenate([y_fox, y_pool, y_ret, y_conv], axis=-1)
        x = x + g1 * (mix @ w_out[l])

        h = rmsnorm(x, norm_ffn_g[l]) * (1.0 + sc2) + sh2
        f = (jax.nn.silu(h @ ffn_w1[l]) * (h @ ffn_w3[l])) @ ffn_w2[l]
        x = x + g2 * f
    return rmsnorm(x, final_g)


def setup_inputs(seed=0):
    out = dict(first_inputs(seed))
    for name, value in second_inputs(seed + 1).items():
        if name != "x":
            out[name + "_2"] = value
    return out


def reference(
    x, p, positions, g_mix, w_in, w_out, gm_ln_g, gm_ln_b, gm_ws, gm_bs, rw_mu, rw_w0, rw_w_up,
    rw_a0, rw_a_up, rw_g_up, rw_k_k, rw_k_a, rw_r_k, rw_gn_g, rw_gn_b, nsa_cmp_pos, nsa_kc_w1,
    nsa_kc_w2, nsa_vc_w1, nsa_vc_w2, g_ffn, ffn_w1, ffn_w3, ffn_w2, router_w, router_b, moe_w1,
    moe_w3, moe_w2, g_ple, ple_gate_w, ple_proj_w, g_final, c_2, positions_2, ada_w_2, ada_b_2,
    norm_mix_g_2, norm_ffn_g_2, w_in_2, fox_fb_2, pool_w_2, pool_scale_2, ret_gn_g_2, conv_w_2,
    conv_b_2, conv_ln_g_2, conv_ln_b_2, w_out_2, ffn_w1_2, ffn_w3_2, ffn_w2_2, final_g_2,
):
    x = first_block(
        x, p, positions, g_mix, w_in, w_out, gm_ln_g, gm_ln_b, gm_ws, gm_bs, rw_mu, rw_w0,
        rw_w_up, rw_a0, rw_a_up, rw_g_up, rw_k_k, rw_k_a, rw_r_k, rw_gn_g, rw_gn_b, nsa_cmp_pos,
        nsa_kc_w1, nsa_kc_w2, nsa_vc_w1, nsa_vc_w2, g_ffn, ffn_w1, ffn_w3, ffn_w2, router_w,
        router_b, moe_w1, moe_w3, moe_w2, g_ple, ple_gate_w, ple_proj_w, g_final,
    )
    return second_block(
        x, c_2, positions_2, ada_w_2, ada_b_2, norm_mix_g_2, norm_ffn_g_2, w_in_2, fox_fb_2,
        pool_w_2, pool_scale_2, ret_gn_g_2, conv_w_2, conv_b_2, conv_ln_g_2, conv_ln_b_2,
        w_out_2, ffn_w1_2, ffn_w3_2, ffn_w2_2, final_g_2,
    )


_drawn_inputs = setup_inputs


def setup_inputs(seed=0):
    import zlib

    import numpy as np

    out = dict(_drawn_inputs(seed))
    spreads = {}
    factors = {'router_b': 2.801,
     'ada_b_2': 3.617,
     'fox_fb_2': 28.376,
     'pool_scale_2': 3.31,
     'ret_gn_g_2': 3.85,
     'conv_b_2': 8.0,
     'conv_ln_g_2': 3.672,
     'conv_ln_b_2': 42.986}
    for name, (base, spread) in spreads.items():
        noise = np.random.default_rng([zlib.crc32(name.encode()), seed]).standard_normal(out[name].shape)
        drawn = base * np.exp(spread * noise) if base else spread * noise
        out[name] = __import__('jax').numpy.asarray(drawn.astype(out[name].dtype))
    for name, factor in factors.items():
        out[name] = (out[name] * factor).astype(out[name].dtype)
    return out
```

```python
import math

import numpy as np

import concourse.bass as bass
from concourse import mybir

F32 = mybir.dt.float32
I32 = mybir.dt.int32
ALU = mybir.AluOpType
ACT = mybir.ActivationFunctionType
AXX = mybir.AxisListType.X

P = 128
SEQ, D = 256, 1024
NT = SEQ // P
KD = D // P
HD = 64
FF = 2816
FB = FF // P
NE = 8
SLOT = 3072
NSLOT = 11
NWALK = 6
COLS = SLOT // KD
DIN1, DIN2 = 2840, 2564
NEG = -1e30
NCMP = (SEQ - 32) // 16 + 1
POOLW = (2, 4, 8, 16)
CONVW = 31


def const_arrays():
    s = np.arange(P)[:, None]
    t = np.arange(P)[None, :]
    f = np.float32
    one = {}
    one["ident"] = (s == t)
    one["tri"] = (s <= t)
    same = (s // 64 == t // 64)
    one["tri64"] = (s <= t) & same
    one["shift"] = (t == s + 1)
    one["carry"] = (s == P - 1) & (t == 0)
    strict, incl = (s < t) & same, (s <= t) & same
    one["mask4"] = np.concatenate([strict, incl, strict, incl], 1)
    one["levels"] = np.concatenate(
        [((s // (2 * b) == t // (2 * b)) & (s % (2 * b) < b) & (t % (2 * b) >= b)) for b in (1, 2, 4, 8, 16, 32)], 1)
    one["half"] = (np.arange(P)[:, None] // 64 == np.arange(2)[None, :])
    tok = np.arange(P)[:, None, None] + P * np.arange(NT)[None, :, None]
    end = (np.arange(NCMP) * 16 + 31)[None, None, :]
    one["cmp01"] = (end <= tok).reshape(P, -1)
    one["cmpneg"] = np.where(end <= tok, 0.0, NEG).reshape(P, -1)
    one["before"] = np.broadcast_to((np.arange(8)[None, :] < np.arange(8)[:, None]).reshape(1, 64), (P, 64))
    one["inv1"] = np.broadcast_to((1.0 / (f(500000.0) ** (np.arange(0, 16, 2, dtype=f) / f(16)))).astype(f)[None], (P, 8))
    diag = np.where(t <= s, 0.0, NEG)
    one["causal"] = np.concatenate([diag, np.zeros((P, P)), diag], 1)
    two = {k: one[k] for k in ("ident", "tri", "causal")}
    two["ones"] = np.ones((P, P))
    sk = np.arange(SEQ)[:, None]
    tk = np.arange(SEQ)[None, :]
    band = []
    for w in POOLW:
        m = ((sk <= tk) & (sk > tk - w)) / np.minimum(tk + 1, w).astype(f) - (sk == tk)
        band += [m[:P], m[P:, P:]]
    two["band"] = np.concatenate(band, 1)
    decay = []
    for h in range(4):
        lg = math.log(1.0 - 2.0 ** (-5.0 - h))
        m = np.where(sk <= tk, np.exp(lg * np.maximum(tk - sk, 0)), 0.0) * HD ** -0.5
        decay += [m[:P], m[P:, P:]]
    two["decay"] = np.concatenate(decay, 1)
    two["inv2"] = np.broadcast_to((f(10000.0) ** (-np.arange(32, dtype=f) / f(32))).astype(f)[None], (P, 32))
    fix = lambda d: {k: np.ascontiguousarray(v, dtype=f) for k, v in d.items()}
    return fix(one), fix(two)


def const_table(d):
    out, at = {}, 0
    for k, v in d.items():
        out[k] = (at, v.shape[1])
        at += v.shape[1]
    return out, at


SMALL1 = [("g_mix", 8), ("g_ffn", 8), ("g_ple", 8), ("kc_w2", 64), ("vc_w2", 64), ("pos", 16),
          ("lora", 512), ("g_up", 256), ("wst", 512), ("bs", 4), ("router", 64)]
ROWS1 = [("mu", 1024), ("wa0", 512), ("k_k", 256), ("k_a", 256), ("r_k", 256), ("gn_g", 256), ("gn_b", 256)]
ROWS1B = [("ln_g", 256), ("ln_b", 256), ("rb", 8)]
SMALL2 = [("g_mix", 8), ("g_ffn", 8), ("pool_w", 128), ("conv_w", 62), ("conv_b", 2), ("ada_b", 48), ("c", 8)]
ROWS2 = [("pool_scale", 256), ("gn_g", 256), ("ln_g", 256), ("ln_b", 256), ("gate_b", 2048 - 1024), ("fb", 4)]
ROWS2B = [("gate_b2", 1024)]


def spans(fields, at=0):
    out = {}
    for name, width in fields:
        out[name] = (at, width)
        at += width
    return out, at


class Mark:

    def __init__(self, sem, value, loop=None, step=0):
        self.sem, self.value, self.loop, self.step = sem, value, loop, step

    def last(self):
        return Mark(self.sem, self.value + (self.loop.turns - 1) * self.step)


class Loop:
    def __init__(self, turn, turns):
        self.turn, self.turns = turn, turns


class Engine:

    def __init__(self, nc, q, name, chained):
        self.nc, self.q, self.chained = nc, q, chained
        self.sem = nc.alloc_semaphore("s_" + name)
        self.n, self.loop, self.step, self.met = 0, None, 0, {}

    def wait(self, *marks):
        for m in marks:
            if m is None:
                continue
            if isinstance(m, (list, tuple)):
                self.wait(*m)
                continue
            if m.loop is not None and m.loop is self.loop:
                self.q.wait_ge(m.sem, self.loop.turn * m.step + m.value)
                continue
            assert m.loop is None
            key = m.sem.name
            if self.met.get(key, -1) >= m.value:
                continue
            if self.loop is None:
                self.met[key] = m.value
            self.q.wait_ge(m.sem, m.value)

    def mark(self, ins):
        ins.then_inc(self.sem, 1)
        self.n += 1
        return Mark(self.sem, self.n, self.loop, self.step)

    def now(self):
        return Mark(self.sem, self.n, self.loop, self.step)

    def __call__(self, op, *args, after=(), **kw):
        self.wait(*after)
        if self.chained and self.n:
            self.wait(self.now())
        return self.mark(op(*args, **kw))

    def enter(self, loop, step):
        self.loop, self.step, self.first, self.met = loop, step, self.n, {}

    def at(self, offset):
        return Mark(self.sem, self.first + offset, self.loop, self.step)

    def leave(self):
        assert self.n == self.first + self.step, (self.n, self.first, self.step)
        self.n = self.first + self.step * self.loop.turns
        self.loop, self.met = None, {}


class Banks:

    def __init__(self, ps, pe):
        self.ps, self.pe, self.next, self.free = ps, pe, 0, [[] for _ in range(8)]

    def take(self):
        b = self.next
        self.next = (b + 1) % 8
        assert self.free[b] is not None, "bank taken twice"
        self.pe.wait(*self.free[b])
        self.free[b] = None
        return b

    def give(self, b, *marks):
        self.free[b] = list(marks)

    def __getitem__(self, b):
        return self.ps[:, b, :]


class Ring:

    def __init__(self, nc, sp, mem):
        self.nc, self.sp, self.mem = nc, sp, mem
        self.sems = [nc.alloc_semaphore(f"s_slot{i}") for i in range(NSLOT)]
        self.count = [0] * NSLOT
        self.free = [[] for _ in range(NSLOT)]
        self.plan, self.held, self.order = [], {}, list(range(NWALK))

    def schedule(self, tiles):
        self.plan += tiles
        self.pump()

    def pump(self):
        while self.plan and self.order:
            name, parts = self.plan.pop(0)
            s = self.order.pop(0)
            self.sp.wait(*self.free[s])
            for src, at in parts:
                n = src.shape[-1]
                self.sp.q.dma_start(self.mem[:, s, at:at + n], src).then_inc(self.sems[s], 16)
                self.count[s] += 16
            self.held[name] = (s, Mark(self.sems[s], self.count[s]))

    def get(self, name):
        s, m = self.held[name]
        return self.mem[:, s, :], m

    def release(self, name, *marks):
        s, _ = self.held.pop(name)
        self.free[s] = list(marks)
        self.order.append(s)
        self.pump()


class Carve:

    def __init__(self, mem, at=0):
        self.mem, self.at, self.size = mem, at, mem.shape[1]

    def __call__(self, *dims):
        n = 1
        for d in dims:
            n *= d
        ap = self.mem[:, self.at:self.at + n]
        self.at += n
        assert self.at <= self.size, (self.at, self.size)
        if len(dims) == 2:
            ap = ap.rearrange("p (a b) -> p a b", a=dims[0])
        elif len(dims) == 3:
            ap = ap.rearrange("p (a b c) -> p a b c", a=dims[0], b=dims[1])
        elif len(dims) == 4:
            ap = ap.rearrange("p (a b c d) -> p a b c d", a=dims[0], b=dims[1], c=dims[2])
        return ap


def spread(ap, axis, n):
    ap = ap.unsqueeze(axis)
    shape = list(ap.shape)
    shape[axis] = n
    return ap.to_broadcast(shape)


def build(nc, d):
    V, S, T, G = nc.vector, nc.scalar, nc.tensor, nc.gpsimd
    dve = Engine(nc, V, "dve", True)
    act = Engine(nc, S, "act", True)
    pool = Engine(nc, G, "pool", True)
    pe = Engine(nc, T, "pe", False)
    sp = Engine(nc, nc.sync, "sp", False)

    def sb(name, n, dt=F32):
        return nc.alloc_sbuf_tensor(name, [P, n], dt)[:, :]

    one, two = const_arrays()
    tab1, width1 = const_table(one)
    tab2, width2 = const_table(two)
    h = sb("residual", NT * D).rearrange("p (i n) -> p i n", i=NT)
    xn = sb("natural", NT * D).rearrange("p (i n) -> p i n", i=NT)
    xt = sb("transposed", KD * SEQ).rearrange("p (k t) -> p k t", k=KD)
    zbuf = sb("z", NT * DIN1)
    cst = sb("constants", max(width1, width2))
    stat = sb("stat", 256)
    ang = sb("rope", 4 * NT * 32)
    gates2 = sb("gates2", 2 * D).rearrange("p (g n) -> p g n", g=2)
    zero = sb("zero", 512)
    ringm = nc.alloc_sbuf_tensor("ring", [P, NSLOT, SLOT], F32)[:, :, :]
    work = ringm.rearrange("p s n -> p (s n)")[:, NWALK * SLOT:]
    ps = nc.alloc_psum_tensor("ps", [P, 8, 512], F32)[:, :, :]
    bank = Banks(ps, pe)
    ring = Ring(nc, sp, ringm)
    s_misc = nc.alloc_semaphore("s_misc")
    misc = [0]

    def fetch(dst, src, after=()):
        pool.wait(*after)
        if misc[0]:
            pool.wait(Mark(s_misc, misc[0]))
        G.dma_start(dst, src).then_inc(s_misc, 16)
        misc[0] += 16
        return Mark(s_misc, misc[0])

    def join():
        return [dve.now(), act.now(), pe.now(), pool.now()]

    const = [tab1]

    def C(name):
        at, n = const[0][name]
        return cst[:, at:at + n]

    def transpose(b, col, src):
        return T.transpose(ps[:, b, col:col + P], src, C("ident"))

    def rsqrt(ap, after=()):
        m = act(S.activation, ap, ap, ACT.Sqrt, after=after)
        return dve(V.reciprocal, ap, ap, after=[m])

    def rms_rows(after, out):
        for i in range(NT):
            m = dve(V.tensor_tensor_reduce, out=out[:, i, :], in0=h[:, i, :], in1=h[:, i, :], scale=1.0 / D,
                    scalar=1e-6, op0=ALU.mult, op1=ALU.add, accum_out=stat[:, i:i + 1], after=after)
        rsqrt(stat[:, 0:NT], after=[m])
        for i in range(NT):
            m = dve(V.tensor_scalar, out[:, i, :], h[:, i, :], stat[:, i:i + 1], None, ALU.mult)
        return m

    def turn_xn(after, mult=None, add=None, after_w=()):
        for i in range(NT):
            for q in range(2):
                pe.wait(*after)
                b = bank.take()
                for k in range(4):
                    t = transpose(b, k * P, xn[:, i, (4 * q + k) * P:(4 * q + k + 1) * P])
                t = pe.mark(t)
                out = xt[:, 4 * q:4 * q + 4, i * P:(i + 1) * P]
                src = bank[b].rearrange("p (k t) -> p k t", k=4)
                if mult is None:
                    m = act(S.copy, out, src, after=[t])
                    bank.give(b, m)
                else:
                    m = dve(V.tensor_tensor, out, src, spread(mult[:, 4 * q:4 * q + 4], 2, P), ALU.mult,
                            after=[t] + list(after_w))
                    bank.give(b, m)
                    if add is not None:
                        m = dve(V.tensor_tensor, out, out, spread(add[:, 4 * q:4 * q + 4], 2, P), ALU.add)
        return m

    def project(z, width, tag, ready):
        pe.wait(ready)
        for c in range(-(-width // COLS)):
            n = min(COLS, width - c * COLS)
            w, loaded = ring.get(f"{tag}{c}")
            w = w[:, 0:KD * n].rearrange("p (k n) -> p k n", k=KD)
            pe.wait(loaded)
            for i in range(NT):
                b = bank.take()
                for k in range(KD):
                    t = T.matmul(ps[:, b, 0:n], xt[:, k, i * P:(i + 1) * P], w[:, k, :],
                                 start=(k == 0), stop=(k == KD - 1))
                t = pe.mark(t)
                m = act(S.copy, z[:, i, c * COLS:c * COLS + n], ps[:, b, 0:n], after=[t])
                bank.give(b, m)
            ring.release(f"{tag}{c}", t)
        return m

    def out_project(tag, ready, add):
        pe.wait(ready)
        bs = [bank.take() for _ in range(4)]
        for c in range(3):
            ks = range(3 * c, min(3 * c + 3, KD))
            w, loaded = ring.get(f"{tag}{c}")
            pe.wait(loaded)
            for i in range(NT):
                for q in range(2):
                    for k in ks:
                        t = T.matmul(ps[:, bs[2 * i + q], :], xt[:, k, i * P:(i + 1) * P],
                                     w[:, (k - 3 * c) * D + q * 512:(k - 3 * c) * D + (q + 1) * 512],
                                     start=(k == 0), stop=(k == KD - 1))
            t = pe.mark(t)
            ring.release(f"{tag}{c}", t)
        for i in range(NT):
            for q in range(2):
                m = add(i, q, bank[bs[2 * i + q]], t)
                bank.give(bs[2 * i + q], m)
        return m

    def head_norm(x, n, width, eps, tmp, after=()):
        s1, s2 = stat[:, 16:16 + n], stat[:, 32:32 + n]
        dve(V.tensor_reduce, s1, x, AXX, ALU.add, after=after)
        dve(V.tensor_scalar, s1, s1, 1.0 / width, None, ALU.mult)
        dve(V.tensor_tensor, x, x, spread(s1, 2, width), ALU.subtract)
        dve(V.tensor_tensor, tmp, x, x, ALU.mult)
        dve(V.tensor_reduce, s2, tmp, AXX, ALU.add)
        m = dve(V.tensor_scalar, s2, s2, 1.0 / width, eps, ALU.mult, ALU.add)
        rsqrt(s2, after=[m])
        return dve(V.tensor_tensor, x, x, spread(s2, 2, width), ALU.mult)

    def rope_tables(pos, inv, n, w, after):
        cos = ang[:, 0:NT * n].rearrange("p (i n) -> p i n", i=NT)
        sin = ang[:, 64:64 + NT * n].rearrange("p (i n) -> p i n", i=NT)
        posf, a, k = w(NT), w(NT, n), w(NT, n)
        dve(V.tensor_copy, posf, pos, after=after)
        dve(V.tensor_tensor, a, spread(posf, 2, n), spread(inv, 1, NT), ALU.mult)
        magic = 1.5 * 2 ** 23
        dve(V.tensor_scalar, k, a, 1.0 / (2 * math.pi), magic, ALU.mult, ALU.add)
        dve(V.tensor_scalar, k, k, magic, None, ALU.subtract)
        c1 = 6.28125
        c2 = float(np.float32(round((2 * math.pi - c1) * 2 ** 19) / 2 ** 19))
        c3 = 2 * math.pi - c1 - c2
        for c in (c1, c2, c3):
            dve(V.scalar_tensor_tensor, out=a, in0=k, scalar=-c, in1=a, op0=ALU.mult, op1=ALU.add)
        m = dve(V.tensor_scalar, a, a, 3.1415925, -3.1415925, ALU.min, ALU.max)
        act(S.activation, sin, a, ACT.Sin, after=[m])
        m = act(S.activation, k, a, ACT.Abs)
        m = dve(V.tensor_scalar, k, k, -1.0, math.pi / 2, ALU.mult, ALU.add, after=[m])
        return cos, sin, act(S.activation, cos, k, ACT.Sin, after=[m])

    def rotate(out, x, heads, half, cos, sin, tmp, after=()):
        c, s = spread(cos, 2, heads), spread(sin, 2, heads)
        x1, x2 = x[:, :, :, 0:half], x[:, :, :, half:2 * half]
        ta = tmp[:, 0:NT * heads * half].rearrange("p (i h n) -> p i h n", i=NT, h=heads)
        tb = tmp[:, 512:512 + NT * heads * half].rearrange("p (i h n) -> p i h n", i=NT, h=heads)
        dve(V.tensor_tensor, ta, x1, c, ALU.mult, after=after)
        dve(V.tensor_tensor, tb, x2, s, ALU.mult)
        dve(V.tensor_tensor, out[:, :, :, 0:half], ta, tb, ALU.subtract)
        dve(V.tensor_tensor, ta, x1, s, ALU.mult)
        dve(V.tensor_tensor, tb, x2, c, ALU.mult)
        return dve(V.tensor_tensor, out[:, :, :, half:2 * half], ta, tb, ALU.add)

    def softmax_rows(sc, heads, after=()):
        mx, sm = stat[:, 48:48 + heads], stat[:, 64:64 + heads]
        n = sc.shape[2]
        dve(V.tensor_reduce, mx, sc, AXX, ALU.max, after=after)
        m = dve(V.tensor_tensor, sc, sc, spread(mx, 2, n), ALU.subtract)
        m = act(S.activation, sc, sc, ACT.Exp, after=[m])
        dve(V.tensor_reduce, sm, sc, AXX, ALU.add, after=[m])
        m = dve(V.reciprocal, sm, sm)
        return sm, m

    def weighted_values(pr, heads, ns, pt, value, ready):
        flat = [(m, st) for m in range(heads) for st in range(ns)]
        for g in range(0, len(flat), 4):
            pe.wait(ready)
            b = bank.take()
            for e, (m, st) in enumerate(flat[g:g + 4]):
                t = transpose(b, e * P, pr[:, m, st * P:(st + 1) * P])
            t = pe.mark(t)
            k = act(S.copy, pt[:, g:g + 4, :], bank[b].rearrange("p (a t) -> p a t", a=4), after=[t])
            bank.give(b, k)
        pe.wait(k)
        b = bank.take()
        for e, (m, st) in enumerate(flat):
            t = T.matmul(ps[:, b, m * HD:(m + 1) * HD], pt[:, e, :], value(m, st), start=(st == 0), stop=(st == ns - 1))
        return b, pe.mark(t)

    def feed_forward(tiles, experts, first_tile, gate, ready, add):
        assert not ring.plan and not ring.held
        fw = Carve(zbuf, NE * SEQ)
        silu, hid = fw(2, SEQ), fw(2, SEQ)
        for b in range(8):
            pe.wait(*bank.free[b])
        pe.wait(ready)
        for b in range(4, 8):
            t = T.matmul(ps[:, b, :], zero[:, 0:P], zero[:, :], start=True, stop=False)
        pe.mark(t)
        turns = experts * FB // NSLOT
        half = FB // NSLOT
        base = list(ring.count)
        free0 = [list(f) for f in ring.free]
        all_work = join()
        nv = 2 if gate is not None else 1
        sp.wait()
        with nc.Fori(0, experts) as e, nc.Fori(0, half) as c:
            loop = Loop(e * half + c, turns)
            pe.enter(loop, 2 * NSLOT)
            act.enter(loop, NSLOT)
            dve.enter(loop, nv * NSLOT)
            sp.enter(loop, 0)
            for j in range(NSLOT):
                sp.wait(*(free0[j] if j < NWALK else all_work))
                sp.wait(pe.at(down_at(j) - 2 * NSLOT))
                sp.q.dma_start(ringm[:, j, :], tiles[first_tile + loop.turn * NSLOT + j]).then_inc(ring.sems[j], 16)

            def up(j):
                w = ringm[:, j, :]
                pe.wait(Mark(ring.sems[j], base[j] + 16, loop, 16))
                pe.wait(dve.at(nv * (j - 1)))
                for half_w in range(2):
                    b = 2 * half_w + j % 2
                    for k in range(KD):
                        at = half_w * D + k * P
                        t = T.matmul(ps[:, b, 0:SEQ], w[:, at:at + P], xt[:, k, :], start=(k == 0), stop=(k == KD - 1))
                return pe.mark(t)

            def gated(j, t):
                act.wait(dve.at(nv * (j - 1)))
                m = act(S.activation, silu[:, j % 2, :], ps[:, j % 2, 0:SEQ], ACT.Silu, after=[t])
                if gate is not None:
                    m = dve(V.tensor_tensor, silu[:, j % 2, :], silu[:, j % 2, :], gate[:, e, :], ALU.mult, after=[m])
                dve.wait(pe.at(down_at(j - 2) if j >= 2 else down_at(j - 2 + NSLOT) - 2 * NSLOT))
                return dve(V.tensor_tensor, hid[:, j % 2, :], silu[:, j % 2, :], ps[:, 2 + j % 2, 0:SEQ], ALU.mult,
                           after=[m, t])

            def down(j, m):
                pe.wait(m)
                w = ringm[:, j, 2 * D:3 * D]
                for i in range(NT):
                    for q in range(2):
                        t = T.matmul(ps[:, 4 + 2 * i + q, :], hid[:, j % 2, i * P:(i + 1) * P], w[:, q * 512:(q + 1) * 512],
                                     start=False, stop=False)
                return pe.mark(t)

            m = gated(0, up(0))
            for j in range(NSLOT):
                nxt = gated(j + 1, up(j + 1)) if j + 1 < NSLOT else None
                t = down(j, m)
                m = nxt
            for q in (pe, act, dve, sp):
                q.leave()
        for j in range(NSLOT):
            ring.count[j] += 16 * turns
            ring.free[j] = [pe.now()]
        ring.order = list(range(NWALK))
        bank.next = 0
        for b in range(4):
            bank.free[b] = [dve.now(), act.now()]
        for b in range(4, 8):
            t = T.matmul(ps[:, b, :], zero[:, 0:P], zero[:, :], start=False, stop=True)
        t = pe.mark(t)
        for i in range(NT):
            for q in range(2):
                m = add(i, q, bank[4 + 2 * i + q], t)
                bank.free[4 + 2 * i + q] = [m]
        return m

    def down_at(j):
        return 2 * j + 3 if j + 1 < NSLOT else 2 * NSLOT

    def add_residual(i, q, src, t):
        return dve(V.tensor_tensor, h[:, i, q * 512:(q + 1) * 512], h[:, i, q * 512:(q + 1) * 512], src, ALU.add,
                   after=[t])

    loaded_const = fetch(cst[:, 0:width1], d["const1"])
    loaded_x = fetch(h, d["x"])
    posi = nc.alloc_sbuf_tensor("posi", [P, 2 * NT], I32)[:, :]
    loaded_pos = fetch(posi, d["pos"])
    dve(V.memset, zero, 0.0)
    pe.wait(dve.now(), loaded_const)
    w = Carve(work)
    cos, sin, rope_ready = rope_tables(posi[:, 0:NT], C("inv1"), 8, w, [loaded_const, loaded_pos])
    dve.wait(loaded_x)

    small1, n_small1 = spans(SMALL1)
    rows1b, _ = spans(ROWS1B, n_small1)
    rows1, _ = spans(ROWS1)
    small1.update(rows1b)

    def columns(buf, table):
        def get(name):
            at, n = table[name]
            return buf[:, at:at + n]
        return get

    def layer_tiles(l):
        out = [("small", [(d["small1"][l], 0), (d["rows1b"][l:l + 1].to_broadcast([P, d["rows1b"].shape[1]]), n_small1)]),
               ("rows", [(d["rows1"][l:l + 1].to_broadcast([P, d["rows1"].shape[1]]), 0)])]
        for c in range(-(-DIN1 // COLS)):
            n = min(COLS, DIN1 - c * COLS)
            out.append((f"win{c}", [(d["w_in"][l, c, :, 0:KD * n], 0)]))
        out += [("kc", [(d["kc_w1"][l], 0)]), ("vc", [(d["vc_w1"][l], 0)])]
        out += [(f"wout{c}", [(d["w_out"][l, c], 0)]) for c in range(3)]
        return out

    def ple_tiles(l):
        return [("ple_up", [(d["ple_proj"][l], 0)])] + \
            [(f"pleg{c}", [(d["ple_gate"][l, c, :, 0:KD * min(COLS, D - c * COLS)], 0)]) for c in range(3)]

    def spatial_gating(z, small, ready):
        w = Carve(work)
        u, v, tmp, wst = w(NT, 256), w(NT, 256), w(8, 64), w(4, P)
        act(S.activation, u, z[:, :, 0:256], ACT.Gelu_apprx_tanh, after=ready)
        m = act(S.activation, v, z[:, :, 256:512], ACT.Gelu_apprx_tanh)
        dve(V.tensor_tensor, wst, small("wst").rearrange("p (h t) -> p h t", h=4), spread(C("tri"), 1, 4), ALU.mult,
            after=ready)
        head_norm(v.rearrange("p i (h d) -> p (i h) d", h=4), 8, HD, 1e-5, tmp, after=[m])
        dve(V.tensor_tensor, v, v, spread(small("ln_g"), 1, NT), ALU.mult)
        m = dve(V.tensor_tensor, v, v, spread(small("ln_b"), 1, NT), ALU.add)
        pe.wait(m)
        b = bank.take()
        for i in range(NT):
            for hh in range(4):
                t = T.matmul(ps[:, b, (4 * i + hh) * HD:(4 * i + hh + 1) * HD], wst[:, hh, :],
                             v[:, i, hh * HD:(hh + 1) * HD], start=True, stop=True)
        t = pe.mark(t)
        bs = small("bs")
        mixed = v
        for i in range(NT):
            m = dve(V.tensor_tensor, mixed[:, i, :].rearrange("p (h d) -> p h d", h=4),
                    bank[b][:, i * 256:(i + 1) * 256].rearrange("p (h d) -> p h d", h=4), spread(bs, 2, HD), ALU.add,
                    after=[t])
        bank.give(b, m)
        return dve(V.tensor_tensor, xn[:, :, 0:256], u, mixed, ALU.mult)

    def sparse_attention(z, small, ready, layer):
        Z = 1536
        w = Carve(work)
        q = z[:, :, Z:Z + 512]
        qr, tmp, oacc = w(NT, 512), w(1024), w(NT, 512)
        kr = w(2, NT, P)
        qT, qrT, kT = w(NT, 4, P), w(NT, 4, P), w(2, SEQ)
        gt = w(NT, 24)
        mark1 = w.at
        dve.wait(*ready)
        act(S.activation, gt, z[:, :, Z + 1280:Z + 1304], ACT.Sigmoid, after=ready)
        m = act(S.copy, qr, q)
        heads = lambda ap, n: ap.rearrange("p i (h d) -> p i h d", h=n)
        rotate(heads(qr, 8), heads(q, 8), 8, 8, cos, sin, tmp, after=[m, rope_ready])
        for ty, at in ((0, Z + 768), (1, Z + 1024)):
            m = act(S.copy, kr[:, ty], z[:, :, at:at + P])
            rotate(heads(kr[:, ty], 2), heads(z[:, :, at:at + P], 2), 2, 8, cos, sin, tmp, after=[m])
        r = dve.now()
        for i in range(NT):
            for src, dst, dep in ((q, qT, ready), (qr, qrT, [r])):
                pe.wait(*dep)
                b = bank.take()
                for j in range(4):
                    t = transpose(b, j * P, src[:, i, j * P:(j + 1) * P])
                t = pe.mark(t)
                m = act(S.mul, dst[:, i], bank[b].rearrange("p (j t) -> p j t", j=4), HD ** -0.5, after=[t])
                bank.give(b, m)
        b = bank.take()
        for ty in range(2):
            for i in range(NT):
                t = transpose(b, (2 * ty + i) * P, kr[:, ty, i, :])
        t = pe.mark(t)
        m = act(S.copy, kT, bank[b].rearrange("p (a t) -> p a t", a=2), after=[t])
        bank.give(b, m)
        turned = m

        dup, x2 = w(NT, 4, 2, HD), w(4, SEQ)
        blk = w(4, 16, 15)
        hidden, hrep, kcT, vbd = w(2, 30), w(4, 32), w(16), w(4, HD)
        for i in range(NT):
            m = dve(V.tensor_copy, dup[:, i], spread(z[:, i, Z + 512:Z + 768].rearrange("p (a d) -> p a d", a=4), 2, 2))
        dve(V.memset, hrep, 0.0)
        dve(V.memset, vbd, 0.0)
        for i in range(NT):
            pe.wait(m)
            b = bank.take()
            for a in range(4):
                t = transpose(b, a * P, dup[:, i, a].rearrange("p b d -> p (b d)"))
            t = pe.mark(t)
            src = bank[b].rearrange("p (a t) -> p a t", a=4)
            act(S.copy, x2[0:64, :, i * P:(i + 1) * P], src[0:64], after=[t])
            lo = 1 if i == 0 else 0
            k = act(S.copy, x2[64:128, :, i * P + lo - 1:(i + 1) * P - 1], src[64:128, :, lo:P])
            bank.give(b, k)
        dve.wait(k)
        for a in range(4):
            for hh in range(2):
                m = dve(V.tensor_tensor, blk[:, a, 8 * hh:8 * hh + 8, :],
                        x2[:, a, 16 * hh:16 * hh + 240].rearrange("p (n l b) -> p b l n", l=8, b=2)[:, 0],
                        spread(small("pos")[:, 8 * hh:8 * hh + 8], 2, 15), ALU.add)
        pe.wait(m)
        b = bank.take()
        for kv, tag in ((0, "kc"), (1, "vc")):
            w1, loaded = ring.get(tag)
            pe.wait(loaded)
            for l in range(16):
                t = T.matmul(ps[:, b, 32 * kv:32 * kv + 30], w1[:, l * P:(l + 1) * P], blk[:, 2 * kv:2 * kv + 2, l, :],
                             start=(l == 0), stop=(l == 15))
            t = pe.mark(t)
            ring.release(tag, t)
        m = act(S.activation, hidden, ps[:, b, 0:64].rearrange("p (v n) -> p v n", v=2)[:, :, 0:30], ACT.Gelu_apprx_tanh,
                after=[t])
        bank.give(b, m)
        m2 = dve(V.tensor_copy, hrep.rearrange("p (a g) n -> p a g n", g=2)[:, :, :, 0:15],
                 spread(hidden[:, 1, :].rearrange("p (g n) -> p g n", g=2), 1, 2), after=[m])
        pe.wait(m, m2)
        b = bank.take()
        for g in range(2):
            T.matmul(ps[64 * g:64 * g + 64, b, 0:15], small("kc_w2"), hidden[:, 0, 15 * g:15 * g + 15], start=True, stop=True)
        t = pe.mark(T.matmul(ps[:, b, 64:128], hrep.rearrange("p a n -> p (a n)"), small("vc_w2"), start=True, stop=True))
        act(S.copy, kcT[:, 0:15], ps[:, b, 0:15], after=[t])
        for a in range(4):
            k = act(S.copy, vbd[32 * a:32 * a + 32, a, :], ps[32 * a:32 * a + 32, b, 64:128])
        bank.give(b, k)
        sc, pct = w(NT * 8, 32), w(4, P)
        m = dve(V.memset, sc, 0.0)
        scv = sc.rearrange("p (i m) n -> p i m n", i=NT)
        neg = C("cmpneg").rearrange("p (i n) -> p i n", i=NT)
        pe.wait(k, turned)
        for i in range(NT):
            for g in range(2):
                b = bank.take()
                for j in range(4):
                    t = T.matmul(ps[:, b, 16 * j:16 * j + 15], qT[64 * g:64 * g + 64, i, j, :],
                                 kcT[64 * g:64 * g + 64, 0:15], start=True, stop=True)
                t = pe.mark(t)
                m = dve(V.tensor_tensor, scv[:, i].rearrange("p (j g) n -> p j g n", g=2)[:, :, g, 0:15],
                        ps[:, b, 0:64].rearrange("p (j n) -> p j n", j=4)[:, :, 0:15], spread(neg[:, i], 1, 4), ALU.add,
                        after=[t])
                bank.give(b, m)
        rs, m = softmax_rows(sc[:, :, 0:15], NT * 8)
        dve(V.tensor_tensor, sc[:, :, 0:15], sc[:, :, 0:15], spread(rs, 2, 15), ALU.mult)
        for i in range(NT):
            m = dve(V.tensor_tensor, scv[:, i, :, 0:15], scv[:, i, :, 0:15],
                    spread(C("cmp01").rearrange("p (i n) -> p i n", i=NT)[:, i], 1, 8), ALU.mult)
        pe.wait(m)
        b = bank.take()
        for e in range(4):
            t = transpose(b, e * P, sc[:, 4 * e:4 * e + 4, :].rearrange("p m n -> p (m n)"))
        t = pe.mark(t)
        m = act(S.copy, pct, bank[b].rearrange("p (a t) -> p a t", a=4), after=[t])
        bank.give(b, m)
        pe.wait(m)
        for i in range(NT):
            b = bank.take()
            for c in range(2):
                t = T.matmul(ps[:, b, 256 * c:256 * c + 256], pct[:, 2 * i + c, :], vbd.rearrange("p a d -> p (a d)"),
                             start=True, stop=True)
            t = pe.mark(t)
            m = dve(V.tensor_tensor, oacc[:, i, :].rearrange("p (m d) -> p m d", m=8),
                    bank[b].rearrange("p (m d) -> p m d", m=8), spread(gt[:, i, 0:8], 2, HD), ALU.mult, after=[t])
            bank.give(b, m)
        compressed = join()

        w.at = mark1
        sbuf, pt = w(8 * 256), w(16, P)
        for ty in range(2):
            vat = Z + 896 + 256 * ty
            for i in range(NT):
                n = P * (i + 1)
                s8 = sbuf[:, 0:8 * n].rearrange("p (m s) -> p m s", m=8)
                s8g = s8.rearrange("p (j g) s -> p j g s", g=2)
                mask = C("causal")[:, P * i:P * i + n]
                pe.wait(*compressed)
                dve.wait(*compressed)
                per = 512 // n
                for g in range(2):
                    for j0 in range(0, 4, per):
                        b = bank.take()
                        for j in range(j0, j0 + per):
                            t = T.matmul(ps[:, b, (j - j0) * n:(j - j0 + 1) * n], qrT[64 * g:64 * g + 64, i, j, :],
                                         kT[64 * g:64 * g + 64, ty, 0:n], start=True, stop=True)
                        t = pe.mark(t)
                        m = dve(V.tensor_tensor, s8g[:, j0:j0 + per, g, :],
                                bank[b].rearrange("p (j s) -> p j s", j=per), spread(mask, 1, per), ALU.add, after=[t])
                        bank.give(b, m)
                rs, m = softmax_rows(s8, 8)
                b, t = weighted_values(s8, 8, i + 1, pt[:, 0:8 * (i + 1), :],
                                       lambda mm, st: z[:, st, vat + (mm % 2) * HD:vat + (mm % 2 + 1) * HD], m)
                dve(V.tensor_tensor, rs, rs, gt[:, i, 8 * (ty + 1):8 * (ty + 2)], ALU.mult)
                o = tmp[:, 0:512].rearrange("p (m d) -> p m d", m=8)
                m = dve(V.tensor_tensor, o, bank[b].rearrange("p (m d) -> p m d", m=8), spread(rs, 2, HD), ALU.mult,
                        after=[t])
                bank.give(b, m)
                dst = oacc[:, i, :] if ty == 0 else xn[:, i, 512:1024]
                m = dve(V.tensor_tensor, dst, oacc[:, i, :], tmp[:, 0:512], ALU.add)
                compressed = [m]
        return m

    def time_mix(z, small, rows, ready):
        w = Carve(work)
        zb = z[:, :, 512:1536]
        zm, gg, k2 = w(NT, 1024), w(NT, 256), w(NT, 256)
        keep = w(NT, 4, 256)
        pr, qT, hT = w(2, NT, 2, P), w(2, SEQ), w(2, SEQ)
        wc, st_e, st_f = w(2, 4), w(2, 2, HD), w(2, 4, HD)
        state, gT = w(4, 2, HD), w(2, SEQ)
        y = w(NT, 256)
        shared = w.at
        tmp, tmp2, lo, loT = w(NT, 256), w(NT, 256), w(NT, 256), w(2, SEQ)
        wa, kk, lw, wi, wx, wn = w(NT, 512), w(NT, 256), w(NT, 256), w(NT, 256), w(NT, 256), w(NT, 256)
        for e in (dve, act, pe):
            e.wait(*ready)
        for i in range(NT):
            for c in range(2):
                cols = slice(512 * c, 512 * c + 512)
                b = bank.take()
                t = T.matmul(bank[b], C("shift"), zb[:, i, cols], start=True, stop=(i == 0))
                if i:
                    t = T.matmul(bank[b], C("carry"), zb[:, i - 1, cols], start=False, stop=True)
                t = pe.mark(t)
                o = zm[:, i, cols]
                m = dve(V.tensor_tensor, o, bank[b], zb[:, i, cols], ALU.subtract, after=[t])
                bank.give(b, m)
                dve(V.tensor_tensor, o, o, rows("mu")[:, cols], ALU.mult)
                m = dve(V.tensor_tensor, o, o, zb[:, i, cols], ALU.add)
        r, k, v = zm[:, :, 0:256], zm[:, :, 256:512], zm[:, :, 512:768]
        act(S.activation, lo[:, :, 0:64], zm[:, :, 768:832], ACT.Tanh, after=[m])
        act(S.copy, lo[:, :, 64:128], zm[:, :, 832:896])
        m = act(S.activation, lo[:, :, 128:256], zm[:, :, 896:1024], ACT.Sigmoid)
        pe.wait(m)
        b = bank.take()
        for c in range(2):
            for i in range(NT):
                t = transpose(b, (2 * c + i) * P, lo[:, i, c * P:(c + 1) * P])
        t = pe.mark(t)
        m = act(S.copy, loT, bank[b].rearrange("p (c t) -> p c t", c=2), after=[t])
        bank.give(b, m)
        pe.wait(m)
        for i in range(NT):
            b = bank.take()
            t = pe.mark(T.matmul(bank[b], loT[:, 0, i * P:(i + 1) * P], small("lora"), start=True, stop=True))
            m = dve(V.tensor_tensor, wa[:, i, :], bank[b], rows("wa0"), ALU.add, after=[t])
            bank.give(b, m)
        b = bank.take()
        for i in range(NT):
            t = T.matmul(ps[:, b, 256 * i:256 * i + 256], loT[:, 1, i * P:(i + 1) * P], small("g_up"), start=True, stop=True)
        t = pe.mark(t)
        act(S.activation, wa, wa, ACT.Sigmoid, after=[m])
        m = act(S.copy, gg, bank[b].rearrange("p (i n) -> p i n", i=NT), after=[t])
        bank.give(b, m)
        a = wa[:, :, 256:512]
        lwr = dve(V.tensor_scalar, lw, wa[:, :, 0:256], -math.exp(-0.5), None, ALU.mult, after=[m])
        dve(V.tensor_tensor, kk, k, spread(rows("k_k"), 1, NT), ALU.mult)
        dve(V.tensor_tensor, tmp, kk, kk, ALU.mult)
        per_head = lambda ap: ap.rearrange("p i (h d) -> p (i h) d", h=4)
        ss = stat[:, 80:88]
        dve(V.tensor_reduce, ss, per_head(tmp), AXX, ALU.add)
        m = dve(V.tensor_scalar, ss, ss, 1e-24, None, ALU.max)
        rsqrt(ss, after=[m])
        dve(V.tensor_tensor, per_head(kk), per_head(kk), spread(ss, 2, HD), ALU.mult)
        dve(V.tensor_scalar, tmp, a, -1.0, None, ALU.add)
        dve(V.tensor_tensor, tmp, tmp, spread(rows("k_a"), 1, NT), ALU.mult)
        dve(V.tensor_scalar, tmp, tmp, 1.0, None, ALU.add)
        dve(V.tensor_tensor, k2, k, tmp, ALU.mult)
        pe.wait(lwr)
        b = bank.take()
        for i in range(NT):
            t = T.matmul(ps[:, b, 256 * i:256 * i + 256], C("tri64"), lw[:, i, :], start=True, stop=True)
        t = pe.mark(t)
        cum = bank[b].rearrange("p (i n) -> p i n", i=NT)
        m = dve(V.tensor_tensor, wx, cum, lw, ALU.subtract, after=[t])
        act(S.activation, wi, cum, ACT.Exp, after=[m])
        k_ = act(S.activation, wn, cum, ACT.Exp, scale=-1.0)
        bank.give(b, m, k_)
        m = act(S.activation, wx, wx, ACT.Exp, after=[m])
        b = bank.take()
        for pair in range(2):
            for i in range(NT):
                t = T.matmul(ps[:, b, 4 * pair + 2 * i:4 * pair + 2 * i + 2], lw[:, i, pair * P:(pair + 1) * P], C("half"),
                             start=True, stop=True)
        t = pe.mark(t)
        k_ = act(S.activation, wc, ps[:, b, 0:8].rearrange("p (a c) -> p a c", a=2), ACT.Exp, after=[t])
        bank.give(b, k_)
        kp, kq, kh, kr = (keep[:, :, e, :] for e in range(4))
        dve(V.tensor_tensor, kp, wx, kk, ALU.mult, after=[m])
        dve(V.tensor_tensor, tmp, kk, a, ALU.mult)
        dve(V.tensor_tensor, kq, tmp, wn, ALU.mult)
        dve(V.tensor_tensor, kh, k2, wn, ALU.mult)
        m = dve(V.tensor_tensor, kr, r, wi, ALU.mult)
        pe.wait(m)
        for src, dst in ((kp, pr[:, :, :, 0, :]), (kr, pr[:, :, :, 1, :]), (kq, qT.rearrange("p a (i t) -> p a i t", i=NT)),
                         (kh, hT.rearrange("p a (i t) -> p a i t", i=NT))):
            b = bank.take()
            for pair in range(2):
                for i in range(NT):
                    t = transpose(b, (2 * pair + i) * P, src[:, i, pair * P:(pair + 1) * P])
            t = pe.mark(t)
            m = act(S.copy, dst, bank[b].rearrange("p (a i t) -> p a i t", a=2, i=NT), after=[t])
            bank.give(b, m)
        w.at = shared
        prod = w(8, 4, P)
        reused = join()
        pe.wait(m)
        dve.wait(*reused)
        for i in range(NT):
            for hh in range(4):
                lo_p = 64 * (hh % 2)
                rhs = pr[lo_p:lo_p + 64, hh // 2, i].rearrange("p a t -> p (a t)")
                b = bank.take()
                for e, src in enumerate((qT, hT)):
                    t = T.matmul(ps[:, b, 256 * e:256 * e + 256], src[lo_p:lo_p + 64, hh // 2, i * P:(i + 1) * P], rhs,
                                 start=True, stop=True)
                t = pe.mark(t)
                m = dve(V.tensor_tensor, prod[:, 4 * i + hh], bank[b].rearrange("p (e t) -> p e t", e=4),
                        C("mask4").rearrange("p (e t) -> p e t", e=4), ALU.mult, after=[t])
                bank.give(b, m)
        zc = Carve(zbuf)
        xinv, xinvT, lev, cx = zc(8, P), zc(8, P), zc(8, P), zc(8, P)
        idb = spread(C("ident"), 1, 8)
        dve(V.tensor_copy, xinv, idb)
        m = dve(V.tensor_copy, xinvT, idb)
        lvl = C("levels").rearrange("p (l t) -> p l t", l=6)
        for l in range(6):
            m = dve(V.tensor_tensor, lev, prod[:, :, 0, :], spread(lvl[:, l, :], 1, 8), ALU.mult)
            pe.wait(m)
            for g in range(2):
                b = bank.take()
                for e in range(4):
                    t = T.matmul(ps[:, b, e * P:(e + 1) * P], lev[:, 4 * g + e, :], xinv[:, 4 * g + e, :], start=True, stop=True)
                t = pe.mark(t)
                k_ = act(S.copy, cx[:, 4 * g:4 * g + 4, :], bank[b].rearrange("p (e t) -> p e t", e=4), after=[t])
                bank.give(b, k_)
            pe.wait(k_)
            bx, bt = [], []
            for g in range(2):
                b1, b2 = bank.take(), bank.take()
                for e in range(4):
                    T.matmul(ps[:, b1, e * P:(e + 1) * P], xinvT[:, 4 * g + e, :], cx[:, 4 * g + e, :], start=True, stop=True)
                    t = T.matmul(ps[:, b2, e * P:(e + 1) * P], cx[:, 4 * g + e, :], xinvT[:, 4 * g + e, :], start=True, stop=True)
                bx.append(b1)
                bt.append(b2)
                t = pe.mark(t)
            for g in range(2):
                for b, dst in ((bx[g], xinv), (bt[g], xinvT)):
                    m = dve(V.tensor_tensor, dst[:, 4 * g:4 * g + 4, :], dst[:, 4 * g:4 * g + 4, :],
                            bank[b].rearrange("p (e t) -> p e t", e=4), ALU.subtract, after=[t])
                    bank.give(b, m)
        np_, utp, yg = xinv, lev, cx
        pe.wait(m)
        b = bank.take()
        for e in range(8):
            i, hh = divmod(e, 4)
            t = T.matmul(ps[:, b, e * HD:(e + 1) * HD], prod[:, e, 2, :], v[:, i, hh * HD:(hh + 1) * HD], start=True, stop=True)
        t = pe.mark(t)
        m = dve(V.tensor_copy, np_[:, :, 0:HD], bank[b].rearrange("p (e d) -> p e d", e=8), after=[t])
        bank.give(b, m)
        for i in range(NT):
            m = dve(V.tensor_copy, np_[:, 4 * i:4 * i + 4, HD:P], kp[:, i, :].rearrange("p (h d) -> p h d", h=4))
        pe.wait(m)
        for g in range(2):
            b = bank.take()
            for e in range(4):
                t = T.matmul(ps[:, b, e * P:(e + 1) * P], xinvT[:, 4 * g + e, :], np_[:, 4 * g + e, :], start=True, stop=True)
            t = pe.mark(t)
            m = dve(V.tensor_scalar, utp[:, 4 * g:4 * g + 4, :], bank[b].rearrange("p (e t) -> p e t", e=4), -1.0, None,
                    ALU.mult, after=[t])
            bank.give(b, m)
        pe.wait(m)
        for g in range(2):
            b = bank.take()
            for e in range(4):
                m3 = prod[:, 4 * g + e, 1, :]
                T.matmul(ps[:, b, e * P:e * P + HD], m3, utp[:, 4 * g + e, 0:HD], start=True, stop=False)
                T.matmul(ps[:, b, e * P:e * P + HD], prod[:, 4 * g + e, 3, :], v[:, g, e * HD:(e + 1) * HD],
                         start=False, stop=True)
                t = T.matmul(ps[:, b, e * P + HD:(e + 1) * P], m3, utp[:, 4 * g + e, HD:P], start=True, stop=True)
            t = pe.mark(t)
            src = bank[b].rearrange("p (e t) -> p e t", e=4)
            dve(V.tensor_copy, y[:, g, :].rearrange("p (h d) -> p h d", h=4), src[:, :, 0:HD], after=[t])
            m = dve(V.tensor_tensor, yg[:, 4 * g:4 * g + 4, 0:HD], src[:, :, HD:P],
                    kr[:, g, :].rearrange("p (h d) -> p h d", h=4), ALU.add)
            bank.give(b, m)
        pe.wait(m)
        gnat = w(NT, 256)
        for i in range(NT):
            m = dve(V.tensor_copy, gnat[:, i, :].rearrange("p (h d) -> p h d", h=4), yg[:, 4 * i:4 * i + 4, 0:HD])
        pe.wait(m)
        b = bank.take()
        for pair in range(2):
            for i in range(NT):
                t = transpose(b, (2 * pair + i) * P, gnat[:, i, pair * P:(pair + 1) * P])
        t = pe.mark(t)
        m = act(S.copy, gT, bank[b].rearrange("p (a t) -> p a t", a=2), after=[t])
        bank.give(b, m)
        fb = [bank.take(), bank.take()]
        eb = [bank.take(), bank.take()]
        for c in range(3):
            i, lo_t = c // 2, 64 * (c % 2)
            rows_c = slice(lo_t, lo_t + 64)
            for hh in range(4):
                e, lo_p = 4 * i + hh, 64 * (hh % 2)
                out = ps[lo_p:lo_p + 64, fb[c % 2], (2 * i + hh // 2) * HD:(2 * i + hh // 2 + 1) * HD]
                hc = slice(hh * HD, (hh + 1) * HD)
                T.matmul(out, kq[rows_c, i, hc], utp[rows_c, e, 0:HD], start=True, stop=False)
                t = T.matmul(out, kh[rows_c, i, hc], v[rows_c, i, hc], start=False, stop=True)
        for c in (1, 2):
            i, lo_t = c // 2, 64 * (c % 2)
            rows_c = slice(lo_t, lo_t + 64)
            for hh in range(4):
                e, lo_p = 4 * i + hh, 64 * (hh % 2)
                t = T.matmul(ps[lo_p:lo_p + 64, eb[c % 2], (hh // 2) * HD:(hh // 2 + 1) * HD],
                             utp[rows_c, e, HD:P], kq[rows_c, i, hh * HD:(hh + 1) * HD], start=True, stop=True)
        t = pe.mark(t)
        for c in range(3):
            m = dve(V.tensor_copy, st_f[:, :, c, :],
                    ps[:, fb[c % 2], 128 * (c // 2):128 * (c // 2) + 128].rearrange("p (a d) -> p a d", a=2), after=[t])
        for c in (1, 2):
            k_ = [dve(V.tensor_tensor, st_e[lo_p:lo_p + 64, c - 1], ps[lo_p:lo_p + 64, eb[c % 2], 0:128]
                      .rearrange("p (a d) -> p a d", a=2), spread(C("ident")[lo_p:lo_p + 64, lo_p:lo_p + 64], 1, 2), ALU.add)
                  for lo_p in (0, 64)][-1]
        for b in fb + eb:
            bank.give(b, k_)
        for pair in range(2):
            m = dve(V.tensor_scalar, state[:, 1, pair, :], st_f[:, pair, 0, :], wc[:, pair, 0:1], None, ALU.mult)
        for c in (1, 2):
            pe.wait(m)
            sbk = [bank.take(), bank.take()]
            for hh in range(4):
                lo_p = 64 * (hh % 2)
                t = T.matmul(ps[lo_p:lo_p + 64, sbk[hh % 2], (hh // 2) * HD:(hh // 2 + 1) * HD],
                             st_e[lo_p:lo_p + 64, c - 1, hh // 2, :], state[lo_p:lo_p + 64, c, hh // 2, :],
                             start=True, stop=True)
            t = pe.mark(t)
            for par in range(2):
                lo_p = 64 * par
                m = dve(V.tensor_tensor, state[lo_p:lo_p + 64, c + 1],
                        ps[lo_p:lo_p + 64, sbk[par], 0:128].rearrange("p (a d) -> p a d", a=2),
                        st_f[lo_p:lo_p + 64, :, c, :], ALU.add, after=[t])
                bank.give(sbk[par], m)
            for pair in range(2):
                m = dve(V.tensor_scalar, state[:, c + 1, pair, :], state[:, c + 1, pair, :], wc[:, pair, c:c + 1], None,
                        ALU.mult)
        pe.wait(m)
        yb = [bank.take(), bank.take()]
        for c in (1, 2, 3):
            lo_t = 64 * (c % 2)
            for hh in range(4):
                lo_p = 64 * (hh % 2)
                t = T.matmul(ps[lo_t:lo_t + 64, yb[hh % 2], (2 * (c // 2) + hh // 2) * HD:(2 * (c // 2) + hh // 2 + 1) * HD],
                             gT[lo_p:lo_p + 64, hh // 2, 64 * c:64 * c + 64], state[lo_p:lo_p + 64, c, hh // 2, :],
                             start=True, stop=True)
        t = pe.mark(t)
        yv = y.rearrange("p i (a b d) -> p i a b d", a=2, b=2)
        for par in range(2):
            src = ps[:, yb[par], 0:256].rearrange("p (i a d) -> p i a d", i=2, a=2)
            dve(V.tensor_tensor, yv[64:128, 0, :, par, :], yv[64:128, 0, :, par, :], src[64:128, 0], ALU.add, after=[t])
            m = dve(V.tensor_tensor, yv[:, 1, :, par, :], yv[:, 1, :, par, :], src[:, 1], ALU.add)
            bank.give(yb[par], m)
        t1, t2 = gnat, w(NT, 256)
        head_norm(per_head(y), 8, HD, 64e-5, per_head(t1))
        dve(V.tensor_tensor, y, y, spread(rows("gn_g"), 1, NT), ALU.mult)
        dve(V.tensor_tensor, y, y, spread(rows("gn_b"), 1, NT), ALU.add)
        dve(V.tensor_tensor, t1, r, k2, ALU.mult)
        dve(V.tensor_tensor, t1, t1, spread(rows("r_k"), 1, NT), ALU.mult)
        dve(V.tensor_reduce, ss, per_head(t1), AXX, ALU.add)
        for i in range(NT):
            dve(V.tensor_tensor, t2[:, i, :].rearrange("p (h d) -> p h d", h=4),
                v[:, i, :].rearrange("p (h d) -> p h d", h=4), spread(ss[:, 4 * i:4 * i + 4], 2, HD), ALU.mult)
        dve(V.tensor_tensor, y, y, t2, ALU.add)
        return dve(V.tensor_tensor, xn[:, :, 256:512], y, gg, ALU.mult)

    def route(small, ready):
        lw = Carve(stat, 96)
        L, ex = lw(NT, NE), lw(NT, NE)
        ww = Carve(zbuf, NE * SEQ)
        gt, eq, rank = ww(NE, NE), ww(NE, NE), ww(NT, NE)
        gate_all = zbuf[:, 0:NE * SEQ].rearrange("p (e t) -> p e t", e=NE)
        pe.wait(ready)
        b = bank.take()
        router = small("router").rearrange("p (k e) -> p k e", k=KD)
        for i in range(NT):
            for k in range(KD):
                t = T.matmul(ps[:, b, NE * i:NE * i + NE], xt[:, k, i * P:(i + 1) * P], router[:, k, :],
                             start=(k == 0), stop=(k == KD - 1))
        t = pe.mark(t)
        m = dve(V.tensor_tensor, L, ps[:, b, 0:NT * NE].rearrange("p (i e) -> p i e", i=NT), spread(small("rb"), 1, NT),
                ALU.add, after=[t])
        bank.give(b, m)
        for i in range(NT):
            other, own = spread(L[:, i, :], 1, NE), spread(L[:, i, :], 2, NE)
            dve(V.tensor_tensor, gt, other, own, ALU.is_gt)
            dve(V.tensor_tensor, eq, other, own, ALU.is_equal)
            dve(V.tensor_tensor, eq, eq, C("before").rearrange("p (e j) -> p e j", e=NE), ALU.mult)
            dve(V.tensor_tensor, gt, gt, eq, ALU.add)
            dve(V.tensor_reduce, rank[:, i, :], gt, AXX, ALU.add)
        dve(V.tensor_scalar, rank, rank, 1.5, None, ALU.is_lt)
        dve(V.tensor_copy, ex, L)
        sm = stat[:, 48:48 + NT]
        dve(V.tensor_reduce, sm, L, AXX, ALU.max)
        m = dve(V.tensor_tensor, ex, ex, spread(sm, 2, NE), ALU.subtract)
        m = act(S.activation, ex, ex, ACT.Exp, after=[m])
        dve(V.tensor_tensor, ex, ex, rank, ALU.mult, after=[m])
        dve(V.tensor_reduce, sm, ex, AXX, ALU.add)
        dve(V.reciprocal, sm, sm)
        m = dve(V.tensor_tensor, ex, ex, spread(sm, 2, NE), ALU.mult)
        rep = xn.rearrange("p i n -> p (i n)")[:, 0:NT * NE * P].rearrange("p (i e t) -> p i e t", i=NT, e=NE)
        for i in range(NT):
            m = dve(V.tensor_copy, rep[:, i], spread(ex[:, i, :], 2, P))
        pe.wait(m)
        for i in range(NT):
            for e0 in range(0, NE, 4):
                b = bank.take()
                for e in range(4):
                    t = T.matmul(ps[:, b, e * P:(e + 1) * P], rep[:, i, e0 + e, :], C("ident"), start=True, stop=True)
                t = pe.mark(t)
                m = dve(V.tensor_copy, gate_all[:, e0:e0 + 4, i * P:(i + 1) * P],
                        bank[b].rearrange("p (e t) -> p e t", e=4), after=[t])
                bank.give(b, m)
        return gate_all, m

    z1 = zbuf[:, 0:NT * DIN1].rearrange("p (i n) -> p i n", i=NT)
    keep_small = sb("layer_cols", 256)
    for l in range(2):
        ring.schedule(layer_tiles(l))
        buf, got = ring.get("small")
        small = columns(buf, small1)
        rbuf, got_rows = ring.get("rows")
        rows = columns(rbuf, rows1)
        at_router = small1["router"][0]
        a = dve(V.tensor_copy, keep_small[:, 0:24], buf[:, 0:24], after=[got] + join())
        dve(V.tensor_copy, keep_small[:, 24:88], buf[:, at_router:at_router + 64])
        dve(V.tensor_copy, keep_small[:, 88:96], small("rb"))
        kept = columns(keep_small, {"g_mix": (0, 8), "g_ffn": (8, 8), "g_ple": (16, 8), "router": (24, 64), "rb": (88, 8)})
        m = rms_rows([], xn)
        m = turn_xn([m], kept("g_mix"))
        m = project(z1, DIN1, "win", m)
        ready = [m, got, got_rows]
        act.wait(*join())
        m1 = spatial_gating(z1, small, ready)
        j1 = join()
        for e in (dve, act, pe):
            e.wait(*j1)
        sparse_attention(z1, small, ready, l)
        j1 = join()
        for e in (dve, act, pe):
            e.wait(*j1)
        m = time_mix(z1, small, rows, ready)
        done = join()
        ring.release("small", *done)
        ring.release("rows", *done)
        turned = turn_xn(done)
        m = out_project("wout", turned, add_residual)
        m = rms_rows(join(), xn)
        m = turn_xn([m], kept("g_ffn"), after_w=join())
        if l == 0:
            m = feed_forward(d["ffn"], 1, 0, None, m, add_residual)
        else:
            gate_all, g = route(kept, m)
            m = feed_forward(d["moe"], NE, 0, gate_all, [m, g], add_residual)
        ring.schedule(ple_tiles(l))
        m = rms_rows(join(), xn)
        m = turn_xn([m], kept("g_ple"))
        up, got_up = ring.get("ple_up")
        pT = up[:, 2 * D:2 * D + 2 * SEQ].rearrange("p (k t) -> p k t", k=2)
        tb = Carve(work)
        sg = tb(2, COLS)
        pe.wait(m)
        free_sg = [[], []]
        for c in range(3):
            n = min(COLS, D - c * COLS)
            wt, got_w = ring.get(f"pleg{c}")
            wt = wt[:, 0:KD * n].rearrange("p (k n) -> p k n", k=KD)
            pe.wait(got_w, got_up)
            for i in range(NT):
                b = bank.take()
                for k in range(KD):
                    t = T.matmul(ps[:, b, 0:n], xt[:, k, i * P:(i + 1) * P], wt[:, k, :], start=(k == 0), stop=(k == KD - 1))
                t = pe.mark(t)
                m = act(S.activation, sg[:, i, 0:n], ps[:, b, 0:n], ACT.Sigmoid, after=[t] + free_sg[i])
                bank.give(b, m)
                b = bank.take()
                for k in range(2):
                    u = T.matmul(ps[:, b, 0:n], pT[:, k, i * P:(i + 1) * P], up[:, k * D + c * COLS:k * D + c * COLS + n],
                                 start=(k == 0), stop=(k == 1))
                u = pe.mark(u)
                m = dve(V.tensor_tensor, sg[:, i, 0:n], sg[:, i, 0:n], ps[:, b, 0:n], ALU.mult, after=[m, u])
                bank.give(b, m)
                hs = h[:, i, c * COLS:c * COLS + n]
                m = dve(V.tensor_tensor, hs, hs, sg[:, i, 0:n], ALU.add)
                free_sg[i] = [m]
            ring.release(f"pleg{c}", u)
        ring.release("ple_up", u)

    ring.schedule([("final1", [(d["g_final"][0:1].to_broadcast([P, D]), 0)])])
    gf, got = ring.get("final1")
    rms_rows(join(), xn)
    m = dve(V.tensor_tensor, h, xn, spread(gf[:, 0:D], 1, NT), ALU.mult, after=[got])
    ring.release("final1", m)

    z2 = zbuf[:, 0:NT * DIN2].rearrange("p (i n) -> p i n", i=NT)
    loaded_const = fetch(cst[:, 0:width2], d["const2"], after=join())
    const[0] = tab2
    for e in (dve, act, pe):
        e.wait(loaded_const)
    cos2, sin2, rope2 = rope_tables(posi[:, NT:2 * NT], C("inv2"), 32, Carve(work), join())
    small2, n_small2 = spans(SMALL2)
    rows2, n_rows2 = spans(ROWS2, n_small2)
    small2.update(rows2)
    rows2b, _ = spans(ROWS2B)

    def layer2_tiles(l):
        out = [("small", [(d["small2"][l], 0), (d["rows2"][l:l + 1].to_broadcast([P, d["rows2"].shape[1]]), n_small2)]),
               ("gateb", [(d["rows2b"][l:l + 1].to_broadcast([P, d["rows2b"].shape[1]]), 0)])]
        out += [(f"ada{c}", [(d["ada"][l, c], 0)]) for c in range(16)]
        for c in range(-(-DIN2 // COLS)):
            n = min(COLS, DIN2 - c * COLS)
            out.append((f"win{c}", [(d["w_in2"][l, c, :, 0:KD * n], 0)]))
        out += [(f"wout{c}", [(d["w_out2"][l, c], 0)]) for c in range(3)]
        return out

    def adaptive(small, gateb, ready):
        w = Carve(work)
        ca, cb, mod = w(KD), w(KD, P), keep_small[:, 128:176]
        m = act(S.activation, ca, small("c"), ACT.Silu, after=ready)
        m = dve(V.tensor_copy, cb, spread(ca, 2, P), after=[m])
        pe.wait(m)
        bm = bank.take()
        bg = [bank.take() for _ in range(4)]
        for c in range(16):
            wt, got = ring.get(f"ada{c}")
            wt = wt.rearrange("p (k n) -> p k n", k=KD)
            pe.wait(got)
            for e in range(3):
                n = 3 * c + e
                part, blk = divmod(n, KD)
                for k in range(KD):
                    cols = wt[:, k, e * P:(e + 1) * P]
                    if part in (2, 5):
                        g = (part == 5) * 2 + blk // 4
                        t = T.matmul(ps[:, bg[g], (blk % 4) * P:(blk % 4 + 1) * P], cb[:, k, :], cols,
                                     start=(k == 0), stop=(k == KD - 1))
                    else:
                        t = T.matmul(ps[:, bm, n:n + 1], cols, ca[:, k:k + 1], start=(k == 0), stop=(k == KD - 1))
            t = pe.mark(t)
            ring.release(f"ada{c}", t)
        for a, b in ((0, 16), (24, 40)):
            m = dve(V.tensor_tensor, mod[:, a:b], ps[:, bm, a:b], small("ada_b")[:, a:b], ALU.add, after=[t])
        bank.give(bm, m)
        for g in range(4):
            bias = (small("gate_b") if g < 2 else gateb)[:, (g % 2) * 512:(g % 2 + 1) * 512]
            m = dve(V.tensor_tensor, gates2[:, g // 2, (g % 2) * 512:(g % 2 + 1) * 512], bank[bg[g]], bias, ALU.add)
            bank.give(bg[g], m)
        gains = keep_small[:, 176:192]
        for e, (sc_at, name) in enumerate(((8, "g_mix"), (32, "g_ffn"))):
            o = gains[:, 8 * e:8 * e + 8]
            dve(V.tensor_scalar, o, mod[:, sc_at:sc_at + 8], 1.0, None, ALU.add)
            m = dve(V.tensor_tensor, o, o, small(name), ALU.mult)
        return gains, mod, m

    def fox(z, small, ready):
        w = Carve(work)
        qT, kT = w(NT, 2, P), w(2, SEQ)
        lf, e1, cq, rep = w(NT, 4), w(NT, 4), w(NT, 4), w(NT * 4, P)
        ck, cm, sbuf, pt, o = w(4, SEQ), w(4, SEQ), w(4 * SEQ), w(8, P), w(4, HD)
        dve(V.tensor_tensor, lf, z[:, :, 768:772], spread(small("fb"), 1, NT), ALU.add, after=ready)
        dve(V.tensor_scalar, cq, lf, -1.0, None, ALU.mult)
        m = dve(V.tensor_tensor, e1, lf, cq, ALU.max)
        m = act(S.activation, e1, e1, ACT.Exp, scale=-1.0, after=[m])
        m = dve(V.tensor_scalar, e1, e1, 1.0, None, ALU.add, after=[m])
        m = act(S.activation, e1, e1, ACT.Ln, after=[m])
        dve(V.tensor_scalar, lf, lf, 0.0, None, ALU.min, after=[m])
        dve(V.tensor_tensor, lf, lf, e1, ALU.subtract)
        m = dve(V.tensor_copy, rep, spread(lf.rearrange("p i h -> p (i h)"), 2, P))
        pe.wait(m, *ready)
        b = bank.take()
        T.matmul(ps[:, b, 0:4], C("tri"), lf[:, 0, :], start=True, stop=True)
        T.matmul(ps[:, b, 4:8], C("tri"), lf[:, 1, :], start=True, stop=False)
        t = pe.mark(T.matmul(ps[:, b, 4:8], C("ones"), lf[:, 0, :], start=False, stop=True))
        m = dve(V.tensor_copy, cq, ps[:, b, 0:8].rearrange("p (i h) -> p i h", i=NT), after=[t])
        bank.give(b, m)
        for pair in range(2):
            b = bank.take()
            for e in range(2):
                hh = 2 * pair + e
                T.matmul(ps[:, b, e * SEQ:e * SEQ + P], rep[:, hh, :], C("tri"), start=True, stop=True)
                T.matmul(ps[:, b, e * SEQ + P:(e + 1) * SEQ], rep[:, 4 + hh, :], C("tri"), start=True, stop=False)
                t = T.matmul(ps[:, b, e * SEQ + P:(e + 1) * SEQ], rep[:, hh, :], C("ones"), start=False, stop=True)
            t = pe.mark(t)
            m = dve(V.tensor_copy, ck[:, 2 * pair:2 * pair + 2, :], bank[b].rearrange("p (a s) -> p a s", a=2), after=[t])
            bank.give(b, m)
        for which in range(2):
            b = bank.take()
            for pair in range(2):
                for i in range(NT):
                    t = transpose(b, (2 * pair + i) * P, z[:, i, 256 * which + pair * P:256 * which + (pair + 1) * P])
            t = pe.mark(t)
            src = bank[b].rearrange("p (a i t) -> p a i t", a=2, i=NT)
            if which == 0:
                m = act(S.mul, qT.rearrange("p i a t -> p a i t"), src, HD ** -0.5, after=[t])
            else:
                m = act(S.copy, kT.rearrange("p a (i t) -> p a i t", i=NT), src, after=[t])
            bank.give(b, m)
        turned = m
        last = [dve.now()]
        for i in range(NT):
            n = P * (i + 1)
            pe.wait(turned, *last)
            dve(V.tensor_tensor, cm[:, :, 0:n], spread(C("causal")[:, P * i:P * i + n], 1, 4), ck[:, :, 0:n], ALU.subtract,
                after=last)
            s4 = sbuf[:, 0:4 * n].rearrange("p (h s) -> p h s", h=4)
            for par in range(2):
                b = bank.take()
                for a in range(2):
                    t = T.matmul(ps[:, b, a * n:(a + 1) * n], qT[64 * par:64 * par + 64, i, a, :],
                                 kT[64 * par:64 * par + 64, a, 0:n], start=True, stop=True)
                t = pe.mark(t)
                for a in range(2):
                    hh = 2 * a + par
                    m = dve(V.scalar_tensor_tensor, out=s4[:, hh, :], in0=ps[:, b, a * n:(a + 1) * n],
                            scalar=cq[:, i, hh:hh + 1], in1=cm[:, hh, 0:n], op0=ALU.add, op1=ALU.add, after=[t])
                bank.give(b, m)
            rs, m = softmax_rows(s4, 4)
            b, t = weighted_values(s4, 4, i + 1, pt[:, 0:4 * (i + 1), :],
                                   lambda mm, st: z[:, st, 512 + mm * HD:512 + (mm + 1) * HD], m)
            m = dve(V.tensor_tensor, xn[:, i, 0:256].rearrange("p (h d) -> p h d", h=4),
                    ps[:, b, 0:256].rearrange("p (h d) -> p h d", h=4), spread(rs, 2, HD), ALU.mult, after=[t])
            bank.give(b, m)
            last = [m]
        return m

    def pooling(z, small, ready):
        w = Carve(work)
        dT = w(2, SEQ)
        band = C("band").rearrange("p (g n) -> p g n", g=4)
        pe.wait(*ready)
        b = bank.take()
        for g in range(4):
            o = ps[64 * (g % 2):64 * (g % 2) + 64, b, (g // 2) * SEQ:(g // 2 + 1) * SEQ]
            u0, u1 = (z[:, i, 772 + g * HD:772 + (g + 1) * HD] for i in range(NT))
            T.matmul(o[:, 0:P], u0, band[:, g, 0:P], start=True, stop=True)
            T.matmul(o[:, P:SEQ], u0, band[:, g, P:SEQ], start=True, stop=False)
            t = T.matmul(o[:, P:SEQ], u1, band[:, g, SEQ:SEQ + P], start=False, stop=True)
        t = pe.mark(t)
        m = act(S.copy, dT, bank[b].rearrange("p (a t) -> p a t", a=2), after=[t] + ready)
        bank.give(b, m)
        pe.wait(m)
        pw = small("pool_w").rearrange("p (a d) -> p a d", a=2)
        for par in range(2):
            b = bank.take()
            for i in range(NT):
                for a in range(2):
                    t = T.matmul(ps[:, b, (2 * i + a) * HD:(2 * i + a + 1) * HD], dT[64 * par:64 * par + 64, a, i * P:(i + 1) * P],
                                 pw[64 * par:64 * par + 64, a, :], start=True, stop=True)
            t = pe.mark(t)
            for i in range(NT):
                m = dve(V.tensor_tensor, xn[:, i, 256:512].rearrange("p (a b d) -> p a b d", a=2, b=2)[:, :, par, :],
                        ps[:, b, i * P:(i + 1) * P].rearrange("p (a d) -> p a d", a=2),
                        small("pool_scale").rearrange("p (a b d) -> p a b d", a=2, b=2)[:, :, par, :], ALU.mult, after=[t])
            bank.give(b, m)
        return m

    def retention(z, small, ready):
        w = Carve(work)
        qk, tmp = w(2, NT, 256), w(1024)
        qT, kT, st, o, t1 = w(2, SEQ), w(2, SEQ), w(4, 384), w(NT, 256), w(NT, 256)
        hv = lambda ap: ap.rearrange("p i (h d) -> p i h d", h=4)
        for which in range(2):
            src = z[:, :, 1028 + 256 * which:1284 + 256 * which]
            m = rotate(hv(qk[:, which]), hv(src), 4, 32, cos2, sin2, tmp, after=ready + [rope2])
        pe.wait(m)
        for which, dst in ((0, qT), (1, kT)):
            b = bank.take()
            for pair in range(2):
                for i in range(NT):
                    t = transpose(b, (2 * pair + i) * P, qk[:, which, i, pair * P:(pair + 1) * P])
            t = pe.mark(t)
            m = act(S.copy, dst, bank[b].rearrange("p (a t) -> p a t", a=2), after=[t])
            bank.give(b, m)
        pe.wait(m)
        dec = C("decay").rearrange("p (h n) -> p h n", h=4)
        for hh in range(4):
            lo_p = 64 * (hh % 2)
            b = bank.take()
            qh, kh = qT[lo_p:lo_p + 64, hh // 2, :], kT[lo_p:lo_p + 64, hh // 2, :]
            T.matmul(ps[:, b, 0:SEQ], kh[:, 0:P], qh, start=True, stop=True)
            t = pe.mark(T.matmul(ps[:, b, SEQ:SEQ + P], kh[:, P:SEQ], qh[:, P:SEQ], start=True, stop=True))
            m = dve(V.tensor_tensor, st[:, hh, :], ps[:, b, 0:384], dec[:, hh, :], ALU.mult, after=[t])
            bank.give(b, m)
        pe.wait(m)
        b = bank.take()
        for hh in range(4):
            v = lambda i: z[:, i, 1540 + hh * HD:1540 + (hh + 1) * HD]
            T.matmul(ps[:, b, hh * HD:(hh + 1) * HD], st[:, hh, 0:P], v(0), start=True, stop=True)
            T.matmul(ps[:, b, 256 + hh * HD:256 + (hh + 1) * HD], st[:, hh, P:SEQ], v(0), start=True, stop=False)
            t = T.matmul(ps[:, b, 256 + hh * HD:256 + (hh + 1) * HD], st[:, hh, SEQ:SEQ + P], v(1), start=False, stop=True)
        t = pe.mark(t)
        m = dve(V.tensor_copy, o, bank[b].rearrange("p (i n) -> p i n", i=NT), after=[t])
        bank.give(b, m)
        g = act(S.activation, tmp[:, 0:512].rearrange("p (i n) -> p i n", i=NT), z[:, :, 1796:2052], ACT.Silu,
                after=ready + [dve.now()])
        per_head = lambda ap: ap.rearrange("p i (h d) -> p (i h) d", h=4)
        head_norm(per_head(o), 8, HD, 1e-6, per_head(t1))
        dve(V.tensor_tensor, o, o, spread(small("gn_g"), 1, NT), ALU.mult)
        return dve(V.tensor_tensor, xn[:, :, 512:768], o, tmp[:, 0:512].rearrange("p (i n) -> p i n", i=NT), ALU.mult,
                   after=[g])

    def conformer(z, small, ready):
        w = Carve(work)
        gl, padded, acc, y, t1 = w(NT, 256), w(2, CONVW - 1 + SEQ), w(2, SEQ), w(NT, 256), w(NT, 256)
        m = act(S.activation, gl, z[:, :, 2308:2564], ACT.Sigmoid, after=ready)
        m = dve(V.tensor_tensor, gl, gl, z[:, :, 2052:2308], ALU.mult, after=[m])
        dve(V.memset, padded[:, :, 0:CONVW - 1], 0.0)
        pe.wait(m)
        b = bank.take()
        for a in range(2):
            for i in range(NT):
                t = transpose(b, (2 * a + i) * P, gl[:, i, a * P:(a + 1) * P])
        t = pe.mark(t)
        m = act(S.copy, padded[:, :, CONVW - 1:], bank[b].rearrange("p (a t) -> p a t", a=2), after=[t, dve.now()])
        bank.give(b, m)
        cw = small("conv_w").rearrange("p (a j) -> p a j", a=2)
        for a in range(2):
            dve(V.tensor_scalar, acc[:, a, :], padded[:, a, 0:SEQ], cw[:, a, 0:1], small("conv_b")[:, a:a + 1],
                ALU.mult, ALU.add, after=[m])
        for j in range(1, CONVW):
            for a in range(2):
                m = dve(V.scalar_tensor_tensor, out=acc[:, a, :], in0=padded[:, a, j:j + SEQ], scalar=cw[:, a, j:j + 1],
                        in1=acc[:, a, :], op0=ALU.mult, op1=ALU.add)
        pe.wait(m)
        b = bank.take()
        for i in range(NT):
            for a in range(2):
                t = transpose(b, (2 * i + a) * P, acc[:, a, i * P:(i + 1) * P])
        t = pe.mark(t)
        m = dve(V.tensor_copy, y, bank[b].rearrange("p (i n) -> p i n", i=NT), after=[t])
        bank.give(b, m)
        head_norm(y, NT, 256, 1e-6, t1)
        dve(V.tensor_tensor, y, y, spread(small("ln_g"), 1, NT), ALU.mult)
        m = dve(V.tensor_tensor, y, y, spread(small("ln_b"), 1, NT), ALU.add)
        return act(S.activation, xn[:, :, 768:1024], y, ACT.Silu, after=[m])

    def gated_add(which):
        def add(i, q, src, t):
            tmp = xn[:, i, q * 512:(q + 1) * 512]
            dve(V.tensor_tensor, tmp, src, gates2[:, which, q * 512:(q + 1) * 512], ALU.mult, after=[t])
            hs = h[:, i, q * 512:(q + 1) * 512]
            return dve(V.tensor_tensor, hs, hs, tmp, ALU.add)
        return add

    for l in range(2):
        ring.schedule(layer2_tiles(l))
        buf, got = ring.get("small")
        small = columns(buf, small2)
        gb, got_gb = ring.get("gateb")
        gains, mod, m = adaptive(small, gb, [got, got_gb] + join())
        ring.release("gateb", m)
        rms_rows(join(), xn)
        m = turn_xn([dve.now()], gains[:, 0:8], mod[:, 0:8])
        m = project(z2, DIN2, "win", m)
        ready = [m, got]
        for mixer in (fox, pooling, retention, conformer):
            j1 = join()
            for e in (dve, act, pe):
                e.wait(*j1)
            mixer(z2, small, ready)
        done = join()
        ring.release("small", *done)
        turned = turn_xn(done)
        m = out_project("wout", turned, gated_add(0))
        m = rms_rows(join(), xn)
        m = turn_xn([m], gains[:, 8:16], mod[:, 24:32], after_w=join())
        m = feed_forward(d["ffn2"], 1, l * FB, None, m, gated_add(1))

    ring.schedule([("final2", [(d["g_final"][1:2].to_broadcast([P, D]), 0)])])
    gf, got = ring.get("final2")
    rms_rows(join(), xn)
    m = dve(V.tensor_tensor, xn, xn, spread(gf[:, 0:D], 1, NT), ALU.mult, after=[got])
    sp.wait(m)
    s_out = nc.alloc_semaphore("s_out")
    nc.sync.dma_start(d["out"], xn).then_inc(s_out, 16)
    nc.sync.wait_ge(s_out, 16)


def column_tiles(w, cols=COLS):
    L, _, n = w.shape
    t = -(-n // cols)
    out = np.zeros((L, t, P, KD * cols), np.float32)
    for c in range(t):
        m = min(cols, n - c * cols)
        out[:, c, :, 0:KD * m] = w[:, :, c * cols:c * cols + m].reshape(L, KD, P, m).transpose(0, 2, 1, 3).reshape(L, P, KD * m)
    return out


def row_tiles(w):
    L = w.shape[0]
    out = np.zeros((L, 3, P, 3, D), np.float32)
    blocks = w.reshape(L, KD, P, D)
    for k in range(KD):
        out[:, k // 3, :, k % 3] = blocks[:, k]
    return out.reshape(L, 3, P, 3 * D)


def ffn_tiles(w1, w3, w2):
    E = w1.shape[0]
    out = np.empty((E, FB, P, 3, D), np.float32)
    for e, w in enumerate((w1, w3)):
        out[:, :, :, e] = w.reshape(E, KD, P, FB, P).transpose(0, 3, 2, 1, 4).reshape(E, FB, P, D)
    out[:, :, :, 2] = w2.reshape(E, FB, P, D)
    return out.reshape(E * FB, P, 3 * D)


def by_partition(v):
    return v.reshape(v.shape[0], -1, P).transpose(0, 2, 1)


def pack(fields, values):
    return np.concatenate([np.asarray(values[n], np.float32).reshape(2, P, w) for n, w in fields], axis=2)


def pack_rows(fields, values):
    return np.concatenate([values[n].reshape(2, w) for n, w in fields], axis=1)


def lay_out(a):
    one, two = const_arrays()
    w_in = a["w_in"]
    zc = 1536
    q = w_in[:, :, zc:zc + 512].reshape(2, D, 2, 4, HD).transpose(0, 1, 3, 2, 4).reshape(2, D, 512)
    gates = w_in[:, :, zc + 1280:].reshape(2, D, 2, 4, 3).transpose(0, 1, 4, 3, 2).reshape(2, D, 24)
    w_in = np.concatenate([w_in[:, :, :zc], q, w_in[:, :, zc + 512:zc + 1280], gates], axis=2)
    w_out = a["w_out"]
    tail = w_out[:, 512:].reshape(2, 2, 4, HD, D).transpose(0, 2, 1, 3, 4).reshape(2, 512, D)
    w_out = np.concatenate([w_out[:, :512], tail], axis=1)
    lora = np.zeros((2, P, 512), np.float32)
    lora[:, :64, :256] = a["rw_w_up"]
    lora[:, 64:, 256:] = a["rw_a_up"]
    pos = a["nsa_cmp_pos"].reshape(2, 16, 2, HD).transpose(0, 2, 3, 1).reshape(2, P, 16)
    router = a["router_w"].reshape(1, KD, P, NE).transpose(0, 2, 1, 3).reshape(1, P, KD * NE)
    small1 = pack(SMALL1, {
        "g_mix": by_partition(a["g_mix"]), "g_ffn": by_partition(a["g_ffn"]), "g_ple": by_partition(a["g_ple"]),
        "kc_w2": a["nsa_kc_w2"], "vc_w2": a["nsa_vc_w2"], "pos": pos, "lora": lora, "g_up": a["rw_g_up"],
        "wst": a["gm_ws"].transpose(0, 3, 1, 2).reshape(2, P, 512), "bs": a["gm_bs"].transpose(0, 2, 1),
        "router": np.concatenate([router, router])})
    rows1 = pack_rows(ROWS1, {"mu": a["rw_mu"], "wa0": np.concatenate([a["rw_w0"], a["rw_a0"]], 1), "k_k": a["rw_k_k"],
                              "k_a": a["rw_k_a"], "r_k": a["rw_r_k"], "gn_g": a["rw_gn_g"], "gn_b": a["rw_gn_b"]})
    rows1b = pack_rows(ROWS1B, {"ln_g": a["gm_ln_g"], "ln_b": a["gm_ln_b"],
                                "rb": np.concatenate([a["router_b"], a["router_b"]])})
    cmp_w1 = lambda w: w.reshape(2, 16, P, P).transpose(0, 2, 1, 3).reshape(2, P, 2048)
    ple = np.concatenate([a["ple_proj_w"].reshape(2, 2, P, D).transpose(0, 2, 1, 3).reshape(2, P, 2 * D),
                          a["p"].reshape(2, SEQ, 2, P).transpose(0, 3, 2, 1).reshape(2, P, 2 * SEQ)], axis=2)
    ada_b = a["ada_b_2"]
    c = by_partition(a["c_2"])
    pool_w = a["pool_w_2"].reshape(2, 2, 2, HD, HD).transpose(0, 2, 3, 1, 4).reshape(2, P, 128)
    conv_w = a["conv_w_2"].reshape(2, CONVW, 2, P).transpose(0, 3, 2, 1).reshape(2, P, 62)
    small2 = pack(SMALL2, {
        "g_mix": by_partition(a["norm_mix_g_2"]), "g_ffn": by_partition(a["norm_ffn_g_2"]), "pool_w": pool_w,
        "conv_w": conv_w, "conv_b": by_partition(a["conv_b_2"]), "ada_b": by_partition(ada_b),
        "c": np.concatenate([c, c])})
    rows2 = pack_rows(ROWS2, {"pool_scale": a["pool_scale_2"], "gn_g": a["ret_gn_g_2"], "ln_g": a["conv_ln_g_2"],
                              "ln_b": a["conv_ln_b_2"], "gate_b": ada_b[:, 2 * D:3 * D], "fb": a["fox_fb_2"]})
    tokens = lambda v: v.reshape(NT, P).transpose(1, 0)
    return {
        "const1": np.concatenate(list(one.values()), 1), "const2": np.concatenate(list(two.values()), 1),
        "x": a["x"].reshape(NT, P, D).transpose(1, 0, 2),
        "pos": np.concatenate([tokens(a["positions"]), tokens(a["positions_2"])], 1),
        "small1": small1, "rows1": rows1, "rows1b": rows1b, "w_in": column_tiles(w_in), "w_out": row_tiles(w_out),
        "kc_w1": cmp_w1(a["nsa_kc_w1"]), "vc_w1": cmp_w1(a["nsa_vc_w1"]), "ple_proj": ple,
        "ple_gate": column_tiles(a["ple_gate_w"]), "ffn": ffn_tiles(a["ffn_w1"], a["ffn_w3"], a["ffn_w2"]),
        "moe": ffn_tiles(a["moe_w1"][0], a["moe_w3"][0], a["moe_w2"][0]),
        "g_final": np.concatenate([a["g_final"], a["final_g_2"]]).reshape(2, D),
        "small2": small2, "rows2": rows2, "rows2b": ada_b[:, 5 * D:6 * D], "ada": column_tiles(a["ada_w_2"]),
        "w_in2": column_tiles(a["w_in_2"]), "w_out2": row_tiles(a["w_out_2"]),
        "ffn2": ffn_tiles(a["ffn_w1_2"], a["ffn_w3_2"], a["ffn_w2_2"]),
    }


def kernel(**inputs):
    import concourse.bacc as bacc
    from concourse.bass_utils import run_bass_kernel_spmd

    arrays = lay_out({k: np.asarray(v) for k, v in inputs.items()})
    nc = bacc.Bacc("TRN2", target_bir_lowering=False, num_devices=1)
    ins, d = {}, {}
    for name, v in arrays.items():
        v = np.ascontiguousarray(v)
        ins["in_" + name] = v
        d[name] = nc.dram_tensor("in_" + name, v.shape, mybir.dt.from_np(v.dtype), kind="ExternalInput").ap()
    d["out"] = nc.dram_tensor("out", (P, NT, D), F32, kind="ExternalOutput").ap()
    build(nc, d)
    r = run_bass_kernel_spmd(nc, [ins], core_ids=[0])
    out = r.results[0]["out"]
    return np.ascontiguousarray(out.transpose(1, 0, 2).reshape(1, SEQ, D))
```

```python
import math

import numpy as np

import concourse.bass as bass
from concourse import mybir
from concourse.mybir import EngineType

F32 = mybir.dt.float32
I32 = mybir.dt.int32
ALU = mybir.AluOpType
ACT = mybir.ActivationFunctionType
AXX = mybir.AxisListType.X
LOADER = (EngineType.SP,)
WORKERS = (EngineType.PE, EngineType.Activation, EngineType.DVE)

P = 128
SEQ, D = 256, 1024
NT = SEQ // P
KD = D // P
HD = 64
FF = 2816
FB = FF // P
NE = 8
SLOT = 3072
NSLOT = 11
NWALK = 4
COLS = SLOT // KD
DIN1, DIN2 = 2840, 2564
NEG = -1e30
NCMP = (SEQ - 32) // 16 + 1
POOLW = (2, 4, 8, 16)
CONVW = 31


def const_arrays():
    s = np.arange(P)[:, None]
    t = np.arange(P)[None, :]
    f = np.float32
    one = {}
    one["ident"] = (s == t)
    one["tri"] = (s <= t)
    same = (s // 64 == t // 64)
    one["tri64"] = (s <= t) & same
    one["shift"] = (t == s + 1)
    one["carry"] = (s == P - 1) & (t == 0)
    strict, incl = (s < t) & same, (s <= t) & same
    one["mask4"] = np.concatenate([strict, incl, strict, incl], 1)
    one["levels"] = np.concatenate(
        [((s // (2 * b) == t // (2 * b)) & (s % (2 * b) < b) & (t % (2 * b) >= b)) for b in (1, 2, 4, 8, 16, 32)], 1)
    one["half"] = (np.arange(P)[:, None] // 64 == np.arange(2)[None, :])
    tok = np.arange(P)[:, None, None] + P * np.arange(NT)[None, :, None]
    end = (np.arange(NCMP) * 16 + 31)[None, None, :]
    one["cmp01"] = (end <= tok).reshape(P, -1)
    one["cmpneg"] = np.where(end <= tok, 0.0, NEG).reshape(P, -1)
    one["before"] = np.broadcast_to((np.arange(8)[None, :] < np.arange(8)[:, None]).reshape(1, 64), (P, 64))
    one["inv1"] = np.broadcast_to((1.0 / (f(500000.0) ** (np.arange(0, 16, 2, dtype=f) / f(16)))).astype(f)[None], (P, 8))
    diag = np.where(t <= s, 0.0, NEG)
    one["causal"] = np.concatenate([diag, np.zeros((P, P)), diag], 1)
    one["ones"] = np.ones((P, P))
    one["slots"] = np.broadcast_to(np.arange(P)[None, :], (P, P))
    two = {k: one[k] for k in ("ident", "tri", "causal", "ones")}
    sk = np.arange(SEQ)[:, None]
    tk = np.arange(SEQ)[None, :]
    band = []
    for w in POOLW:
        m = ((sk <= tk) & (sk > tk - w)) / np.minimum(tk + 1, w).astype(f) - (sk == tk)
        band += [m[:P], m[P:, P:]]
    two["band"] = np.concatenate(band, 1)
    decay = []
    for h in range(4):
        lg = math.log(1.0 - 2.0 ** (-5.0 - h))
        m = np.where(sk <= tk, np.exp(lg * np.maximum(tk - sk, 0)), 0.0) * HD ** -0.5
        decay += [m[:P], m[P:, P:]]
    two["decay"] = np.concatenate(decay, 1)
    two["inv2"] = np.broadcast_to((f(10000.0) ** (-np.arange(32, dtype=f) / f(32))).astype(f)[None], (P, 32))
    fix = lambda d: {k: np.ascontiguousarray(v, dtype=f) for k, v in d.items()}
    return fix(one), fix(two)


def const_table(d):
    out, at = {}, 0
    for k, v in d.items():
        out[k] = (at, v.shape[1])
        at += v.shape[1]
    return out, at


COLS1 = [("g_mix", 8), ("g_ffn", 8), ("g_ple", 8), ("router", 64), ("rb", 8)]
SMALL1 = [("kc_w2", 64), ("vc_w2", 64), ("pos", 16), ("lora", 512), ("g_up", 256), ("wst", 512), ("bs", 4)]
ROWS1 = [("mu", 1024), ("wa0", 512), ("k_k", 256), ("k_a", 256), ("r_k", 256), ("gn_g", 256), ("gn_b", 256)]
ROWS1B = [("ln_g", 256), ("ln_b", 256)]
SMALL2 = [("g_mix", 8), ("g_ffn", 8), ("pool_w", 128), ("conv_w", 62), ("conv_b", 2), ("ada_b", 48)]
ROWS2 = [("pool_scale", 256), ("gn_g", 256), ("ln_g", 256), ("ln_b", 256), ("fb", 4)]


def spans(fields, at=0):
    out = {}
    for name, width in fields:
        out[name] = (at, width)
        at += width
    return out, at


class Mark:

    def __init__(self, sem, value, loop=None, step=0):
        self.sem, self.value, self.loop, self.step = sem, value, loop, step

    def last(self):
        return Mark(self.sem, self.value + (self.loop.turns - 1) * self.step)


class Loop:
    def __init__(self, turn, turns):
        self.turn, self.turns = turn, turns


class Engine:

    def __init__(self, nc, q, name, chained):
        self.nc, self.q, self.chained = nc, q, chained
        self.sem = nc.alloc_semaphore("s_" + name)
        self.n, self.loop, self.step, self.met = 0, None, 0, {}

    def wait(self, *marks):
        for m in marks:
            if m is None:
                continue
            if isinstance(m, (list, tuple)):
                self.wait(*m)
                continue
            if m.loop is not None and m.loop is self.loop:
                self.q.wait_ge(m.sem, self.loop.turn * m.step + m.value)
                continue
            assert m.loop is None
            key = m.sem.name
            if self.met.get(key, -1) >= m.value:
                continue
            if self.loop is None:
                self.met[key] = m.value
            self.q.wait_ge(m.sem, m.value)

    def mark(self, ins):
        ins.then_inc(self.sem, 1)
        self.n += 1
        return Mark(self.sem, self.n, self.loop, self.step)

    def now(self):
        return Mark(self.sem, self.n, self.loop, self.step)

    def __call__(self, op, *args, after=(), **kw):
        self.wait(*after)
        if self.chained and self.n:
            self.wait(self.now())
        return self.mark(op(*args, **kw))

    def enter(self, loop, step):
        self.loop, self.step, self.first, self.met = loop, step, self.n, {}

    def at(self, offset):
        return Mark(self.sem, self.first + offset, self.loop, self.step)

    def branch(self, name):
        self.common = (self.sem, self.n)
        self.sem, self.n, self.met = self.nc.alloc_semaphore(f"s_{name}_{self.sem.name[2:]}"), 0, {}

    def rejoin(self):
        (self.sem, self.n), self.met = self.common, {}

    def leave(self):
        assert self.n == self.first + self.step, (self.n, self.first, self.step)
        self.n = self.first + self.step * self.loop.turns
        self.loop, self.met = None, {}


class Banks:

    def __init__(self, ps, pe):
        self.ps, self.pe, self.order, self.free = ps, pe, list(range(8)), [[] for _ in range(8)]

    def take(self):
        b = self.order.pop(0)
        self.pe.wait(*self.free[b])
        return b

    def give(self, b, *marks):
        self.free[b] = list(marks)
        self.order.append(b)

    def __getitem__(self, b):
        return self.ps[:, b, :]


class Ring:

    def __init__(self, nc, sp, mem):
        self.nc, self.sp, self.mem = nc, sp, mem
        self.sems = [nc.alloc_semaphore(f"s_slot{i}") for i in range(NSLOT)]
        self.count = [0] * NSLOT
        self.free = [[] for _ in range(NSLOT)]
        self.plan, self.held, self.order = [], {}, list(range(NWALK))

    def schedule(self, tiles):
        self.plan += tiles
        self.pump()

    def pump(self):
        while self.plan and self.order:
            name, parts = self.plan.pop(0)
            s = self.order.pop(0)
            self.sp.wait(*self.free[s])
            for src, at in parts:
                n = src.shape[-1]
                self.sp.q.dma_start(self.mem[:, s, at:at + n], src).then_inc(self.sems[s], 16)
                self.count[s] += 16
            self.held[name] = (s, Mark(self.sems[s], self.count[s]))

    def get(self, name):
        s, m = self.held[name]
        return self.mem[:, s, :], m

    def release(self, name, *marks):
        s, _ = self.held.pop(name)
        self.free[s] = list(marks)
        self.order.append(s)
        self.pump()


class Carve:

    def __init__(self, mem, at=0):
        self.mem, self.at, self.size = mem, at, mem.shape[1]

    def __call__(self, *dims):
        n = 1
        for d in dims:
            n *= d
        ap = self.mem[:, self.at:self.at + n]
        self.at += n
        assert self.at <= self.size, (self.at, self.size)
        if len(dims) == 2:
            ap = ap.rearrange("p (a b) -> p a b", a=dims[0])
        elif len(dims) == 3:
            ap = ap.rearrange("p (a b c) -> p a b c", a=dims[0], b=dims[1])
        elif len(dims) == 4:
            ap = ap.rearrange("p (a b c d) -> p a b c d", a=dims[0], b=dims[1], c=dims[2])
        return ap


def alternate(*parts):
    parts = list(parts)
    while parts:
        parts = [p for p in parts if next(p, "end") != "end"]


def spread(ap, axis, n):
    ap = ap.unsqueeze(axis)
    shape = list(ap.shape)
    shape[axis] = n
    return ap.to_broadcast(shape)


def build(nc, d):
    V, S, T, G = nc.vector, nc.scalar, nc.tensor, nc.gpsimd
    dve = Engine(nc, V, "dve", True)
    act = Engine(nc, S, "act", True)
    pool = Engine(nc, G, "pool", True)
    pe = Engine(nc, T, "pe", False)
    sp = Engine(nc, nc.sync, "sp", False)

    def sb(name, n, dt=F32):
        return nc.alloc_sbuf_tensor(name, [P, n], dt)[:, :]

    one, two = const_arrays()
    tab1, width1 = const_table(one)
    tab2, width2 = const_table(two)
    h = sb("residual", NT * D).rearrange("p (i n) -> p i n", i=NT)
    xn = sb("natural", NT * D).rearrange("p (i n) -> p i n", i=NT)
    xt = sb("transposed", KD * SEQ).rearrange("p (k t) -> p k t", k=KD)
    zbuf = sb("z", NT * DIN1)
    cst = sb("constants", max(width1, width2))
    stat = sb("stat", 64 + 4 * 48)
    ang = sb("rope", 4 * NT * 32)
    gates2 = sb("gates2", 2 * D).rearrange("p (g n) -> p g n", g=2)
    zero = sb("zero", 512)
    ringm = nc.alloc_sbuf_tensor("ring", [P, NSLOT, SLOT], F32)[:, :, :]
    work = ringm.rearrange("p s n -> p (s n)")[:, NWALK * SLOT:]
    ps = nc.alloc_psum_tensor("ps", [P, 8, 512], F32)[:, :, :]
    bank = Banks(ps, pe)
    ring = Ring(nc, sp, ringm)
    s_misc = nc.alloc_semaphore("s_misc")
    misc = [0]

    def fetch(dst, src, after=()):
        pool.wait(*after)
        if misc[0]:
            pool.wait(Mark(s_misc, misc[0]))
        G.dma_start(dst, src).then_inc(s_misc, 16)
        misc[0] += 16
        return Mark(s_misc, misc[0])

    def join():
        return [dve.now(), act.now(), pe.now(), pool.now()]

    const = [tab1]

    def C(name):
        at, n = const[0][name]
        return cst[:, at:at + n]

    def transpose(b, col, src):
        return T.transpose(ps[:, b, col:col + P], src, C("ident"))

    def rsqrt(ap, after=()):
        m = act(S.activation, ap, ap, ACT.Sqrt, after=after)
        return dve(V.reciprocal, ap, ap, after=[m])

    def rms_rows(after, out):
        for i in range(NT):
            m = dve(V.tensor_tensor_reduce, out=out[:, i, :], in0=h[:, i, :], in1=h[:, i, :], scale=1.0 / D,
                    scalar=1e-6, op0=ALU.mult, op1=ALU.add, accum_out=stat[:, i:i + 1], after=after)
        rsqrt(stat[:, 0:NT], after=[m])
        for i in range(NT):
            m = dve(V.tensor_scalar, out[:, i, :], h[:, i, :], stat[:, i:i + 1], None, ALU.mult)
        return m

    def turn_xn(after, mult=None, add=None, after_w=()):
        for i in range(NT):
            for q in range(2):
                pe.wait(*after)
                b = bank.take()
                for k in range(4):
                    t = transpose(b, k * P, xn[:, i, (4 * q + k) * P:(4 * q + k + 1) * P])
                t = pe.mark(t)
                out = xt[:, 4 * q:4 * q + 4, i * P:(i + 1) * P]
                src = bank[b].rearrange("p (k t) -> p k t", k=4)
                if mult is None:
                    m = act(S.copy, out, src, after=[t])
                    bank.give(b, m)
                else:
                    m = dve(V.tensor_tensor, out, src, spread(mult[:, 4 * q:4 * q + 4], 2, P), ALU.mult,
                            after=[t] + list(after_w))
                    bank.give(b, m)
                    if add is not None:
                        m = dve(V.tensor_tensor, out, out, spread(add[:, 4 * q:4 * q + 4], 2, P), ALU.add)
        return m

    def project(z, width, tag, tiles, marks):
        for c in tiles:
            n = min(COLS, width - c * COLS)
            w, loaded = ring.get(f"{tag}{c}")
            w = w[:, 0:KD * n].rearrange("p (k n) -> p k n", k=KD)
            pe.wait(loaded)
            for i in range(NT):
                b = bank.take()
                for k in range(KD):
                    t = T.matmul(ps[:, b, 0:n], xt[:, k, i * P:(i + 1) * P], w[:, k, :],
                                 start=(k == 0), stop=(k == KD - 1))
                t = pe.mark(t)
                m = act(S.copy, z[:, i, c * COLS:c * COLS + n], ps[:, b, 0:n], after=[t])
                bank.give(b, m)
                if i == NT - 1:
                    ring.release(f"{tag}{c}", t)
                    marks[c] = m
                yield

    def out_project(tag, ready, add):
        pe.wait(ready)
        bs = [bank.take() for _ in range(4)]
        for c in range(3):
            ks = range(3 * c, min(3 * c + 3, KD))
            w, loaded = ring.get(f"{tag}{c}")
            pe.wait(loaded)
            for i in range(NT):
                for q in range(2):
                    for k in ks:
                        t = T.matmul(ps[:, bs[2 * i + q], :], xt[:, k, i * P:(i + 1) * P],
                                     w[:, (k - 3 * c) * D + q * 512:(k - 3 * c) * D + (q + 1) * 512],
                                     start=(k == 0), stop=(k == KD - 1))
            t = pe.mark(t)
            ring.release(f"{tag}{c}", t)
        for i in range(NT):
            for q in range(2):
                m = add(i, q, bank[bs[2 * i + q]], t)
                bank.give(bs[2 * i + q], m)
        return m

    def head_norm(x, n, width, eps, tmp, st, after=()):
        s1, s2 = st[:, 0:n], st[:, 8:8 + n]
        dve(V.tensor_reduce, s1, x, AXX, ALU.add, after=after)
        dve(V.tensor_scalar, s1, s1, 1.0 / width, None, ALU.mult)
        dve(V.tensor_tensor, x, x, spread(s1, 2, width), ALU.subtract)
        dve(V.tensor_tensor, tmp, x, x, ALU.mult)
        dve(V.tensor_reduce, s2, tmp, AXX, ALU.add)
        m = dve(V.tensor_scalar, s2, s2, 1.0 / width, eps, ALU.mult, ALU.add)
        rsqrt(s2, after=[m])
        return dve(V.tensor_tensor, x, x, spread(s2, 2, width), ALU.mult)

    def rope_tables(pos, inv, n, w, after):
        cos = ang[:, 0:NT * n].rearrange("p (i n) -> p i n", i=NT)
        sin = ang[:, 64:64 + NT * n].rearrange("p (i n) -> p i n", i=NT)
        posf, a, k = w(NT), w(NT, n), w(NT, n)
        dve(V.tensor_copy, posf, pos, after=after)
        dve(V.tensor_tensor, a, spread(posf, 2, n), spread(inv, 1, NT), ALU.mult)
        magic = 1.5 * 2 ** 23
        dve(V.tensor_scalar, k, a, 1.0 / (2 * math.pi), magic, ALU.mult, ALU.add)
        dve(V.tensor_scalar, k, k, magic, None, ALU.subtract)
        c1 = 6.28125
        c2 = float(np.float32(round((2 * math.pi - c1) * 2 ** 19) / 2 ** 19))
        c3 = 2 * math.pi - c1 - c2
        for c in (c1, c2, c3):
            dve(V.scalar_tensor_tensor, out=a, in0=k, scalar=-c, in1=a, op0=ALU.mult, op1=ALU.add)
        m = dve(V.tensor_scalar, a, a, 3.1415925, -3.1415925, ALU.min, ALU.max)
        act(S.activation, sin, a, ACT.Sin, after=[m])
        m = act(S.activation, k, a, ACT.Abs)
        m = dve(V.tensor_scalar, k, k, -1.0, math.pi / 2, ALU.mult, ALU.add, after=[m])
        return cos, sin, act(S.activation, cos, k, ACT.Sin, after=[m])

    def rotate(out, x, heads, half, cos, sin, tmp, after=()):
        c, s = spread(cos, 2, heads), spread(sin, 2, heads)
        x1, x2 = x[:, :, :, 0:half], x[:, :, :, half:2 * half]
        n = NT * heads * half
        ta, tb, tc, td = (tmp[:, e * n:(e + 1) * n].rearrange("p (i h n) -> p i h n", i=NT, h=heads) for e in range(4))
        dve(V.tensor_tensor, ta, x1, c, ALU.mult, after=after)
        dve(V.tensor_tensor, tb, x2, s, ALU.mult)
        dve(V.tensor_tensor, tc, x1, s, ALU.mult)
        dve(V.tensor_tensor, td, x2, c, ALU.mult)
        dve(V.tensor_tensor, out[:, :, :, 0:half], ta, tb, ALU.subtract)
        return dve(V.tensor_tensor, out[:, :, :, half:2 * half], tc, td, ALU.add)

    def softmax_rows(sc, heads, st, after=()):
        mx, sm = st[:, 0:heads], st[:, 16:16 + heads]
        n = sc.shape[2]
        dve(V.tensor_reduce, mx, sc, AXX, ALU.max, after=after)
        m = dve(V.tensor_tensor, sc, sc, spread(mx, 2, n), ALU.subtract)
        m = act(S.activation, sc, sc, ACT.Exp, after=[m])
        dve(V.tensor_reduce, sm, sc, AXX, ALU.add, after=[m])
        m = dve(V.reciprocal, sm, sm)
        return sm, m

    def weighted_values(pr, heads, ns, pt, value, ready):
        flat = [(m, st) for m in range(heads) for st in range(ns)]
        for g in range(0, len(flat), 4):
            pe.wait(ready)
            b = bank.take()
            for e, (m, st) in enumerate(flat[g:g + 4]):
                t = transpose(b, e * P, pr[:, m, st * P:(st + 1) * P])
            t = pe.mark(t)
            k = act(S.copy, pt[:, g:g + 4, :], bank[b].rearrange("p (a t) -> p a t", a=4), after=[t])
            bank.give(b, k)
            yield
        pe.wait(k)
        b = bank.take()
        for e, (m, st) in enumerate(flat):
            t = T.matmul(ps[:, b, m * HD:(m + 1) * HD], pt[:, e, :], value(m, st), start=(st == 0), stop=(st == ns - 1))
        return b, pe.mark(t)

    def stream_blocks(tiles, first_tile, blocks, work_free):
        free0 = [list(f) for f in ring.free]
        loop_base, base = freed[0], list(ring.count)
        for j in range(NSLOT):
            ring.count[j] += 16 * (blocks // NSLOT)
        sp.met = {}
        with nc.Fori(0, blocks // NSLOT, engines=LOADER) as turn:
            loop = Loop(turn, blocks // NSLOT)
            sp.enter(loop, 0)
            for j in range(NSLOT):
                sp.wait(*(free0[j] if j < NWALK else work_free))
                sp.wait(Mark(s_freed, loop_base + j + 1 - NSLOT, loop, NSLOT))
                sp.q.dma_start(ringm[:, j, :], tiles[first_tile + turn * NSLOT + j]).then_inc(ring.sems[j], 16)
            sp.leave()
        return loop_base, base

    def blocks_done(n):
        freed[0] += n
        for j in range(NSLOT):
            ring.free[j] = [Mark(s_freed, freed[0] - (NSLOT - 1 - j))]
        ring.order = list(range(NWALK))

    def ffn_block(loop, j, per_turn, bases, tokens, src, silu, hid, nv, gate, banks_up, acc, accumulate, dve_before):
        freed0, base = bases
        slot = j % NSLOT
        w = ringm[:, slot, :]

        def up():
            loads = 16 * (per_turn // NSLOT)
            pe.wait(Mark(ring.sems[slot], base[slot] + 16 * (j // NSLOT + 1), loop, loads))
            pe.wait(dve_before)
            for half_w in range(2):
                for k in range(KD):
                    at = half_w * D + k * P
                    t = T.matmul(banks_up[half_w], w[:, at:at + P], src[:, k, :], start=(k == 0), stop=(k == KD - 1))
            return pe.mark(t)

        def gated(t):
            act.wait(dve_before)
            m = act(S.activation, silu[:, j % 2, :], banks_up[0], ACT.Silu, after=[t])
            if gate is not None:
                m = dve(V.tensor_tensor, silu[:, j % 2, :], silu[:, j % 2, :], gate, ALU.mult, after=[m])
            dve.wait(Mark(s_freed, freed0 + j - 1, loop, per_turn))
            return dve(V.tensor_tensor, hid[:, j % 2, :], silu[:, j % 2, :], banks_up[1], ALU.mult, after=[m, t])

        def down(m):
            pe.wait(m)
            for i in range(tokens // P):
                for q in range(2):
                    t = T.matmul(acc[2 * i + q], hid[:, j % 2, i * P:(i + 1) * P], w[:, 2 * D + q * 512:2 * D + (q + 1) * 512],
                                 start=accumulate == "first", stop=accumulate == "last")
            t.then_inc(s_freed, 1)
            return Mark(s_freed, freed0 + j + 1, loop, per_turn)

        return up, gated, down

    def dense_loop(experts, bases, gate, ready, add):
        fw = Carve(zbuf, NE * SEQ)
        silu, hid = fw(2, SEQ), fw(2, SEQ)
        pe.wait(ready)
        for b in range(4, 8):
            t = T.matmul(ps[:, b, :], zero[:, 0:P], zero[:, :], start=True, stop=False)
        pe.mark(t)
        half = FB // NSLOT
        nv = 2 if gate is not None else 1
        with nc.Fori(0, experts, engines=WORKERS) as e, nc.Fori(0, half, engines=WORKERS) as c:
            loop = Loop(e * half + c, experts * half)
            pe.enter(loop, NSLOT)
            act.enter(loop, NSLOT)
            dve.enter(loop, nv * NSLOT)
            steps = [ffn_block(loop, j, NSLOT, bases, SEQ, xt, silu, hid, nv, gate[:, e, :] if gate is not None else None,
                               (ps[:, j % 2, 0:SEQ], ps[:, 2 + j % 2, 0:SEQ]), [bank[b] for b in range(4, 8)], "middle",
                               dve.at(nv * (j - 1))) for j in range(NSLOT)]
            m = steps[0][1](steps[0][0]())
            for j in range(NSLOT):
                nxt = steps[j + 1][1](steps[j + 1][0]()) if j + 1 < NSLOT else None
                steps[j][2](m)
                m = nxt
            for q in (pe, act, dve):
                q.leave()
        for b in range(4, 8):
            t = T.matmul(ps[:, b, :], zero[:, 0:P], zero[:, :], start=False, stop=True)
        t = pe.mark(t)
        for i in range(NT):
            for q in range(2):
                m = add(i, q, bank[4 + 2 * i + q], t)
        return m

    def all_banks():
        for b in range(8):
            pe.wait(*bank.free[b])

    def feed_forward(tiles, first_tile, ready, add):
        assert not ring.plan and not ring.held
        bases = stream_blocks(tiles, first_tile, FB, work_done[0])
        all_banks()
        m = dense_loop(1, bases, None, ready, add)
        blocks_done(FB)
        for b in range(8):
            bank.free[b] = [m, act.now()]
        bank.order = list(range(8))
        return m

    def routed_feed_forward(kept, ready):
        assert not ring.plan and not ring.held
        bases = stream_blocks(d["moe"], 0, NE * FB, work_done[0])
        ex, posx, gatx, count, m = route(kept, ready)
        all_banks()
        for e in (pe, act, dve):
            e.wait(m)
        start = dve.n
        most = nc.values_load(count[0:1, 0:1], engines=WORKERS, min_val=0, max_val=SEQ)
        with nc.If(most <= P):
            for e in (pe, act, dve):
                e.branch("gathered")
            m = gathered_loop(bases, kept, posx, gatx)
            for e in (pe, act, dve):
                e.rejoin()
            m = dve(V.memset, stat[:, 8:9], 0.0, after=[m])
        dve.n = start
        with nc.Else():
            for e in (pe, act, dve):
                e.branch("everywhere")
            gate_all, m = spread_gates(ex)
            m = dense_loop(NE, bases, gate_all, m, add_residual)
            for e in (pe, act, dve):
                e.rejoin()
            m = dve(V.memset, stat[:, 8:9], 0.0, after=[m])
        blocks_done(NE * FB)
        for b in range(8):
            bank.free[b] = [m]
        bank.order = list(range(8))
        for e in (pe, act, sp, pool):
            e.wait(m)

    def gathered_loop(bases, kept, posx, gatx):
        fw = Carve(zbuf)
        xg, ysb = fw(KD, P), fw(D)
        pick, pickg, gT, silu, hid = fw(NT, P), fw(NT, P), fw(NT, P), fw(2, P), fw(2, P)
        slots = C("slots")

        def select(e, out, weighted):
            for i in range(NT):
                if weighted:
                    m = dve(V.tensor_scalar, out[:, i, :], slots, posx[:, e, i:i + 1], gatx[:, e, i:i + 1],
                            ALU.is_equal, ALU.mult)
                else:
                    m = dve(V.tensor_scalar, out[:, i, :], slots, posx[:, e, i:i + 1], None, ALU.is_equal)
            return m

        def gather(m, free):
            pe.wait(m, free)
            for k in range(KD):
                for i in range(NT):
                    t = T.matmul(ps[:, 4 + k // 4, (k % 4) * P:(k % 4 + 1) * P], xn[:, i, k * P:(k + 1) * P],
                                 pick[:, i, :], start=(i == 0), stop=(i == NT - 1))
            t = pe.mark(t)
            for q in range(2):
                m = dve(V.tensor_tensor, xg[:, 4 * q:4 * q + 4, :], bank[4 + q].rearrange("p (k t) -> p k t", k=4),
                        spread(kept("g_ffn")[:, 4 * q:4 * q + 4], 2, P), ALU.mult, after=[t])
            return m

        def scatter(marks):
            pe.wait(*marks)
            for n, b in enumerate((0, 1, 6, 7)):
                t = T.matmul(bank[b], gT[:, n // 2, :], ysb[:, (n % 2) * 512:(n % 2 + 1) * 512], start=True, stop=True)
            t = pe.mark(t)
            for n, b in enumerate((0, 1, 6, 7)):
                m = add_residual(n // 2, n % 2, bank[b], t)
            return m

        m = select(0, pick, False)
        gather(m, None)
        with nc.Fori(0, NE, engines=WORKERS) as e:
            loop = Loop(e, NE)
            pe.enter(loop, FB + 3)
            act.enter(loop, FB + 3)
            dve.enter(loop, FB + 10)
            steps = []
            m = select(e, pickg, True)
            weighted = m

            def step(j, before):
                return ffn_block(loop, j, FB, bases, P, xg, silu, hid, 1, None,
                                 (ps[:, j % 2, 0:P], ps[:, j % 2, P:2 * P]), [bank[2], bank[3]],
                                 "first" if j == 0 else "last" if j == FB - 1 else "middle", before)

            prev = [dve.at(0), dve.at(0)]
            cur = step(0, prev[0])
            m = cur[1](cur[0]())
            done = [m]
            turned = None
            for j in range(FB):
                if j + 1 < FB:
                    nxt = step(j + 1, dve.at(0) if j == 0 else done[j - 1])
                    m2 = nxt[1](nxt[0]())
                    done.append(m2)
                if j == 0:
                    pe.wait(act.at(0))
                last = cur[2](m)
                if j == 1:
                    pe.wait(weighted)
                    for i in range(NT):
                        t = transpose(6, i * P, pickg[:, i, :])
                    t = pe.mark(t)
                    turned = act(S.copy, gT, ps[:, 6, 0:2 * P].rearrange("p (i t) -> p i t", i=NT), after=[t])
                if j == 2:
                    picked = select(e + 1, pick, False)
                if j + 1 < FB:
                    cur, m = nxt, m2
            for q in range(2):
                y = act(S.copy, ysb[:, q * 512:(q + 1) * 512], bank[2 + q], after=[last])
            gather(picked, None)
            scatter([y, turned, done[-1]])
            for q in (pe, act, dve):
                q.leave()
        return dve.now()

    def add_residual(i, q, src, t):
        return dve(V.tensor_tensor, h[:, i, q * 512:(q + 1) * 512], h[:, i, q * 512:(q + 1) * 512], src, ALU.add,
                   after=[t])

    s_x = nc.alloc_semaphore("s_x")
    nc.sync.dma_start(h, d["x"]).then_inc(s_x, 16)
    loaded_x = Mark(s_x, 16)
    cols = sb("layer_cols", 2 * 96).rearrange("p (l n) -> p l n", l=2)
    mods = sb("modulation", 2 * 48 + 16 + KD).rearrange("p n -> p n")
    loaded_cols = fetch(cols, d["cols"])
    loaded_const = fetch(cst[:, 0:width1], d["const1"])
    posi = nc.alloc_sbuf_tensor("posi", [P, 2 * NT], I32)[:, :]
    most_i = nc.alloc_sbuf_tensor("most_tokens", [P, 1], I32)[:, :]
    route_mem = sb("routing", 3 * NT * NE + 2 * NT * (NE + 1))
    s_freed = nc.alloc_semaphore("s_freed")
    nc.sync.sem_inc(s_freed, NSLOT)
    freed = [NSLOT]
    work_done = [[]]
    loaded_pos = fetch(posi, d["pos"])
    loaded_c = fetch(mods[:, 112:112 + KD], d["c"])
    dve(V.memset, zero, 0.0)
    pe.wait(dve.now(), loaded_const)
    dve.wait(loaded_x, loaded_cols)
    cact = mods[:, 112:112 + KD]

    small1, n_small1 = spans(SMALL1)
    rows1b, _ = spans(ROWS1B, n_small1)
    rows1, _ = spans(ROWS1)
    small1.update(rows1b)

    def columns(buf, table):
        def get(name):
            at, n = table[name]
            return buf[:, at:at + n]
        return get

    def layer_tiles(l):
        out = []
        for c in range(-(-DIN1 // COLS)):
            n = min(COLS, DIN1 - c * COLS)
            out.append((f"win{c}", [(d["w_in"][l, c, :, 0:KD * n], 0)]))
        small = [("rows", [(d["rows1"][l:l + 1].to_broadcast([P, d["rows1"].shape[1]]), 0)]),
                 ("small", [(d["small1"][l], 0), (d["rows1b"][l:l + 1].to_broadcast([P, d["rows1b"].shape[1]]), n_small1)])]
        out[2:2] = small
        out += [("kc", [(d["kc_w1"][l], 0)]), ("vc", [(d["vc_w1"][l], 0)])]
        out += [(f"ada{c}", [(d["ada"][l, c], 0)]) for c in range(16)]
        out += [(f"wout{c}", [(d["w_out"][l, c], 0)]) for c in range(3)]
        return out

    def ple_tiles(l):
        return [("ple_up", [(d["ple_proj"][l], 0)])] + \
            [(f"pleg{c}", [(d["ple_gate"][l, c, :, 0:KD * min(COLS, D - c * COLS)], 0)]) for c in range(3)]

    def spatial_gating(z, small, tiles, ready):
        while 3 not in tiles:
            yield
        ready = ready + [tiles[3]]
        w, st = Carve(gates_flat), stats(0)
        u, v, tmp, wst = w(NT, 256), w(NT, 256), w(8, 64), w(4, P)
        act(S.activation, u, z[:, :, ZA:ZA + 256], ACT.Gelu_apprx_tanh, after=ready)
        m = act(S.activation, v, z[:, :, ZA + 256:ZA + 512], ACT.Gelu_apprx_tanh)
        dve(V.tensor_tensor, wst, small("wst").rearrange("p (h t) -> p h t", h=4), spread(C("tri"), 1, 4), ALU.mult,
            after=ready)
        yield
        head_norm(v.rearrange("p i (h d) -> p (i h) d", h=4), 8, HD, 1e-5, tmp, st, after=[m])
        dve(V.tensor_tensor, v, v, spread(small("ln_g"), 1, NT), ALU.mult)
        m = dve(V.tensor_tensor, v, v, spread(small("ln_b"), 1, NT), ALU.add)
        yield
        pe.wait(m)
        b = bank.take()
        for i in range(NT):
            for hh in range(4):
                t = T.matmul(ps[:, b, (4 * i + hh) * HD:(4 * i + hh + 1) * HD], wst[:, hh, :],
                             v[:, i, hh * HD:(hh + 1) * HD], start=True, stop=True)
        t = pe.mark(t)
        bs = small("bs")
        mixed = v
        for i in range(NT):
            m = dve(V.tensor_tensor, mixed[:, i, :].rearrange("p (h d) -> p h d", h=4),
                    bank[b][:, i * 256:(i + 1) * 256].rearrange("p (h d) -> p h d", h=4), spread(bs, 2, HD), ALU.add,
                    after=[t])
        bank.give(b, m)
        marks["gating"] = dve(V.tensor_tensor, xn[:, :, 0:256], u, mixed, ALU.mult)

    def sparse_attention(z, small, tiles, ready, w):
        Z = 1536
        while 7 not in tiles:
            yield
        ready = ready + [tiles[c] for c in (4, 5, 6, 7)]
        st = stats(1)
        q = z[:, :, Z:Z + 512]
        tmp = w(512)
        qT, qrT, kT = w(NT, 4, P), w(NT, 4, P), w(2, SEQ)
        gt = w(NT, 24)
        mark1 = w.at
        oacc = xn[:, :, 512:1024]
        act(S.activation, gt, z[:, :, Z + 1280:Z + 1304], ACT.Sigmoid, after=ready)
        heads = lambda ap, n: ap.rearrange("p i (h d) -> p i h d", h=n)

        def turn_queries(dst, dep):
            pe.wait(*dep)
            for i in range(NT):
                b = bank.take()
                for j in range(4):
                    t = transpose(b, j * P, q[:, i, j * P:(j + 1) * P])
                t = pe.mark(t)
                m = act(S.mul, dst[:, i], bank[b].rearrange("p (j t) -> p j t", j=4), HD ** -0.5, after=[t])
                bank.give(b, m)
            return t, m

        raw, _ = turn_queries(qT, ready)
        yield
        for at in (Z + 768, Z + 1024):
            k2_ = heads(z[:, :, at:at + P], 2)
            r = rotate(k2_, k2_, 2, 8, cos, sin, tmp, after=ready + [rope_ready])
            yield
        pe.wait(r)
        b = bank.take()
        for ty in range(2):
            for i in range(NT):
                t = transpose(b, (2 * ty + i) * P, z[:, i, Z + 768 + 256 * ty:Z + 896 + 256 * ty])
        t = pe.mark(t)
        m = act(S.copy, kT, bank[b].rearrange("p (a t) -> p a t", a=2), after=[t])
        bank.give(b, m)
        r = rotate(heads(q, 8), heads(q, 8), 8, 8, cos, sin, tmp, after=[raw])
        yield
        _, turned = turn_queries(qrT, [r])
        yield

        dup, x2 = w(NT, 4, 2, HD), w(4, SEQ)
        blk = w(4, 16, 15)
        hidden, hrep, kcT, vbd = w(2, 30), w(4, 32), w(16), w(4, HD)
        for i in range(NT):
            m = dve(V.tensor_copy, dup[:, i], spread(z[:, i, Z + 512:Z + 768].rearrange("p (a d) -> p a d", a=4), 2, 2))
        dve(V.memset, hrep, 0.0)
        dve(V.memset, vbd, 0.0)
        for i in range(NT):
            pe.wait(m)
            b = bank.take()
            for a in range(4):
                t = transpose(b, a * P, dup[:, i, a].rearrange("p b d -> p (b d)"))
            t = pe.mark(t)
            src = bank[b].rearrange("p (a t) -> p a t", a=4)
            act(S.copy, x2[0:64, :, i * P:(i + 1) * P], src[0:64], after=[t])
            lo = 1 if i == 0 else 0
            k = act(S.copy, x2[64:128, :, i * P + lo - 1:(i + 1) * P - 1], src[64:128, :, lo:P])
            bank.give(b, k)
            yield
        dve.wait(k)
        for a in range(4):
            for hh in range(2):
                m = dve(V.tensor_tensor, blk[:, a, 8 * hh:8 * hh + 8, :],
                        x2[:, a, 16 * hh:16 * hh + 240].rearrange("p (n l b) -> p b l n", l=8, b=2)[:, 0],
                        spread(small("pos")[:, 8 * hh:8 * hh + 8], 2, 15), ALU.add)
        while "kc" not in ring.held or "vc" not in ring.held:
            yield
        pe.wait(m)
        b = bank.take()
        for kv, tag in ((0, "kc"), (1, "vc")):
            w1, loaded = ring.get(tag)
            pe.wait(loaded)
            for l in range(16):
                t = T.matmul(ps[:, b, 32 * kv:32 * kv + 30], w1[:, l * P:(l + 1) * P], blk[:, 2 * kv:2 * kv + 2, l, :],
                             start=(l == 0), stop=(l == 15))
            t = pe.mark(t)
            ring.release(tag, t)
        m = act(S.activation, hidden, ps[:, b, 0:64].rearrange("p (v n) -> p v n", v=2)[:, :, 0:30], ACT.Gelu_apprx_tanh,
                after=[t])
        bank.give(b, m)
        yield
        m2 = dve(V.tensor_copy, hrep.rearrange("p (a g) n -> p a g n", g=2)[:, :, :, 0:15],
                 spread(hidden[:, 1, :].rearrange("p (g n) -> p g n", g=2), 1, 2), after=[m])
        pe.wait(m, m2)
        b = bank.take()
        for g in range(2):
            T.matmul(ps[64 * g:64 * g + 64, b, 0:15], small("kc_w2"), hidden[:, 0, 15 * g:15 * g + 15], start=True, stop=True)
        t = pe.mark(T.matmul(ps[:, b, 64:128], hrep.rearrange("p a n -> p (a n)"), small("vc_w2"), start=True, stop=True))
        act(S.copy, kcT[:, 0:15], ps[:, b, 0:15], after=[t])
        for a in range(4):
            k = act(S.copy, vbd[32 * a:32 * a + 32, a, :], ps[32 * a:32 * a + 32, b, 64:128])
        bank.give(b, k)
        yield
        sc, pct = w(NT * 8, 32), w(4, P)
        m = dve(V.memset, sc, 0.0)
        scv = sc.rearrange("p (i m) n -> p i m n", i=NT)
        neg = C("cmpneg").rearrange("p (i n) -> p i n", i=NT)
        pe.wait(k, turned)
        for i in range(NT):
            for g in range(2):
                b = bank.take()
                for j in range(4):
                    t = T.matmul(ps[:, b, 16 * j:16 * j + 15], qT[64 * g:64 * g + 64, i, j, :],
                                 kcT[64 * g:64 * g + 64, 0:15], start=True, stop=True)
                t = pe.mark(t)
                m = dve(V.tensor_tensor, scv[:, i].rearrange("p (j g) n -> p j g n", g=2)[:, :, g, 0:15],
                        ps[:, b, 0:64].rearrange("p (j n) -> p j n", j=4)[:, :, 0:15], spread(neg[:, i], 1, 4), ALU.add,
                        after=[t])
                bank.give(b, m)
        yield
        rs, m = softmax_rows(sc[:, :, 0:15], NT * 8, st)
        dve(V.tensor_tensor, sc[:, :, 0:15], sc[:, :, 0:15], spread(rs, 2, 15), ALU.mult)
        for i in range(NT):
            m = dve(V.tensor_tensor, scv[:, i, :, 0:15], scv[:, i, :, 0:15],
                    spread(C("cmp01").rearrange("p (i n) -> p i n", i=NT)[:, i], 1, 8), ALU.mult)
        yield
        pe.wait(m)
        b = bank.take()
        for e in range(4):
            t = transpose(b, e * P, sc[:, 4 * e:4 * e + 4, :].rearrange("p m n -> p (m n)"))
        t = pe.mark(t)
        m = act(S.copy, pct, bank[b].rearrange("p (a t) -> p a t", a=4), after=[t])
        bank.give(b, m)
        yield
        pe.wait(m)
        for i in range(NT):
            b = bank.take()
            for c in range(2):
                t = T.matmul(ps[:, b, 256 * c:256 * c + 256], pct[:, 2 * i + c, :], vbd.rearrange("p a d -> p (a d)"),
                             start=True, stop=True)
            t = pe.mark(t)
            m = dve(V.tensor_tensor, oacc[:, i, :].rearrange("p (m d) -> p m d", m=8),
                    bank[b].rearrange("p (m d) -> p m d", m=8), spread(gt[:, i, 0:8], 2, HD), ALU.mult, after=[t])
            bank.give(b, m)
        compressed = [m, act.now(), pe.now()]
        yield

        w.at = mark1
        sbuf, pt = w(8 * 256), w(16, P)
        for ty in range(2):
            vat = Z + 896 + 256 * ty
            for i in range(NT):
                n = P * (i + 1)
                s8 = sbuf[:, 0:8 * n].rearrange("p (m s) -> p m s", m=8)
                s8g = s8.rearrange("p (j g) s -> p j g s", g=2)
                mask = C("causal")[:, P * i:P * i + n]
                dve.wait(*compressed)
                act.wait(*compressed)
                per = 512 // n
                for g in range(2):
                    for j0 in range(0, 4, per):
                        b = bank.take()
                        for j in range(j0, j0 + per):
                            t = T.matmul(ps[:, b, (j - j0) * n:(j - j0 + 1) * n], qrT[64 * g:64 * g + 64, i, j, :],
                                         kT[64 * g:64 * g + 64, ty, 0:n], start=True, stop=True)
                        t = pe.mark(t)
                        m = dve(V.tensor_tensor, s8g[:, j0:j0 + per, g, :],
                                bank[b].rearrange("p (j s) -> p j s", j=per), spread(mask, 1, per), ALU.add, after=[t])
                        bank.give(b, m)
                        yield
                rs, m = softmax_rows(s8, 8, st)
                yield
                b, t = yield from weighted_values(s8, 8, i + 1, pt[:, 0:8 * (i + 1), :],
                                       lambda mm, st: z[:, st, vat + (mm % 2) * HD:vat + (mm % 2 + 1) * HD], m)
                dve(V.tensor_tensor, rs, rs, gt[:, i, 8 * (ty + 1):8 * (ty + 2)], ALU.mult)
                o = tmp[:, 0:512].rearrange("p (m d) -> p m d", m=8)
                m = dve(V.tensor_tensor, o, bank[b].rearrange("p (m d) -> p m d", m=8), spread(rs, 2, HD), ALU.mult,
                        after=[t])
                bank.give(b, m)
                dst = oacc[:, i, :]
                m = dve(V.tensor_tensor, dst, oacc[:, i, :], tmp[:, 0:512], ALU.add)
                compressed = [m]
                yield
        marks["attention"] = m

    def time_mix(z, small, rows, tiles, ready, w):
        st = stats(2)
        zb = z[:, :, 0:1024]
        zm, gg, k2 = w(NT, 1024), w(NT, 256), w(NT, 256)
        keep = w(NT, 4, 256)
        pr, qT, hT = w(2, NT, 2, P), w(2, SEQ), w(2, SEQ)
        wc, st_e = w(2, 4), w(2, 2, HD)
        state = w(4, 2, HD)
        y = w(NT, 256)
        gT, st_f = qT, hT.rearrange("p a t -> p (a t)").rearrange("p (a c d) -> p a c d", a=2, c=4)
        pr_flat = pr.rearrange("p a i e t -> p (a i e t)")
        lo, loT = (pr_flat[:, 512 * e:512 * e + 512].rearrange("p (a t) -> p a t", a=2) for e in range(2))
        gnat, t2 = lo, loT
        shared = w.at
        tmp = w(NT, 256)
        wa, kk, lw, wi, wx, wn = w(NT, 512), w(NT, 256), w(NT, 256), w(NT, 256), w(NT, 256), w(NT, 256)
        for i in range(NT):
            for c in range(2):
                cols = slice(512 * c, 512 * c + 512)
                pe.wait(*ready)
                b = bank.take()
                t = T.matmul(bank[b], C("shift"), zb[:, i, cols], start=True, stop=(i == 0))
                if i:
                    t = T.matmul(bank[b], C("carry"), zb[:, i - 1, cols], start=False, stop=True)
                t = pe.mark(t)
                o = zm[:, i, cols]
                m = dve(V.tensor_tensor, o, bank[b], zb[:, i, cols], ALU.subtract, after=[t] + ready)
                bank.give(b, m)
                dve(V.tensor_tensor, o, o, rows("mu")[:, cols], ALU.mult)
                m = dve(V.tensor_tensor, o, o, zb[:, i, cols], ALU.add)
                yield
        r, k, v = zm[:, :, 0:256], zm[:, :, 256:512], zm[:, :, 512:768]
        act(S.activation, lo[:, :, 0:64], zm[:, :, 768:832], ACT.Tanh, after=[m])
        act(S.copy, lo[:, :, 64:128], zm[:, :, 832:896])
        m = act(S.activation, lo[:, :, 128:256], zm[:, :, 896:1024], ACT.Sigmoid)
        pe.wait(m)
        b = bank.take()
        for c in range(2):
            for i in range(NT):
                t = transpose(b, (2 * c + i) * P, lo[:, i, c * P:(c + 1) * P])
        t = pe.mark(t)
        m = act(S.copy, loT, bank[b].rearrange("p (c t) -> p c t", c=2), after=[t])
        bank.give(b, m)
        yield
        pe.wait(m)
        for i in range(NT):
            b = bank.take()
            t = pe.mark(T.matmul(bank[b], loT[:, 0, i * P:(i + 1) * P], small("lora"), start=True, stop=True))
            m = dve(V.tensor_tensor, wa[:, i, :], bank[b], rows("wa0"), ALU.add, after=[t])
            bank.give(b, m)
        b = bank.take()
        for i in range(NT):
            t = T.matmul(ps[:, b, 256 * i:256 * i + 256], loT[:, 1, i * P:(i + 1) * P], small("g_up"), start=True, stop=True)
        t = pe.mark(t)
        act(S.activation, wa, wa, ACT.Sigmoid, after=[m])
        m = act(S.copy, gg, bank[b].rearrange("p (i n) -> p i n", i=NT), after=[t])
        bank.give(b, m)
        yield
        a = wa[:, :, 256:512]
        lwr = dve(V.tensor_scalar, lw, wa[:, :, 0:256], -math.exp(-0.5), None, ALU.mult, after=[m])
        dve(V.tensor_tensor, kk, k, spread(rows("k_k"), 1, NT), ALU.mult)
        dve(V.tensor_tensor, tmp, kk, kk, ALU.mult)
        per_head = lambda ap: ap.rearrange("p i (h d) -> p (i h) d", h=4)
        ss = st[:, 16:24]
        dve(V.tensor_reduce, ss, per_head(tmp), AXX, ALU.add)
        m = dve(V.tensor_scalar, ss, ss, 1e-24, None, ALU.max)
        rsqrt(ss, after=[m])
        dve(V.tensor_tensor, per_head(kk), per_head(kk), spread(ss, 2, HD), ALU.mult)
        dve(V.tensor_scalar, tmp, a, -1.0, None, ALU.add)
        dve(V.tensor_tensor, tmp, tmp, spread(rows("k_a"), 1, NT), ALU.mult)
        dve(V.tensor_scalar, tmp, tmp, 1.0, None, ALU.add)
        dve(V.tensor_tensor, k2, k, tmp, ALU.mult)
        yield
        pe.wait(lwr)
        b = bank.take()
        for i in range(NT):
            t = T.matmul(ps[:, b, 256 * i:256 * i + 256], C("tri64"), lw[:, i, :], start=True, stop=True)
        t = pe.mark(t)
        cum = bank[b].rearrange("p (i n) -> p i n", i=NT)
        m = dve(V.tensor_tensor, wx, cum, lw, ALU.subtract, after=[t])
        act(S.activation, wi, cum, ACT.Exp, after=[m])
        k_ = act(S.activation, wn, cum, ACT.Exp, scale=-1.0)
        bank.give(b, m, k_)
        m = act(S.activation, wx, wx, ACT.Exp, after=[m])
        yield
        b = bank.take()
        for pair in range(2):
            for i in range(NT):
                t = T.matmul(ps[:, b, 4 * pair + 2 * i:4 * pair + 2 * i + 2], lw[:, i, pair * P:(pair + 1) * P], C("half"),
                             start=True, stop=True)
        t = pe.mark(t)
        k_ = act(S.activation, wc, ps[:, b, 0:8].rearrange("p (a c) -> p a c", a=2), ACT.Exp, after=[t])
        bank.give(b, k_)
        kp, kq, kh, kr = (keep[:, :, e, :] for e in range(4))
        dve(V.tensor_tensor, kp, wx, kk, ALU.mult, after=[m])
        dve(V.tensor_tensor, tmp, kk, a, ALU.mult)
        dve(V.tensor_tensor, kq, tmp, wn, ALU.mult)
        dve(V.tensor_tensor, kh, k2, wn, ALU.mult)
        m = dve(V.tensor_tensor, kr, r, wi, ALU.mult)
        ended = m
        yield
        pe.wait(m)
        for src, dst in ((kp, pr[:, :, :, 0, :]), (kr, pr[:, :, :, 1, :]), (kq, qT.rearrange("p a (i t) -> p a i t", i=NT)),
                         (kh, hT.rearrange("p a (i t) -> p a i t", i=NT))):
            b = bank.take()
            for pair in range(2):
                for i in range(NT):
                    t = transpose(b, (2 * pair + i) * P, src[:, i, pair * P:(pair + 1) * P])
            t = pe.mark(t)
            m = act(S.copy, dst, bank[b].rearrange("p (a i t) -> p a i t", a=2, i=NT), after=[t])
            bank.give(b, m)
            yield
        w.at = shared
        prod = w(8, 4, P)
        reused = [ended, pe.now(), act.now()]
        pe.wait(m)
        dve.wait(*reused)
        for i in range(NT):
            for hh in range(4):
                lo_p = 64 * (hh % 2)
                rhs = pr[lo_p:lo_p + 64, hh // 2, i].rearrange("p a t -> p (a t)")
                b = bank.take()
                for e, src in enumerate((qT, hT)):
                    t = T.matmul(ps[:, b, 256 * e:256 * e + 256], src[lo_p:lo_p + 64, hh // 2, i * P:(i + 1) * P], rhs,
                                 start=True, stop=True)
                t = pe.mark(t)
                m = dve(V.tensor_tensor, prod[:, 4 * i + hh], bank[b].rearrange("p (e t) -> p e t", e=4),
                        C("mask4").rearrange("p (e t) -> p e t", e=4), ALU.mult, after=[t])
                bank.give(b, m)
                yield
        while len(tiles) < 8 or "gating" not in marks:
            yield
        xc, gc = Carve(xt_flat), Carve(gates_flat)
        xinv, xinvT, lev, cx = xc(8, P), xc(8, P), gc(8, P), gc(8, P)
        idb = spread(C("ident"), 1, 8)
        lvl = C("levels").rearrange("p (l t) -> p l t", l=6)
        dve(V.tensor_tensor, lev, prod[:, :, 0, :], spread(lvl[:, 0, :], 1, 8), ALU.mult,
            after=[tiles[7], marks["gating"], pe.now()])
        m = dve(V.tensor_tensor, xinvT, idb, lev, ALU.subtract)
        pe.wait(m)
        for g in range(2):
            b = bank.take()
            for e in range(4):
                t = transpose(b, e * P, xinvT[:, 4 * g + e, :])
            t = pe.mark(t)
            m = act(S.copy, xinv[:, 4 * g:4 * g + 4, :], bank[b].rearrange("p (e t) -> p e t", e=4), after=[t, m])
            bank.give(b, m)
        pe.wait(m)
        dve.wait(m)
        for l in range(1, 6):
            m = dve(V.tensor_tensor, lev, prod[:, :, 0, :], spread(lvl[:, l, :], 1, 8), ALU.mult)
            yield
            pe.wait(m)
            for g in range(2):
                b = bank.take()
                for e in range(4):
                    t = T.matmul(ps[:, b, e * P:(e + 1) * P], lev[:, 4 * g + e, :], xinv[:, 4 * g + e, :], start=True, stop=True)
                t = pe.mark(t)
                k_ = act(S.copy, cx[:, 4 * g:4 * g + 4, :], bank[b].rearrange("p (e t) -> p e t", e=4), after=[t])
                bank.give(b, k_)
            yield
            pe.wait(k_)
            for g in range(2):
                b1, b2 = bank.take(), bank.take()
                for e in range(4):
                    T.matmul(ps[:, b1, e * P:(e + 1) * P], xinvT[:, 4 * g + e, :], cx[:, 4 * g + e, :], start=True, stop=True)
                    t = T.matmul(ps[:, b2, e * P:(e + 1) * P], cx[:, 4 * g + e, :], xinvT[:, 4 * g + e, :], start=True, stop=True)
                t = pe.mark(t)
                for b, dst in ((b1, xinv), (b2, xinvT)):
                    m = dve(V.tensor_tensor, dst[:, 4 * g:4 * g + 4, :], dst[:, 4 * g:4 * g + 4, :],
                            bank[b].rearrange("p (e t) -> p e t", e=4), ALU.subtract, after=[t])
                    bank.give(b, m)
                yield
        np_, utp, yg = xinv, lev, cx
        pe.wait(m)
        b = bank.take()
        for e in range(8):
            i, hh = divmod(e, 4)
            t = T.matmul(ps[:, b, e * HD:(e + 1) * HD], prod[:, e, 2, :], v[:, i, hh * HD:(hh + 1) * HD], start=True, stop=True)
        t = pe.mark(t)
        m = dve(V.tensor_copy, np_[:, :, 0:HD], bank[b].rearrange("p (e d) -> p e d", e=8), after=[t])
        bank.give(b, m)
        for i in range(NT):
            m = dve(V.tensor_copy, np_[:, 4 * i:4 * i + 4, HD:P], kp[:, i, :].rearrange("p (h d) -> p h d", h=4))
        yield
        pe.wait(m)
        for g in range(2):
            b = bank.take()
            for e in range(4):
                t = T.matmul(ps[:, b, e * P:(e + 1) * P], xinvT[:, 4 * g + e, :], np_[:, 4 * g + e, :], start=True, stop=True)
            t = pe.mark(t)
            m = dve(V.tensor_scalar, utp[:, 4 * g:4 * g + 4, :], bank[b].rearrange("p (e t) -> p e t", e=4), -1.0, None,
                    ALU.mult, after=[t])
            bank.give(b, m)
        yield
        pe.wait(m)
        for g in range(2):
            b = bank.take()
            for e in range(4):
                m3 = prod[:, 4 * g + e, 1, :]
                T.matmul(ps[:, b, e * P:e * P + HD], m3, utp[:, 4 * g + e, 0:HD], start=True, stop=False)
                T.matmul(ps[:, b, e * P:e * P + HD], prod[:, 4 * g + e, 3, :], v[:, g, e * HD:(e + 1) * HD],
                         start=False, stop=True)
                t = T.matmul(ps[:, b, e * P + HD:(e + 1) * P], m3, utp[:, 4 * g + e, HD:P], start=True, stop=True)
            t = pe.mark(t)
            src = bank[b].rearrange("p (e t) -> p e t", e=4)
            dve(V.tensor_copy, y[:, g, :].rearrange("p (h d) -> p h d", h=4), src[:, :, 0:HD], after=[t])
            m = dve(V.tensor_tensor, yg[:, 4 * g:4 * g + 4, 0:HD], src[:, :, HD:P],
                    kr[:, g, :].rearrange("p (h d) -> p h d", h=4), ALU.add)
            bank.give(b, m)
        pe.wait(m)
        yield
        for i in range(NT):
            m = dve(V.tensor_copy, gnat[:, i, :].rearrange("p (h d) -> p h d", h=4), yg[:, 4 * i:4 * i + 4, 0:HD])
        pe.wait(m)
        b = bank.take()
        for pair in range(2):
            for i in range(NT):
                t = transpose(b, (2 * pair + i) * P, gnat[:, i, pair * P:(pair + 1) * P])
        t = pe.mark(t)
        m = act(S.copy, gT, bank[b].rearrange("p (a t) -> p a t", a=2), after=[t])
        bank.give(b, m)
        yield
        fb = [bank.take(), bank.take()]
        eb = [bank.take(), bank.take()]
        for c in range(3):
            i, lo_t = c // 2, 64 * (c % 2)
            rows_c = slice(lo_t, lo_t + 64)
            for hh in range(4):
                e, lo_p = 4 * i + hh, 64 * (hh % 2)
                out = ps[lo_p:lo_p + 64, fb[c % 2], (2 * i + hh // 2) * HD:(2 * i + hh // 2 + 1) * HD]
                hc = slice(hh * HD, (hh + 1) * HD)
                T.matmul(out, kq[rows_c, i, hc], utp[rows_c, e, 0:HD], start=True, stop=False)
                t = T.matmul(out, kh[rows_c, i, hc], v[rows_c, i, hc], start=False, stop=True)
        for c in (1, 2):
            i, lo_t = c // 2, 64 * (c % 2)
            rows_c = slice(lo_t, lo_t + 64)
            for hh in range(4):
                e, lo_p = 4 * i + hh, 64 * (hh % 2)
                t = T.matmul(ps[lo_p:lo_p + 64, eb[c % 2], (hh // 2) * HD:(hh // 2 + 1) * HD],
                             utp[rows_c, e, HD:P], kq[rows_c, i, hh * HD:(hh + 1) * HD], start=True, stop=True)
        t = pe.mark(t)
        for c in range(3):
            m = dve(V.tensor_copy, st_f[:, :, c, :],
                    ps[:, fb[c % 2], 128 * (c // 2):128 * (c // 2) + 128].rearrange("p (a d) -> p a d", a=2), after=[t])
        for c in (1, 2):
            k_ = [dve(V.tensor_tensor, st_e[lo_p:lo_p + 64, c - 1], ps[lo_p:lo_p + 64, eb[c % 2], 0:128]
                      .rearrange("p (a d) -> p a d", a=2), spread(C("ident")[lo_p:lo_p + 64, lo_p:lo_p + 64], 1, 2), ALU.add)
                  for lo_p in (0, 64)][-1]
        for b in fb + eb:
            bank.give(b, k_)
        yield
        for pair in range(2):
            m = dve(V.tensor_scalar, state[:, 1, pair, :], st_f[:, pair, 0, :], wc[:, pair, 0:1], None, ALU.mult)
        for c in (1, 2):
            pe.wait(m)
            sbk = [bank.take(), bank.take()]
            for hh in range(4):
                lo_p = 64 * (hh % 2)
                t = T.matmul(ps[lo_p:lo_p + 64, sbk[hh % 2], (hh // 2) * HD:(hh // 2 + 1) * HD],
                             st_e[lo_p:lo_p + 64, c - 1, hh // 2, :], state[lo_p:lo_p + 64, c, hh // 2, :],
                             start=True, stop=True)
            t = pe.mark(t)
            for par in range(2):
                lo_p = 64 * par
                m = dve(V.tensor_tensor, state[lo_p:lo_p + 64, c + 1],
                        ps[lo_p:lo_p + 64, sbk[par], 0:128].rearrange("p (a d) -> p a d", a=2),
                        st_f[lo_p:lo_p + 64, :, c, :], ALU.add, after=[t])
                bank.give(sbk[par], m)
            for pair in range(2):
                m = dve(V.tensor_scalar, state[:, c + 1, pair, :], state[:, c + 1, pair, :], wc[:, pair, c:c + 1], None,
                        ALU.mult)
            yield
        pe.wait(m)
        yb = [bank.take(), bank.take()]
        for c in (1, 2, 3):
            lo_t = 64 * (c % 2)
            for hh in range(4):
                lo_p = 64 * (hh % 2)
                t = T.matmul(ps[lo_t:lo_t + 64, yb[hh % 2], (2 * (c // 2) + hh // 2) * HD:(2 * (c // 2) + hh // 2 + 1) * HD],
                             gT[lo_p:lo_p + 64, hh // 2, 64 * c:64 * c + 64], state[lo_p:lo_p + 64, c, hh // 2, :],
                             start=True, stop=True)
        t = pe.mark(t)
        yv = y.rearrange("p i (a b d) -> p i a b d", a=2, b=2)
        for par in range(2):
            src = ps[:, yb[par], 0:256].rearrange("p (i a d) -> p i a d", i=2, a=2)
            dve(V.tensor_tensor, yv[64:128, 0, :, par, :], yv[64:128, 0, :, par, :], src[64:128, 0], ALU.add, after=[t])
            m = dve(V.tensor_tensor, yv[:, 1, :, par, :], yv[:, 1, :, par, :], src[:, 1], ALU.add)
            bank.give(yb[par], m)
        yield
        t1 = gnat
        head_norm(per_head(y), 8, HD, 64e-5, per_head(t1), st, after=[pe.now(), act.now()])
        dve(V.tensor_tensor, y, y, spread(rows("gn_g"), 1, NT), ALU.mult)
        dve(V.tensor_tensor, y, y, spread(rows("gn_b"), 1, NT), ALU.add)
        dve(V.tensor_tensor, t1, r, k2, ALU.mult)
        dve(V.tensor_tensor, t1, t1, spread(rows("r_k"), 1, NT), ALU.mult)
        dve(V.tensor_reduce, ss, per_head(t1), AXX, ALU.add)
        for i in range(NT):
            dve(V.tensor_tensor, t2[:, i, :].rearrange("p (h d) -> p h d", h=4),
                v[:, i, :].rearrange("p (h d) -> p h d", h=4), spread(ss[:, 4 * i:4 * i + 4], 2, HD), ALU.mult)
        dve(V.tensor_tensor, y, y, t2, ALU.add)
        dve(V.tensor_tensor, xn[:, :, 256:512], y, gg, ALU.mult)

    def route(small, ready):
        lw = Carve(route_mem)
        L, ex, sel, posx, gatx = lw(NT, NE), lw(NT, NE), lw(NT, NE), lw(NE + 1, NT), lw(NE + 1, NT)
        ww = Carve(zbuf)
        gt, eq = ww(NE, NE), ww(NE, NE)
        pe.wait(ready)
        b = bank.take()
        router = small("router").rearrange("p (k e) -> p k e", k=KD)
        for i in range(NT):
            for k in range(KD):
                t = T.matmul(ps[:, b, NE * i:NE * i + NE], xt[:, k, i * P:(i + 1) * P], router[:, k, :],
                             start=(k == 0), stop=(k == KD - 1))
        t = pe.mark(t)
        m = dve(V.tensor_tensor, L, ps[:, b, 0:NT * NE].rearrange("p (i e) -> p i e", i=NT), spread(small("rb"), 1, NT),
                ALU.add, after=[t])
        bank.give(b, m)
        for i in range(NT):
            other, own = spread(L[:, i, :], 1, NE), spread(L[:, i, :], 2, NE)
            dve(V.tensor_tensor, gt, other, own, ALU.is_gt)
            dve(V.tensor_tensor, eq, other, own, ALU.is_equal)
            dve(V.tensor_tensor, eq, eq, C("before").rearrange("p (e j) -> p e j", e=NE), ALU.mult)
            dve(V.tensor_tensor, gt, gt, eq, ALU.add)
            dve(V.tensor_reduce, sel[:, i, :], gt, AXX, ALU.add)
        selected = dve(V.tensor_scalar, sel, sel, 1.5, None, ALU.is_lt)
        sm = stat[:, 48:48 + NT]
        dve(V.tensor_reduce, sm, L, AXX, ALU.max)
        m = dve(V.tensor_tensor, ex, L, spread(sm, 2, NE), ALU.subtract)
        m = act(S.activation, ex, ex, ACT.Exp, after=[m])
        dve(V.tensor_tensor, ex, ex, sel, ALU.mult, after=[m])
        dve(V.tensor_reduce, sm, ex, AXX, ALU.add)
        dve(V.reciprocal, sm, sm)
        dve(V.tensor_tensor, ex, ex, spread(sm, 2, NE), ALU.mult)
        dve(V.memset, posx, -1.0)
        dve(V.memset, gatx, 0.0)
        pe.wait(selected)
        b = bank.take()
        T.matmul(ps[:, b, 0:NE], C("tri"), sel[:, 0, :], start=True, stop=True)
        T.matmul(ps[:, b, NE:2 * NE], C("tri"), sel[:, 1, :], start=True, stop=False)
        T.matmul(ps[:, b, NE:2 * NE], C("ones"), sel[:, 0, :], start=False, stop=True)
        T.matmul(ps[:, b, 2 * NE:3 * NE], C("ones"), sel[:, 0, :], start=True, stop=False)
        t = pe.mark(T.matmul(ps[:, b, 2 * NE:3 * NE], C("ones"), sel[:, 1, :], start=False, stop=True))
        counts = ps[:, b, 0:2 * NE].rearrange("p (i e) -> p i e", i=NT)
        dve(V.tensor_copy, gatx.rearrange("p e i -> p i e")[:, :, 0:NE], ex)
        pv = posx.rearrange("p e i -> p i e")[:, :, 0:NE]
        dve(V.tensor_tensor, pv, counts, sel, ALU.mult, after=[t])
        dve(V.tensor_scalar, pv, pv, -1.0, None, ALU.add)
        dve(V.tensor_reduce, sm[:, 0:1], ps[:, b, 2 * NE:3 * NE], AXX, ALU.max)
        m = dve(V.tensor_copy, most_i, sm[:, 0:1])
        bank.give(b, m)
        return ex, posx, gatx, most_i, m

    def spread_gates(ex):
        gate_all = zbuf[:, 0:NE * SEQ].rearrange("p (e t) -> p e t", e=NE)
        rep = xn.rearrange("p i n -> p (i n)").rearrange("p (i e t) -> p i e t", i=NT, e=NE)
        for i in range(NT):
            m = dve(V.tensor_copy, rep[:, i], spread(ex[:, i, :], 2, P))
        for n, (i, e0) in enumerate((i, e0) for i in range(NT) for e0 in (0, 4)):
            pe.wait(m)
            for e in range(4):
                t = T.matmul(ps[:, n, e * P:(e + 1) * P], rep[:, i, e0 + e, :], C("ident"), start=True, stop=True)
            t = pe.mark(t)
            k = dve(V.tensor_copy, gate_all[:, e0:e0 + 4, i * P:(i + 1) * P],
                    bank[n].rearrange("p (e t) -> p e t", e=4), after=[t])
        return gate_all, k

    def modulation(l, w):
        acc = w(2, COLS)
        bm = bank.take()
        read = [None, None]
        for c in range(16):
            while f"ada{c}" not in ring.held:
                yield
            wt, got = ring.get(f"ada{c}")
            wt = wt.rearrange("p (k n) -> p k n", k=KD)
            a = acc[:, c % 2, :]
            m = dve(V.tensor_scalar, a, wt[:, 0, :], cact[:, 0:1], None, ALU.mult, after=[got, read[c % 2]])
            for k in range(1, KD):
                if k == 4:
                    yield
                m = dve(V.scalar_tensor_tensor, out=a, in0=wt[:, k, :], scalar=cact[:, k:k + 1], in1=a, op0=ALU.mult,
                        op1=ALU.add)
            ring.release(f"ada{c}", m)
            pe.wait(m)
            for e in range(3):
                t = T.matmul(ps[:, bm, 3 * c + e:3 * c + e + 1], a[:, e * P:(e + 1) * P], C("ones")[:, 0:1], start=True, stop=True)
            read[c % 2] = pe.mark(t)
            yield
        m = act(S.copy, mods[:, 48 * l:48 * l + 48], ps[:, bm, 0:48], after=[read[1]])
        bank.give(bm, m)

    ZA = 1024
    gates_flat = gates2.rearrange("p g n -> p (g n)")
    xt_flat = xt.rearrange("p k t -> p (k t)")
    stats = lambda n: stat[:, 64 + 48 * n:112 + 48 * n]
    z1 = zbuf[:, 0:NT * DIN1].rearrange("p (i n) -> p i n", i=NT)
    col_at, _ = spans(COLS1)
    ring.schedule(layer_tiles(0))
    for l in range(2):
        kept = columns(cols[:, l, :], col_at)
        if l == 0:
            rms_rows([], xn)
        else:
            rms_rows(join(), xn)
        m = turn_xn([dve.now()], kept("g_mix"), after_w=[] if l else [loaded_cols])
        pe.wait(m)
        tiles, marks = {}, {}
        for _ in project(z1, DIN1, "win", (0, 1, 2), tiles):
            pass
        if l == 0:
            cos, sin, rope_ready = rope_tables(posi[:, 0:NT], C("inv1"), 8, Carve(work, 20000), [loaded_const, loaded_pos])
            act(S.activation, cact, cact, ACT.Silu, after=[loaded_c])
        buf, got = ring.get("small")
        small = columns(buf, small1)
        rbuf, got_rows = ring.get("rows")
        rows = columns(rbuf, rows1)
        ready = [tiles[0], tiles[1], tiles[2], got, got_rows, act.now()] + join()
        w = Carve(work)
        w_mix, w_att = Carve(work[:, 0:13100]), Carve(work[:, 13100:20736])
        alternate(time_mix(z1, small, rows, tiles, ready, w_mix), project(z1, DIN1, "win", range(3, 8), tiles),
                  spatial_gating(z1, small, tiles, ready), sparse_attention(z1, small, tiles, ready, w_att),
                  modulation(l, Carve(work[:, 20736:21504])))
        done = join()
        work_done[0] = done
        ring.release("small", *done)
        ring.release("rows", *done)
        turned = turn_xn(done)
        m = out_project("wout", turned, add_residual)
        m = rms_rows(join(), xn)
        m = turn_xn([m], kept("g_ffn"), after_w=join())
        if l == 0:
            feed_forward(d["ffn"], 0, m, add_residual)
        else:
            routed_feed_forward(kept, m)
        ring.schedule(ple_tiles(l) + (layer_tiles(1) if l == 0 else []))
        m = rms_rows(join(), xn)
        m = turn_xn([m], kept("g_ple"))
        up, got_up = ring.get("ple_up")
        pT = up[:, 2 * D:2 * D + 2 * SEQ].rearrange("p (k t) -> p k t", k=2)
        tb = Carve(zbuf)
        sg = tb(2, COLS)
        pe.wait(m)
        free_sg = [[], []]
        for c in range(3):
            n = min(COLS, D - c * COLS)
            wt, got_w = ring.get(f"pleg{c}")
            wt = wt[:, 0:KD * n].rearrange("p (k n) -> p k n", k=KD)
            pe.wait(got_w, got_up)
            for i in range(NT):
                b = bank.take()
                for k in range(KD):
                    t = T.matmul(ps[:, b, 0:n], xt[:, k, i * P:(i + 1) * P], wt[:, k, :], start=(k == 0), stop=(k == KD - 1))
                t = pe.mark(t)
                m = act(S.activation, sg[:, i, 0:n], ps[:, b, 0:n], ACT.Sigmoid, after=[t] + free_sg[i])
                bank.give(b, m)
                b = bank.take()
                for k in range(2):
                    u = T.matmul(ps[:, b, 0:n], pT[:, k, i * P:(i + 1) * P], up[:, k * D + c * COLS:k * D + c * COLS + n],
                                 start=(k == 0), stop=(k == 1))
                u = pe.mark(u)
                m = dve(V.tensor_tensor, sg[:, i, 0:n], sg[:, i, 0:n], ps[:, b, 0:n], ALU.mult, after=[m, u])
                bank.give(b, m)
                hs = h[:, i, c * COLS:c * COLS + n]
                m = dve(V.tensor_tensor, hs, hs, sg[:, i, 0:n], ALU.add)
                free_sg[i] = [m]
            ring.release(f"pleg{c}", u)
        ring.release("ple_up", u)

    ring.schedule([("final1", [(d["g_final"][0:1].to_broadcast([P, D]), 0)])])
    gf, got = ring.get("final1")
    rms_rows(join(), xn)
    m = dve(V.tensor_tensor, h, xn, spread(gf[:, 0:D], 1, NT), ALU.mult, after=[got])
    ring.release("final1", m)

    z2 = zbuf[:, 0:NT * DIN2].rearrange("p (i n) -> p i n", i=NT)
    loaded_const = fetch(cst[:, 0:width2], d["const2"], after=join())
    const[0] = tab2
    for e in (dve, act, pe):
        e.wait(loaded_const)
    cos2, sin2, rope2 = rope_tables(posi[:, NT:2 * NT], C("inv2"), 32, Carve(zbuf), join())
    small2, n_small2 = spans(SMALL2)
    rows2, n_rows2 = spans(ROWS2, n_small2)
    small2.update(rows2)

    def layer2_tiles(l):
        out = [("small", [(d["small2"][l], 0), (d["rows2"][l:l + 1].to_broadcast([P, d["rows2"].shape[1]]), n_small2)])]
        for c in range(-(-DIN2 // COLS)):
            n = min(COLS, DIN2 - c * COLS)
            out.append((f"win{c}", [(d["w_in2"][l, c, :, 0:KD * n], 0)]))
        out += [(f"wout{c}", [(d["w_out2"][l, c], 0)]) for c in range(3)]
        return out

    def adaptive(l, small, got):
        mod, gains = mods[:, 48 * l:48 * l + 48], mods[:, 96:112]
        m = dve(V.tensor_tensor, mod, mod, small("ada_b"), ALU.add, after=[got] + join())
        for e, (sc_at, name) in enumerate(((8, "g_mix"), (32, "g_ffn"))):
            o = gains[:, 8 * e:8 * e + 8]
            dve(V.tensor_scalar, o, mod[:, sc_at:sc_at + 8], 1.0, None, ALU.add)
            dve(V.tensor_tensor, o, o, small(name), ALU.mult)
        rep = Carve(zbuf)(16, P)
        for g, at in enumerate((16, 40)):
            m = dve(V.tensor_copy, rep[:, 8 * g:8 * g + 8, :], spread(mod[:, at:at + 8], 2, P))
        pe.wait(m)
        for q in range(4):
            b = bank.take()
            for e in range(4):
                t = T.matmul(ps[:, b, e * P:(e + 1) * P], rep[:, 4 * q + e, :], C("ident"), start=True, stop=True)
            t = pe.mark(t)
            m = act(S.copy, gates_flat[:, 512 * q:512 * q + 512], bank[b], after=[t])
            bank.give(b, m)
        return gains, mod, m

    def fox(z, small, tiles, ready, w):
        while 3 not in tiles:
            yield
        ready, st = ready + [tiles[c] for c in range(1, 4)], stats(0)
        qT, kT = w(NT, 2, P), w(2, SEQ)
        lf, e1, cq, rep = w(NT, 4), w(NT, 4), w(NT, 4), w(NT * 4, P)
        ck, cm, sbuf, pt, o = w(4, SEQ), w(4, SEQ), w(4 * SEQ), w(8, P), w(4, HD)
        dve(V.tensor_tensor, lf, z[:, :, 1280:1284], spread(small("fb"), 1, NT), ALU.add, after=ready)
        dve(V.tensor_scalar, cq, lf, -1.0, None, ALU.mult)
        m = dve(V.tensor_tensor, e1, lf, cq, ALU.max)
        m = act(S.activation, e1, e1, ACT.Exp, scale=-1.0, after=[m])
        m = dve(V.tensor_scalar, e1, e1, 1.0, None, ALU.add, after=[m])
        m = act(S.activation, e1, e1, ACT.Ln, after=[m])
        dve(V.tensor_scalar, lf, lf, 0.0, None, ALU.min, after=[m])
        dve(V.tensor_tensor, lf, lf, e1, ALU.subtract)
        m = dve(V.tensor_copy, rep, spread(lf.rearrange("p i h -> p (i h)"), 2, P))
        yield
        pe.wait(m, *ready)
        b = bank.take()
        T.matmul(ps[:, b, 0:4], C("tri"), lf[:, 0, :], start=True, stop=True)
        T.matmul(ps[:, b, 4:8], C("tri"), lf[:, 1, :], start=True, stop=False)
        t = pe.mark(T.matmul(ps[:, b, 4:8], C("ones"), lf[:, 0, :], start=False, stop=True))
        m = dve(V.tensor_copy, cq, ps[:, b, 0:8].rearrange("p (i h) -> p i h", i=NT), after=[t])
        bank.give(b, m)
        for pair in range(2):
            b = bank.take()
            for e in range(2):
                hh = 2 * pair + e
                T.matmul(ps[:, b, e * SEQ:e * SEQ + P], rep[:, hh, :], C("tri"), start=True, stop=True)
                T.matmul(ps[:, b, e * SEQ + P:(e + 1) * SEQ], rep[:, 4 + hh, :], C("tri"), start=True, stop=False)
                t = T.matmul(ps[:, b, e * SEQ + P:(e + 1) * SEQ], rep[:, hh, :], C("ones"), start=False, stop=True)
            t = pe.mark(t)
            m = dve(V.tensor_copy, ck[:, 2 * pair:2 * pair + 2, :], bank[b].rearrange("p (a s) -> p a s", a=2), after=[t])
            bank.give(b, m)
            yield
        for which in range(2):
            b = bank.take()
            for pair in range(2):
                for i in range(NT):
                    t = transpose(b, (2 * pair + i) * P, z[:, i, 512 + 256 * which + pair * P:512 + 256 * which + (pair + 1) * P])
            t = pe.mark(t)
            src = bank[b].rearrange("p (a i t) -> p a i t", a=2, i=NT)
            if which == 0:
                m = act(S.mul, qT.rearrange("p i a t -> p a i t"), src, HD ** -0.5, after=[t])
            else:
                m = act(S.copy, kT.rearrange("p a (i t) -> p a i t", i=NT), src, after=[t])
            bank.give(b, m)
            yield
        turned = m
        last = [dve.now()]
        for i in range(NT):
            n = P * (i + 1)
            pe.wait(turned, *last)
            dve(V.tensor_tensor, cm[:, :, 0:n], spread(C("causal")[:, P * i:P * i + n], 1, 4), ck[:, :, 0:n], ALU.subtract,
                after=last)
            s4 = sbuf[:, 0:4 * n].rearrange("p (h s) -> p h s", h=4)
            for par in range(2):
                b = bank.take()
                for a in range(2):
                    t = T.matmul(ps[:, b, a * n:(a + 1) * n], qT[64 * par:64 * par + 64, i, a, :],
                                 kT[64 * par:64 * par + 64, a, 0:n], start=True, stop=True)
                t = pe.mark(t)
                for a in range(2):
                    hh = 2 * a + par
                    m = dve(V.scalar_tensor_tensor, out=s4[:, hh, :], in0=ps[:, b, a * n:(a + 1) * n],
                            scalar=cq[:, i, hh:hh + 1], in1=cm[:, hh, 0:n], op0=ALU.add, op1=ALU.add, after=[t])
                bank.give(b, m)
            yield
            rs, m = softmax_rows(s4, 4, st)
            yield
            b, t = yield from weighted_values(s4, 4, i + 1, pt[:, 0:4 * (i + 1), :],
                                   lambda mm, st: z[:, st, 1024 + mm * HD:1024 + (mm + 1) * HD], m)
            m = dve(V.tensor_tensor, xn[:, i, 0:256].rearrange("p (h d) -> p h d", h=4),
                    ps[:, b, 0:256].rearrange("p (h d) -> p h d", h=4), spread(rs, 2, HD), ALU.mult, after=[t])
            bank.give(b, m)
            last = [m]
            yield

    def pooling(z, small, tiles, ready, w):
        while 4 not in tiles:
            yield
        ready = ready + [tiles[3], tiles[4]]
        dT = w(2, SEQ)
        band = C("band").rearrange("p (g n) -> p g n", g=4)
        pe.wait(*ready)
        b = bank.take()
        for g in range(4):
            o = ps[64 * (g % 2):64 * (g % 2) + 64, b, (g // 2) * SEQ:(g // 2 + 1) * SEQ]
            u0, u1 = (z[:, i, 1284 + g * HD:1284 + (g + 1) * HD] for i in range(NT))
            T.matmul(o[:, 0:P], u0, band[:, g, 0:P], start=True, stop=True)
            T.matmul(o[:, P:SEQ], u0, band[:, g, P:SEQ], start=True, stop=False)
            t = T.matmul(o[:, P:SEQ], u1, band[:, g, SEQ:SEQ + P], start=False, stop=True)
        t = pe.mark(t)
        m = act(S.copy, dT, bank[b].rearrange("p (a t) -> p a t", a=2), after=[t] + ready)
        bank.give(b, m)
        yield
        pe.wait(m)
        pw = small("pool_w").rearrange("p (a d) -> p a d", a=2)
        for par in range(2):
            b = bank.take()
            for i in range(NT):
                for a in range(2):
                    t = T.matmul(ps[:, b, (2 * i + a) * HD:(2 * i + a + 1) * HD], dT[64 * par:64 * par + 64, a, i * P:(i + 1) * P],
                                 pw[64 * par:64 * par + 64, a, :], start=True, stop=True)
            t = pe.mark(t)
            for i in range(NT):
                m = dve(V.tensor_tensor, xn[:, i, 256:512].rearrange("p (a b d) -> p a b d", a=2, b=2)[:, :, par, :],
                        ps[:, b, i * P:(i + 1) * P].rearrange("p (a d) -> p a d", a=2),
                        small("pool_scale").rearrange("p (a b d) -> p a b d", a=2, b=2)[:, :, par, :], ALU.mult, after=[t])
            bank.give(b, m)
            yield

    def retention(z, small, tiles, ready, w):
        while 6 not in tiles:
            yield
        ready, st_ = ready + [tiles[c] for c in range(4, 7)], stats(1)
        qk, tmp = w(2, NT, 256), w(1024)
        qT, kT, st, o, t1 = w(2, SEQ), w(2, SEQ), w(4, 384), w(NT, 256), w(NT, 256)
        hv = lambda ap: ap.rearrange("p i (h d) -> p i h d", h=4)
        for which in range(2):
            src = z[:, :, 1540 + 256 * which:1796 + 256 * which]
            m = rotate(hv(qk[:, which]), hv(src), 4, 32, cos2, sin2, tmp, after=ready + [rope2])
            yield
        pe.wait(m)
        for which, dst in ((0, qT), (1, kT)):
            b = bank.take()
            for pair in range(2):
                for i in range(NT):
                    t = transpose(b, (2 * pair + i) * P, qk[:, which, i, pair * P:(pair + 1) * P])
            t = pe.mark(t)
            m = act(S.copy, dst, bank[b].rearrange("p (a t) -> p a t", a=2), after=[t])
            bank.give(b, m)
            yield
        pe.wait(m)
        dec = C("decay").rearrange("p (h n) -> p h n", h=4)
        for hh in range(4):
            lo_p = 64 * (hh % 2)
            b = bank.take()
            qh, kh = qT[lo_p:lo_p + 64, hh // 2, :], kT[lo_p:lo_p + 64, hh // 2, :]
            T.matmul(ps[:, b, 0:SEQ], kh[:, 0:P], qh, start=True, stop=True)
            t = pe.mark(T.matmul(ps[:, b, SEQ:SEQ + P], kh[:, P:SEQ], qh[:, P:SEQ], start=True, stop=True))
            m = dve(V.tensor_tensor, st[:, hh, :], ps[:, b, 0:384], dec[:, hh, :], ALU.mult, after=[t])
            bank.give(b, m)
            yield
        pe.wait(m)
        b = bank.take()
        for hh in range(4):
            v = lambda i: z[:, i, 2052 + hh * HD:2052 + (hh + 1) * HD]
            T.matmul(ps[:, b, hh * HD:(hh + 1) * HD], st[:, hh, 0:P], v(0), start=True, stop=True)
            T.matmul(ps[:, b, 256 + hh * HD:256 + (hh + 1) * HD], st[:, hh, P:SEQ], v(0), start=True, stop=False)
            t = T.matmul(ps[:, b, 256 + hh * HD:256 + (hh + 1) * HD], st[:, hh, SEQ:SEQ + P], v(1), start=False, stop=True)
        t = pe.mark(t)
        m = dve(V.tensor_copy, o, bank[b].rearrange("p (i n) -> p i n", i=NT), after=[t])
        bank.give(b, m)
        g = act(S.activation, tmp[:, 0:512].rearrange("p (i n) -> p i n", i=NT), z[:, :, 2308:2564], ACT.Silu,
                after=ready + [dve.now()])
        per_head = lambda ap: ap.rearrange("p i (h d) -> p (i h) d", h=4)
        yield
        head_norm(per_head(o), 8, HD, 1e-6, per_head(t1), st_)
        yield
        dve(V.tensor_tensor, o, o, spread(small("gn_g"), 1, NT), ALU.mult)
        dve(V.tensor_tensor, xn[:, :, 512:768], o, tmp[:, 0:512].rearrange("p (i n) -> p i n", i=NT), ALU.mult,
            after=[g])

    def conformer(z, small, tiles, ready, w):
        while 1 not in tiles:
            yield
        ready, st = ready + [tiles[0], tiles[1]], stats(2)
        gl, padded, acc, y, t1 = w(NT, 256), w(2, CONVW - 1 + SEQ), w(2, SEQ), w(NT, 256), w(NT, 256)
        m = act(S.activation, gl, z[:, :, 256:512], ACT.Sigmoid, after=ready)
        m = dve(V.tensor_tensor, gl, gl, z[:, :, 0:256], ALU.mult, after=[m])
        dve(V.memset, padded[:, :, 0:CONVW - 1], 0.0)
        pe.wait(m)
        b = bank.take()
        for a in range(2):
            for i in range(NT):
                t = transpose(b, (2 * a + i) * P, gl[:, i, a * P:(a + 1) * P])
        t = pe.mark(t)
        m = act(S.copy, padded[:, :, CONVW - 1:], bank[b].rearrange("p (a t) -> p a t", a=2), after=[t, dve.now()])
        bank.give(b, m)
        cw = small("conv_w").rearrange("p (a j) -> p a j", a=2)
        for a in range(2):
            dve(V.tensor_scalar, acc[:, a, :], padded[:, a, 0:SEQ], cw[:, a, 0:1], small("conv_b")[:, a:a + 1],
                ALU.mult, ALU.add, after=[m])
        for j in range(1, CONVW):
            for a in range(2):
                m = dve(V.scalar_tensor_tensor, out=acc[:, a, :], in0=padded[:, a, j:j + SEQ], scalar=cw[:, a, j:j + 1],
                        in1=acc[:, a, :], op0=ALU.mult, op1=ALU.add)
            yield
        pe.wait(m)
        b = bank.take()
        for i in range(NT):
            for a in range(2):
                t = transpose(b, (2 * i + a) * P, acc[:, a, i * P:(i + 1) * P])
        t = pe.mark(t)
        m = dve(V.tensor_copy, y, bank[b].rearrange("p (i n) -> p i n", i=NT), after=[t])
        bank.give(b, m)
        yield
        head_norm(y, NT, 256, 1e-6, t1, st)
        dve(V.tensor_tensor, y, y, spread(small("ln_g"), 1, NT), ALU.mult)
        m = dve(V.tensor_tensor, y, y, spread(small("ln_b"), 1, NT), ALU.add)
        act(S.activation, xn[:, :, 768:1024], y, ACT.Silu, after=[m])

    def gated_add(which):
        def add(i, q, src, t):
            tmp = xn[:, i, q * 512:(q + 1) * 512]
            dve(V.tensor_tensor, tmp, src, gates2[:, which, q * 512:(q + 1) * 512], ALU.mult, after=[t])
            hs = h[:, i, q * 512:(q + 1) * 512]
            return dve(V.tensor_tensor, hs, hs, tmp, ALU.add)
        return add

    for l in range(2):
        ring.schedule(layer2_tiles(l))
        buf, got = ring.get("small")
        small = columns(buf, small2)
        gains, mod, m = adaptive(l, small, got)
        rms_rows(join(), xn)
        m = turn_xn([dve.now()], gains[:, 0:8], mod[:, 0:8])
        pe.wait(m)
        tiles, marks = {}, {}
        ready = [m, got] + join()
        w = Carve(work)
        alternate(project(z2, DIN2, "win", range(7), tiles),
                  conformer(z2, small, tiles, ready, Carve(work[:, 0:2800])),
                  fox(z2, small, tiles, ready, Carve(work[:, 2800:9500])),
                  pooling(z2, small, tiles, ready, Carve(work[:, 9500:10100])),
                  retention(z2, small, tiles, ready, Carve(work[:, 10100:16000])))
        done = join()
        work_done[0] = done
        ring.release("small", *done)
        turned = turn_xn(done)
        m = out_project("wout", turned, gated_add(0))
        m = rms_rows(join(), xn)
        m = turn_xn([m], gains[:, 8:16], mod[:, 24:32], after_w=join())
        m = feed_forward(d["ffn2"], l * FB, m, gated_add(1))

    ring.schedule([("final2", [(d["g_final"][1:2].to_broadcast([P, D]), 0)])])
    gf, got = ring.get("final2")
    rms_rows(join(), xn)
    m = dve(V.tensor_tensor, xn, xn, spread(gf[:, 0:D], 1, NT), ALU.mult, after=[got])
    sp.wait(m)
    s_out = nc.alloc_semaphore("s_out")
    nc.sync.dma_start(d["out"], xn).then_inc(s_out, 16)
    nc.sync.wait_ge(s_out, 16)


def column_tiles(w, cols=COLS):
    L, _, n = w.shape
    t = -(-n // cols)
    out = np.zeros((L, t, P, KD * cols), np.float32)
    for c in range(t):
        m = min(cols, n - c * cols)
        out[:, c, :, 0:KD * m] = w[:, :, c * cols:c * cols + m].reshape(L, KD, P, m).transpose(0, 2, 1, 3).reshape(L, P, KD * m)
    return out


def row_tiles(w):
    L = w.shape[0]
    out = np.zeros((L, 3, P, 3, D), np.float32)
    blocks = w.reshape(L, KD, P, D)
    for k in range(KD):
        out[:, k // 3, :, k % 3] = blocks[:, k]
    return out.reshape(L, 3, P, 3 * D)


def ffn_tiles(w1, w3, w2):
    E = w1.shape[0]
    out = np.empty((E, FB, P, 3, D), np.float32)
    for e, w in enumerate((w1, w3)):
        out[:, :, :, e] = w.reshape(E, KD, P, FB, P).transpose(0, 3, 2, 1, 4).reshape(E, FB, P, D)
    out[:, :, :, 2] = w2.reshape(E, FB, P, D)
    return out.reshape(E * FB, P, 3 * D)


def by_partition(v):
    return v.reshape(v.shape[0], -1, P).transpose(0, 2, 1)


def pack(fields, values):
    return np.concatenate([np.asarray(values[n], np.float32).reshape(2, P, w) for n, w in fields], axis=2)


def pack_rows(fields, values):
    return np.concatenate([values[n].reshape(2, w) for n, w in fields], axis=1)


def lay_out(a):
    one, two = const_arrays()
    w_in = a["w_in"]
    zc = 1536
    q = w_in[:, :, zc:zc + 512].reshape(2, D, 2, 4, HD).transpose(0, 1, 3, 2, 4).reshape(2, D, 512)
    gates = w_in[:, :, zc + 1280:].reshape(2, D, 2, 4, 3).transpose(0, 1, 4, 3, 2).reshape(2, D, 24)
    w_in = np.concatenate([w_in[:, :, 512:zc], w_in[:, :, :512], q, w_in[:, :, zc + 512:zc + 1280], gates], axis=2)
    w_out = a["w_out"]
    tail = w_out[:, 512:].reshape(2, 2, 4, HD, D).transpose(0, 2, 1, 3, 4).reshape(2, 512, D)
    w_out = np.concatenate([w_out[:, :512], tail], axis=1)
    lora = np.zeros((2, P, 512), np.float32)
    lora[:, :64, :256] = a["rw_w_up"]
    lora[:, 64:, 256:] = a["rw_a_up"]
    pos = a["nsa_cmp_pos"].reshape(2, 16, 2, HD).transpose(0, 2, 3, 1).reshape(2, P, 16)
    router = a["router_w"].reshape(1, KD, P, NE).transpose(0, 2, 1, 3).reshape(1, P, KD * NE)
    small1 = pack(SMALL1, {
        "kc_w2": a["nsa_kc_w2"], "vc_w2": a["nsa_vc_w2"], "pos": pos, "lora": lora, "g_up": a["rw_g_up"],
        "wst": a["gm_ws"].transpose(0, 3, 1, 2).reshape(2, P, 512), "bs": a["gm_bs"].transpose(0, 2, 1)})
    rb = np.broadcast_to(a["router_b"][:, None, :], (1, P, NE))
    cols = pack(COLS1, {
        "g_mix": by_partition(a["g_mix"]), "g_ffn": by_partition(a["g_ffn"]), "g_ple": by_partition(a["g_ple"]),
        "router": np.concatenate([router, router]), "rb": np.concatenate([rb, rb])})
    rows1 = pack_rows(ROWS1, {"mu": a["rw_mu"], "wa0": np.concatenate([a["rw_w0"], a["rw_a0"]], 1), "k_k": a["rw_k_k"],
                              "k_a": a["rw_k_a"], "r_k": a["rw_r_k"], "gn_g": a["rw_gn_g"], "gn_b": a["rw_gn_b"]})
    rows1b = pack_rows(ROWS1B, {"ln_g": a["gm_ln_g"], "ln_b": a["gm_ln_b"]})
    cmp_w1 = lambda w: w.reshape(2, 16, P, P).transpose(0, 2, 1, 3).reshape(2, P, 2048)
    ple = np.concatenate([a["ple_proj_w"].reshape(2, 2, P, D).transpose(0, 2, 1, 3).reshape(2, P, 2 * D),
                          a["p"].reshape(2, SEQ, 2, P).transpose(0, 3, 2, 1).reshape(2, P, 2 * SEQ)], axis=2)
    ada_b = a["ada_b_2"]
    c = by_partition(a["c_2"])
    pool_w = a["pool_w_2"].reshape(2, 2, 2, HD, HD).transpose(0, 2, 3, 1, 4).reshape(2, P, 128)
    conv_w = a["conv_w_2"].reshape(2, CONVW, 2, P).transpose(0, 3, 2, 1).reshape(2, P, 62)
    small2 = pack(SMALL2, {
        "g_mix": by_partition(a["norm_mix_g_2"]), "g_ffn": by_partition(a["norm_ffn_g_2"]), "pool_w": pool_w,
        "conv_w": conv_w, "conv_b": by_partition(a["conv_b_2"]), "ada_b": by_partition(ada_b)})
    w_in2 = np.concatenate([a["w_in_2"][:, :, 2052:], a["w_in_2"][:, :, :2052]], axis=2)
    rows2 = pack_rows(ROWS2, {"pool_scale": a["pool_scale_2"], "gn_g": a["ret_gn_g_2"], "ln_g": a["conv_ln_g_2"],
                              "ln_b": a["conv_ln_b_2"], "fb": a["fox_fb_2"]})
    tokens = lambda v: v.reshape(NT, P).transpose(1, 0)
    return {
        "const1": np.concatenate(list(one.values()), 1), "const2": np.concatenate(list(two.values()), 1),
        "x": a["x"].reshape(NT, P, D).transpose(1, 0, 2),
        "pos": np.concatenate([tokens(a["positions"]), tokens(a["positions_2"])], 1),
        "small1": small1, "rows1": rows1, "rows1b": rows1b, "w_in": column_tiles(w_in), "w_out": row_tiles(w_out),
        "kc_w1": cmp_w1(a["nsa_kc_w1"]), "vc_w1": cmp_w1(a["nsa_vc_w1"]), "ple_proj": ple,
        "ple_gate": column_tiles(a["ple_gate_w"]), "ffn": ffn_tiles(a["ffn_w1"], a["ffn_w3"], a["ffn_w2"]),
        "moe": ffn_tiles(a["moe_w1"][0], a["moe_w3"][0], a["moe_w2"][0]),
        "g_final": np.concatenate([a["g_final"], a["final_g_2"]]).reshape(2, D),
        "small2": small2, "rows2": rows2, "cols": cols.transpose(1, 0, 2), "c": c[0], "ada": column_tiles(a["ada_w_2"]),
        "w_in2": column_tiles(w_in2), "w_out2": row_tiles(a["w_out_2"]),
        "ffn2": ffn_tiles(a["ffn_w1_2"], a["ffn_w3_2"], a["ffn_w2_2"]),
    }


def kernel(**inputs):
    import concourse.bacc as bacc
    from concourse.bass_utils import run_bass_kernel_spmd

    arrays = lay_out({k: np.asarray(v) for k, v in inputs.items()})
    nc = bacc.Bacc("TRN2", target_bir_lowering=False, num_devices=1)
    ins, d = {}, {}
    for name, v in arrays.items():
        v = np.ascontiguousarray(v)
        ins["in_" + name] = v
        d[name] = nc.dram_tensor("in_" + name, v.shape, mybir.dt.from_np(v.dtype), kind="ExternalInput").ap()
    d["out"] = nc.dram_tensor("out", (P, NT, D), F32, kind="ExternalOutput").ap()
    build(nc, d)
    r = run_bass_kernel_spmd(nc, [ins], core_ids=[0])
    out = r.results[0]["out"]
    return np.ascontiguousarray(out.transpose(1, 0, 2).reshape(1, SEQ, D))
```

```python
import math

import numpy as np

import concourse.bass as bass
from concourse import mybir
from concourse.mybir import EngineType

F32 = mybir.dt.float32
I32 = mybir.dt.int32
ALU = mybir.AluOpType
ACT = mybir.ActivationFunctionType
AXX = mybir.AxisListType.X
LOADER = (EngineType.SP,)
WORKERS = (EngineType.PE, EngineType.Activation, EngineType.DVE)

P = 128
SEQ, D = 256, 1024
NT = SEQ // P
KD = D // P
HD = 64
FF = 2816
FB = FF // P
NE = 8
SLOT = 3072
NSLOT = 11
NWALK = 4
COLS = SLOT // KD
DIN1, DIN2 = 2840, 2564
NEG = -1e30
NCMP = (SEQ - 32) // 16 + 1
POOLW = (2, 4, 8, 16)
CONVW = 31


def const_arrays():
    s = np.arange(P)[:, None]
    t = np.arange(P)[None, :]
    f = np.float32
    one = {}
    one["ident"] = (s == t)
    one["tri"] = (s <= t)
    same = (s // 64 == t // 64)
    one["tri64"] = (s <= t) & same
    one["shift"] = (t == s + 1)
    one["carry"] = (s == P - 1) & (t == 0)
    strict, incl = (s < t) & same, (s <= t) & same
    one["mask4"] = np.concatenate([strict, incl, strict, incl], 1)
    one["levels"] = np.concatenate(
        [((s // (2 * b) == t // (2 * b)) & (s % (2 * b) < b) & (t % (2 * b) >= b)) for b in (1, 2, 4, 8, 16, 32)], 1)
    one["half"] = (np.arange(P)[:, None] // 64 == np.arange(2)[None, :])
    tok = np.arange(P)[:, None, None] + P * np.arange(NT)[None, :, None]
    end = (np.arange(NCMP) * 16 + 31)[None, None, :]
    one["cmp01"] = (end <= tok).reshape(P, -1)
    one["cmpneg"] = np.where(end <= tok, 0.0, NEG).reshape(P, -1)
    one["before"] = np.broadcast_to((np.arange(8)[None, :] < np.arange(8)[:, None]).reshape(1, 64), (P, 64))
    one["inv1"] = np.broadcast_to((1.0 / (f(500000.0) ** (np.arange(0, 16, 2, dtype=f) / f(16)))).astype(f)[None], (P, 8))
    diag = np.where(t <= s, 0.0, NEG)
    one["causal"] = np.concatenate([diag, np.zeros((P, P)), diag], 1)
    one["ones"] = np.ones((P, P))
    one["slots"] = np.broadcast_to(np.arange(P)[None, :], (P, P))
    two = {k: one[k] for k in ("ident", "tri", "causal", "ones")}
    sk = np.arange(SEQ)[:, None]
    tk = np.arange(SEQ)[None, :]
    band = []
    for w in POOLW:
        m = ((sk <= tk) & (sk > tk - w)) / np.minimum(tk + 1, w).astype(f) - (sk == tk)
        band += [m[:P], m[P:, P:]]
    two["band"] = np.concatenate(band, 1)
    decay = []
    for h in range(4):
        lg = math.log(1.0 - 2.0 ** (-5.0 - h))
        m = np.where(sk <= tk, np.exp(lg * np.maximum(tk - sk, 0)), 0.0) * HD ** -0.5
        decay += [m[:P], m[P:, P:]]
    two["decay"] = np.concatenate(decay, 1)
    two["inv2"] = np.broadcast_to((f(10000.0) ** (-np.arange(32, dtype=f) / f(32))).astype(f)[None], (P, 32))
    fix = lambda d: {k: np.ascontiguousarray(v, dtype=f) for k, v in d.items()}
    return fix(one), fix(two)


def const_table(d):
    out, at = {}, 0
    for k, v in d.items():
        out[k] = (at, v.shape[1])
        at += v.shape[1]
    return out, at


COLS1 = [("g_mix", 8), ("g_ffn", 8), ("g_ple", 8), ("router", 64), ("rb", 8)]
SMALL1 = [("kc_w2", 64), ("vc_w2", 64), ("pos", 16), ("lora", 512), ("g_up", 256), ("wst", 512), ("bs", 4)]
ROWS1 = [("mu", 1024), ("wa0", 512), ("k_k", 256), ("k_a", 256), ("r_k", 256), ("gn_g", 256), ("gn_b", 256)]
ROWS1B = [("ln_g", 256), ("ln_b", 256)]
SMALL2 = [("g_mix", 8), ("g_ffn", 8), ("pool_w", 128), ("conv_w", 62), ("conv_b", 2), ("ada_b", 48)]
ROWS2 = [("pool_scale", 256), ("gn_g", 256), ("ln_g", 256), ("ln_b", 256), ("fb", 4)]


def spans(fields, at=0):
    out = {}
    for name, width in fields:
        out[name] = (at, width)
        at += width
    return out, at


LOAD_US, PE_COLUMN_US = 0.22, 4 / 2400
ELEMENT_US, ISSUE_US, LATENCY_US = 1 / 960, 0.06, 0.15


def columns_of(*aps):
    return max([math.prod(a.shape[1:]) for a in aps if not isinstance(a, (int, float)) and a is not None and "shape" in dir(a)] + [1])


class Mark:

    def __init__(self, sem, value, loop=None, step=0, due=0.0):
        self.sem, self.value, self.loop, self.step, self.due = sem, value, loop, step, due

    def last(self):
        return Mark(self.sem, self.value + (self.loop.turns - 1) * self.step)


class Loop:
    def __init__(self, turn, turns):
        self.turn, self.turns = turn, turns


class Engine:

    def __init__(self, nc, q, name, chained):
        self.nc, self.q, self.chained = nc, q, chained
        self.sem = nc.alloc_semaphore("s_" + name)
        self.n, self.loop, self.step, self.met = 0, None, 0, {}
        self.clock, self.need, self.cost = 0.0, 0.0, 0.0
        self.own, self.part = {}, None

    def spend(self, us):
        self.cost += us

    def wait(self, *marks):
        for m in marks:
            if m is None:
                continue
            if isinstance(m, (list, tuple)):
                self.wait(*m)
                continue
            self.need = max(self.need, m.due)
            if m.loop is not None and m.loop is self.loop:
                self.q.wait_ge(m.sem, self.loop.turn * m.step + m.value)
                continue
            assert m.loop is None
            key = m.sem.name
            if self.met.get(key, -1) >= m.value:
                continue
            if self.loop is None:
                self.met[key] = m.value
            self.q.wait_ge(m.sem, m.value)

    def mark(self, ins):
        ins.then_inc(self.sem, 1)
        self.n += 1
        self.clock = max(self.clock, self.need) + self.cost
        self.need = self.cost = 0.0
        m = Mark(self.sem, self.n, self.loop, self.step, self.clock + LATENCY_US)
        self.own[self.part] = m
        return m

    def now(self):
        if self.part is not None:
            return self.own[self.part]
        return Mark(self.sem, self.n, self.loop, self.step, self.clock + LATENCY_US)

    def __call__(self, op, *args, after=(), **kw):
        self.wait(*after)
        if self.chained and self.n:
            self.wait(self.now())
        self.spend(ISSUE_US + ELEMENT_US * columns_of(*args, *kw.values()))
        return self.mark(op(*args, **kw))

    def enter(self, loop, step):
        self.loop, self.step, self.first, self.met = loop, step, self.n, {}

    def at(self, offset):
        return Mark(self.sem, self.first + offset, self.loop, self.step)

    def branch(self, name):
        self.common = (self.sem, self.n)
        self.sem, self.n, self.met = self.nc.alloc_semaphore(f"s_{name}_{self.sem.name[2:]}"), 0, {}

    def rejoin(self):
        (self.sem, self.n), self.met = self.common, {}

    def leave(self):
        assert self.n == self.first + self.step, (self.n, self.first, self.step)
        self.n = self.first + self.step * self.loop.turns
        self.loop, self.met = None, {}


class Banks:

    def __init__(self, ps, pe):
        self.ps, self.pe, self.order, self.free = ps, pe, list(range(8)), [[] for _ in range(8)]

    def take(self):
        b = self.order.pop(0)
        self.pe.wait(*self.free[b])
        return b

    def give(self, b, *marks):
        self.free[b] = list(marks)
        self.order.append(b)

    def __getitem__(self, b):
        return self.ps[:, b, :]


class Ring:

    def __init__(self, nc, sp, mem):
        self.nc, self.sp, self.mem = nc, sp, mem
        self.sems = [nc.alloc_semaphore(f"s_slot{i}") for i in range(NSLOT)]
        self.count = [0] * NSLOT
        self.free = [[] for _ in range(NSLOT)]
        self.plan, self.held, self.order = [], {}, list(range(NWALK))

    def schedule(self, tiles):
        self.plan += tiles
        self.pump()

    def pump(self):
        while self.plan and self.order:
            name, parts = self.plan.pop(0)
            s = self.order.pop(0)
            self.sp.wait(*self.free[s])
            for src, at in parts:
                n = src.shape[-1]
                self.sp.q.dma_start(self.mem[:, s, at:at + n], src).then_inc(self.sems[s], 16)
                self.count[s] += 16
            self.held[name] = (s, Mark(self.sems[s], self.count[s]))

    def get(self, name):
        s, m = self.held[name]
        return self.mem[:, s, :], m

    def release(self, name, *marks):
        s, _ = self.held.pop(name)
        self.free[s] = list(marks)
        self.order.append(s)
        self.pump()


class Carve:

    def __init__(self, mem, at=0):
        self.mem, self.at, self.size = mem, at, mem.shape[1]

    def __call__(self, *dims):
        n = 1
        for d in dims:
            n *= d
        ap = self.mem[:, self.at:self.at + n]
        self.at += n
        assert self.at <= self.size, (self.at, self.size)
        if len(dims) == 2:
            ap = ap.rearrange("p (a b) -> p a b", a=dims[0])
        elif len(dims) == 3:
            ap = ap.rearrange("p (a b c) -> p a b c", a=dims[0], b=dims[1])
        elif len(dims) == 4:
            ap = ap.rearrange("p (a b c d) -> p a b c d", a=dims[0], b=dims[1], c=dims[2])
        return ap


def alternate(engines, *parts):
    start = max(e.clock for e in engines)
    for e in engines:
        e.clock, e.own = start, {n: e.now() for n in range(len(parts))}
    due, idle = {n: start for n in range(len(parts))}, set()
    while due:
        n = min((n for n in due if n not in idle), key=lambda n: due[n])
        before = [e.n for e in engines]
        for e in engines:
            e.part = n
        going = next(parts[n], "end") != "end"
        if not going:
            del due[n]
        if [e.n for e in engines] != before or not going:
            idle = set()
            if going:
                due[n] = max(e.own[n].due for e, b in zip(engines, before) if e.n != b)
        else:
            idle.add(n)
        if going and len(idle) == len(due):
            again += 1
            assert again < 4
            idle = set()
        else:
            again = 0
    for e in engines:
        e.part = None


def spread(ap, axis, n):
    ap = ap.unsqueeze(axis)
    shape = list(ap.shape)
    shape[axis] = n
    return ap.to_broadcast(shape)


def build(nc, d):
    V, S, T, G = nc.vector, nc.scalar, nc.tensor, nc.gpsimd
    dve = Engine(nc, V, "dve", True)
    act = Engine(nc, S, "act", True)
    pool = Engine(nc, G, "pool", True)
    pe = Engine(nc, T, "pe", False)
    sp = Engine(nc, nc.sync, "sp", False)

    def sb(name, n, dt=F32):
        return nc.alloc_sbuf_tensor(name, [P, n], dt)[:, :]

    one, two = const_arrays()
    tab1, width1 = const_table(one)
    tab2, width2 = const_table(two)
    h = sb("residual", NT * D).rearrange("p (i n) -> p i n", i=NT)
    xn = sb("natural", NT * D).rearrange("p (i n) -> p i n", i=NT)
    xt = sb("transposed", KD * SEQ).rearrange("p (k t) -> p k t", k=KD)
    zbuf = sb("z", NT * DIN1)
    cst = sb("constants", max(width1, width2))
    stat = sb("stat", 64 + 4 * 48)
    ang = sb("rope", 4 * NT * 32)
    gates2 = sb("gates2", 2 * D).rearrange("p (g n) -> p g n", g=2)
    zero = sb("zero", 512)
    ringm = nc.alloc_sbuf_tensor("ring", [P, NSLOT, SLOT], F32)[:, :, :]
    work = ringm.rearrange("p s n -> p (s n)")[:, NWALK * SLOT:]
    ps = nc.alloc_psum_tensor("ps", [P, 8, 512], F32)[:, :, :]
    bank = Banks(ps, pe)
    ring = Ring(nc, sp, ringm)
    s_misc = nc.alloc_semaphore("s_misc")
    misc = [0]

    def fetch(dst, src, after=()):
        pool.wait(*after)
        if misc[0]:
            pool.wait(Mark(s_misc, misc[0]))
        G.dma_start(dst, src).then_inc(s_misc, 16)
        misc[0] += 16
        return Mark(s_misc, misc[0])

    def join():
        return [dve.now(), act.now(), pe.now(), pool.now()]

    const = [tab1]

    def C(name):
        at, n = const[0][name]
        return cst[:, at:at + n]

    def matmul(out, stationary, moving, **kw):
        pe.spend(max(LOAD_US, columns_of(moving) * PE_COLUMN_US))
        return T.matmul(out, stationary, moving, **kw)

    def turn(out, src, ident):
        pe.spend(LOAD_US)
        return T.transpose(out, src, ident)

    def transpose(b, col, src):
        return turn(ps[:, b, col:col + P], src, C("ident"))

    def rsqrt(ap, after=()):
        m = act(S.activation, ap, ap, ACT.Sqrt, after=after)
        return dve(V.reciprocal, ap, ap, after=[m])

    def rms_rows(after, out):
        for i in range(NT):
            m = dve(V.tensor_tensor_reduce, out=out[:, i, :], in0=h[:, i, :], in1=h[:, i, :], scale=1.0 / D,
                    scalar=1e-6, op0=ALU.mult, op1=ALU.add, accum_out=stat[:, i:i + 1], after=after)
        rsqrt(stat[:, 0:NT], after=[m])
        for i in range(NT):
            m = dve(V.tensor_scalar, out[:, i, :], h[:, i, :], stat[:, i:i + 1], None, ALU.mult)
        return m

    def turn_xn(after, mult=None, add=None, after_w=()):
        for i in range(NT):
            for q in range(2):
                pe.wait(*after)
                b = bank.take()
                for k in range(4):
                    t = transpose(b, k * P, xn[:, i, (4 * q + k) * P:(4 * q + k + 1) * P])
                t = pe.mark(t)
                out = xt[:, 4 * q:4 * q + 4, i * P:(i + 1) * P]
                src = bank[b].rearrange("p (k t) -> p k t", k=4)
                if mult is None:
                    m = act(S.copy, out, src, after=[t])
                    bank.give(b, m)
                else:
                    m = dve(V.tensor_tensor, out, src, spread(mult[:, 4 * q:4 * q + 4], 2, P), ALU.mult,
                            after=[t] + list(after_w))
                    bank.give(b, m)
                    if add is not None:
                        m = dve(V.tensor_tensor, out, out, spread(add[:, 4 * q:4 * q + 4], 2, P), ALU.add)
        return m

    def project(z, width, tag, tiles, marks):
        for c in tiles:
            n = min(COLS, width - c * COLS)
            w, loaded = ring.get(f"{tag}{c}")
            w = w[:, 0:KD * n].rearrange("p (k n) -> p k n", k=KD)
            pe.wait(loaded)
            for i in range(NT):
                b = bank.take()
                for k in range(KD):
                    t = matmul(ps[:, b, 0:n], xt[:, k, i * P:(i + 1) * P], w[:, k, :],
                                 start=(k == 0), stop=(k == KD - 1))
                t = pe.mark(t)
                m = act(S.copy, z[:, i, c * COLS:c * COLS + n], ps[:, b, 0:n], after=[t])
                bank.give(b, m)
                if i == NT - 1:
                    ring.release(f"{tag}{c}", t)
                    marks[c] = m
                yield

    def out_project(tag, ready, add):
        pe.wait(ready)
        bs = [bank.take() for _ in range(4)]
        for c in range(3):
            ks = range(3 * c, min(3 * c + 3, KD))
            w, loaded = ring.get(f"{tag}{c}")
            pe.wait(loaded)
            for i in range(NT):
                for q in range(2):
                    for k in ks:
                        t = matmul(ps[:, bs[2 * i + q], :], xt[:, k, i * P:(i + 1) * P],
                                     w[:, (k - 3 * c) * D + q * 512:(k - 3 * c) * D + (q + 1) * 512],
                                     start=(k == 0), stop=(k == KD - 1))
            t = pe.mark(t)
            ring.release(f"{tag}{c}", t)
        for i in range(NT):
            for q in range(2):
                m = add(i, q, bank[bs[2 * i + q]], t)
                bank.give(bs[2 * i + q], m)
        return m

    def head_norm(x, n, width, eps, tmp, st, after=()):
        s1, s2 = st[:, 0:n], st[:, 8:8 + n]
        yield
        dve(V.tensor_reduce, s1, x, AXX, ALU.add, after=after)
        yield
        dve(V.tensor_scalar, s1, s1, 1.0 / width, None, ALU.mult)
        yield
        dve(V.tensor_tensor, x, x, spread(s1, 2, width), ALU.subtract)
        yield
        dve(V.tensor_tensor, tmp, x, x, ALU.mult)
        yield
        dve(V.tensor_reduce, s2, tmp, AXX, ALU.add)
        yield
        m = dve(V.tensor_scalar, s2, s2, 1.0 / width, eps, ALU.mult, ALU.add)
        rsqrt(s2, after=[m])
        yield
        m = dve(V.tensor_tensor, x, x, spread(s2, 2, width), ALU.mult)
        return m

    def rope_tables(pos, inv, n, w, after):
        cos = ang[:, 0:NT * n].rearrange("p (i n) -> p i n", i=NT)
        sin = ang[:, 64:64 + NT * n].rearrange("p (i n) -> p i n", i=NT)
        posf, a, k = w(NT), w(NT, n), w(NT, n)
        dve(V.tensor_copy, posf, pos, after=after)
        dve(V.tensor_tensor, a, spread(posf, 2, n), spread(inv, 1, NT), ALU.mult)
        magic = 1.5 * 2 ** 23
        dve(V.tensor_scalar, k, a, 1.0 / (2 * math.pi), magic, ALU.mult, ALU.add)
        dve(V.tensor_scalar, k, k, magic, None, ALU.subtract)
        c1 = 6.28125
        c2 = float(np.float32(round((2 * math.pi - c1) * 2 ** 19) / 2 ** 19))
        c3 = 2 * math.pi - c1 - c2
        for c in (c1, c2, c3):
            dve(V.scalar_tensor_tensor, out=a, in0=k, scalar=-c, in1=a, op0=ALU.mult, op1=ALU.add)
        m = dve(V.tensor_scalar, a, a, 3.1415925, -3.1415925, ALU.min, ALU.max)
        act(S.activation, sin, a, ACT.Sin, after=[m])
        m = act(S.activation, k, a, ACT.Abs)
        m = dve(V.tensor_scalar, k, k, -1.0, math.pi / 2, ALU.mult, ALU.add, after=[m])
        return cos, sin, act(S.activation, cos, k, ACT.Sin, after=[m])

    def rotate(out, x, heads, half, cos, sin, tmp, after=()):
        c, s = spread(cos, 2, heads), spread(sin, 2, heads)
        x1, x2 = x[:, :, :, 0:half], x[:, :, :, half:2 * half]
        n = NT * heads * half
        ta, tb, tc, td = (tmp[:, e * n:(e + 1) * n].rearrange("p (i h n) -> p i h n", i=NT, h=heads) for e in range(4))
        yield
        dve(V.tensor_tensor, ta, x1, c, ALU.mult, after=after)
        yield
        dve(V.tensor_tensor, tb, x2, s, ALU.mult)
        yield
        dve(V.tensor_tensor, tc, x1, s, ALU.mult)
        yield
        dve(V.tensor_tensor, td, x2, c, ALU.mult)
        yield
        dve(V.tensor_tensor, out[:, :, :, 0:half], ta, tb, ALU.subtract)
        yield
        m = dve(V.tensor_tensor, out[:, :, :, half:2 * half], tc, td, ALU.add)
        return m

    def softmax_rows(sc, heads, st, after=()):
        mx, sm = st[:, 0:heads], st[:, 16:16 + heads]
        n = sc.shape[2]
        yield
        dve(V.tensor_reduce, mx, sc, AXX, ALU.max, after=after)
        yield
        m = dve(V.tensor_tensor, sc, sc, spread(mx, 2, n), ALU.subtract)
        yield
        m = act(S.activation, sc, sc, ACT.Exp, after=[m])
        yield
        dve(V.tensor_reduce, sm, sc, AXX, ALU.add, after=[m])
        yield
        m = dve(V.reciprocal, sm, sm)
        return sm, m

    def weighted_values(pr, heads, ns, pt, value, ready):
        flat = [(m, st) for m in range(heads) for st in range(ns)]
        for g in range(0, len(flat), 4):
            pe.wait(ready)
            while len(bank.order) < 1:
                yield
            b = bank.take()
            for e, (m, st) in enumerate(flat[g:g + 4]):
                t = transpose(b, e * P, pr[:, m, st * P:(st + 1) * P])
            t = pe.mark(t)
            yield
            k = act(S.copy, pt[:, g:g + 4, :], bank[b].rearrange("p (a t) -> p a t", a=4), after=[t])
            bank.give(b, k)
            yield
        pe.wait(k)
        while len(bank.order) < 1:
            yield
        b = bank.take()
        for e, (m, st) in enumerate(flat):
            t = matmul(ps[:, b, m * HD:(m + 1) * HD], pt[:, e, :], value(m, st), start=(st == 0), stop=(st == ns - 1))
        return b, pe.mark(t)

    def stream_blocks(tiles, first_tile, blocks, work_free):
        free0 = [list(f) for f in ring.free]
        loop_base, base = freed[0], list(ring.count)
        for j in range(NSLOT):
            ring.count[j] += 16 * (blocks // NSLOT)
        sp.met = {}
        with nc.Fori(0, blocks // NSLOT, engines=LOADER) as turn:
            loop = Loop(turn, blocks // NSLOT)
            sp.enter(loop, 0)
            for j in range(NSLOT):
                sp.wait(*(free0[j] if j < NWALK else work_free))
                sp.wait(Mark(s_freed, loop_base + j + 1 - NSLOT, loop, NSLOT))
                sp.q.dma_start(ringm[:, j, :], tiles[first_tile + turn * NSLOT + j]).then_inc(ring.sems[j], 16)
            sp.leave()
        return loop_base, base

    def blocks_done(n):
        freed[0] += n
        for j in range(NSLOT):
            ring.free[j] = [Mark(s_freed, freed[0] - (NSLOT - 1 - j))]
        ring.order = list(range(NWALK))

    def ffn_block(loop, j, per_turn, bases, tokens, src, silu, hid, nv, gate, banks_up, acc, accumulate, dve_before):
        freed0, base = bases
        slot = j % NSLOT
        w = ringm[:, slot, :]

        def up():
            loads = 16 * (per_turn // NSLOT)
            pe.wait(Mark(ring.sems[slot], base[slot] + 16 * (j // NSLOT + 1), loop, loads))
            pe.wait(dve_before)
            for half_w in range(2):
                for k in range(KD):
                    at = half_w * D + k * P
                    t = matmul(banks_up[half_w], w[:, at:at + P], src[:, k, :], start=(k == 0), stop=(k == KD - 1))
            return pe.mark(t)

        def gated(t):
            act.wait(dve_before)
            m = act(S.activation, silu[:, j % 2, :], banks_up[0], ACT.Silu, after=[t])
            if gate is not None:
                m = dve(V.tensor_tensor, silu[:, j % 2, :], silu[:, j % 2, :], gate, ALU.mult, after=[m])
            dve.wait(Mark(s_freed, freed0 + j - 1, loop, per_turn))
            return dve(V.tensor_tensor, hid[:, j % 2, :], silu[:, j % 2, :], banks_up[1], ALU.mult, after=[m, t])

        def down(m):
            pe.wait(m)
            for i in range(tokens // P):
                for q in range(2):
                    t = matmul(acc[2 * i + q], hid[:, j % 2, i * P:(i + 1) * P], w[:, 2 * D + q * 512:2 * D + (q + 1) * 512],
                                 start=accumulate == "first", stop=accumulate == "last")
            t.then_inc(s_freed, 1)
            return Mark(s_freed, freed0 + j + 1, loop, per_turn)

        return up, gated, down

    def dense_loop(experts, bases, gate, ready, add):
        fw = Carve(zbuf, NE * SEQ)
        silu, hid = fw(2, SEQ), fw(2, SEQ)
        pe.wait(ready)
        for b in range(4, 8):
            t = matmul(ps[:, b, :], zero[:, 0:P], zero[:, :], start=True, stop=False)
        pe.mark(t)
        half = FB // NSLOT
        nv = 2 if gate is not None else 1
        with nc.Fori(0, experts, engines=WORKERS) as e, nc.Fori(0, half, engines=WORKERS) as c:
            loop = Loop(e * half + c, experts * half)
            pe.enter(loop, NSLOT)
            act.enter(loop, NSLOT)
            dve.enter(loop, nv * NSLOT)
            steps = [ffn_block(loop, j, NSLOT, bases, SEQ, xt, silu, hid, nv, gate[:, e, :] if gate is not None else None,
                               (ps[:, j % 2, 0:SEQ], ps[:, 2 + j % 2, 0:SEQ]), [bank[b] for b in range(4, 8)], "middle",
                               dve.at(nv * (j - 1))) for j in range(NSLOT)]
            m = steps[0][1](steps[0][0]())
            for j in range(NSLOT):
                nxt = steps[j + 1][1](steps[j + 1][0]()) if j + 1 < NSLOT else None
                steps[j][2](m)
                m = nxt
            for q in (pe, act, dve):
                q.leave()
        for b in range(4, 8):
            t = matmul(ps[:, b, :], zero[:, 0:P], zero[:, :], start=False, stop=True)
        t = pe.mark(t)
        for i in range(NT):
            for q in range(2):
                m = add(i, q, bank[4 + 2 * i + q], t)
        return m

    def all_banks():
        for b in range(8):
            pe.wait(*bank.free[b])

    def feed_forward(tiles, first_tile, ready, add):
        assert not ring.plan and not ring.held
        bases = stream_blocks(tiles, first_tile, FB, work_done[0])
        all_banks()
        m = dense_loop(1, bases, None, ready, add)
        blocks_done(FB)
        for b in range(8):
            bank.free[b] = [m, act.now()]
        bank.order = list(range(8))
        return m

    def routed_feed_forward(kept, ready):
        assert not ring.plan and not ring.held
        bases = stream_blocks(d["moe"], 0, NE * FB, work_done[0])
        ex, posx, gatx, count, m = route(kept, ready)
        all_banks()
        for e in (pe, act, dve):
            e.wait(m)
        start = dve.n
        most = nc.values_load(count[0:1, 0:1], engines=WORKERS, min_val=0, max_val=SEQ)
        with nc.If(most <= P):
            for e in (pe, act, dve):
                e.branch("gathered")
            m = gathered_loop(bases, kept, posx, gatx)
            for e in (pe, act, dve):
                e.rejoin()
            m = dve(V.memset, stat[:, 8:9], 0.0, after=[m])
        dve.n = start
        with nc.Else():
            for e in (pe, act, dve):
                e.branch("everywhere")
            gate_all, m = spread_gates(ex)
            m = dense_loop(NE, bases, gate_all, m, add_residual)
            for e in (pe, act, dve):
                e.rejoin()
            m = dve(V.memset, stat[:, 8:9], 0.0, after=[m])
        blocks_done(NE * FB)
        for b in range(8):
            bank.free[b] = [m]
        bank.order = list(range(8))
        for e in (pe, act, sp, pool):
            e.wait(m)

    def gathered_loop(bases, kept, posx, gatx):
        fw = Carve(zbuf)
        xg, ysb = fw(KD, P), fw(D)
        pick, pickg, gT, silu, hid = fw(NT, P), fw(NT, P), fw(NT, P), fw(2, P), fw(2, P)
        slots = C("slots")

        def select(e, out, weighted):
            for i in range(NT):
                if weighted:
                    m = dve(V.tensor_scalar, out[:, i, :], slots, posx[:, e, i:i + 1], gatx[:, e, i:i + 1],
                            ALU.is_equal, ALU.mult)
                else:
                    m = dve(V.tensor_scalar, out[:, i, :], slots, posx[:, e, i:i + 1], None, ALU.is_equal)
            return m

        def gather(m, free):
            pe.wait(m, free)
            for k in range(KD):
                for i in range(NT):
                    t = matmul(ps[:, 4 + k // 4, (k % 4) * P:(k % 4 + 1) * P], xn[:, i, k * P:(k + 1) * P],
                                 pick[:, i, :], start=(i == 0), stop=(i == NT - 1))
            t = pe.mark(t)
            for q in range(2):
                m = dve(V.tensor_tensor, xg[:, 4 * q:4 * q + 4, :], bank[4 + q].rearrange("p (k t) -> p k t", k=4),
                        spread(kept("g_ffn")[:, 4 * q:4 * q + 4], 2, P), ALU.mult, after=[t])
            return m

        def scatter(marks):
            pe.wait(*marks)
            for n, b in enumerate((0, 1, 6, 7)):
                t = matmul(bank[b], gT[:, n // 2, :], ysb[:, (n % 2) * 512:(n % 2 + 1) * 512], start=True, stop=True)
            t = pe.mark(t)
            for n, b in enumerate((0, 1, 6, 7)):
                m = add_residual(n // 2, n % 2, bank[b], t)
            return m

        m = select(0, pick, False)
        gather(m, None)
        with nc.Fori(0, NE, engines=WORKERS) as e:
            loop = Loop(e, NE)
            pe.enter(loop, FB + 3)
            act.enter(loop, FB + 3)
            dve.enter(loop, FB + 10)
            steps = []
            m = select(e, pickg, True)
            weighted = m

            def step(j, before):
                return ffn_block(loop, j, FB, bases, P, xg, silu, hid, 1, None,
                                 (ps[:, j % 2, 0:P], ps[:, j % 2, P:2 * P]), [bank[2], bank[3]],
                                 "first" if j == 0 else "last" if j == FB - 1 else "middle", before)

            prev = [dve.at(0), dve.at(0)]
            cur = step(0, prev[0])
            m = cur[1](cur[0]())
            done = [m]
            turned = None
            for j in range(FB):
                if j + 1 < FB:
                    nxt = step(j + 1, dve.at(0) if j == 0 else done[j - 1])
                    m2 = nxt[1](nxt[0]())
                    done.append(m2)
                if j == 0:
                    pe.wait(act.at(0))
                last = cur[2](m)
                if j == 1:
                    pe.wait(weighted)
                    for i in range(NT):
                        t = transpose(6, i * P, pickg[:, i, :])
                    t = pe.mark(t)
                    turned = act(S.copy, gT, ps[:, 6, 0:2 * P].rearrange("p (i t) -> p i t", i=NT), after=[t])
                if j == 2:
                    picked = select(e + 1, pick, False)
                if j + 1 < FB:
                    cur, m = nxt, m2
            for q in range(2):
                y = act(S.copy, ysb[:, q * 512:(q + 1) * 512], bank[2 + q], after=[last])
            gather(picked, None)
            scatter([y, turned, done[-1]])
            for q in (pe, act, dve):
                q.leave()
        return dve.now()

    def add_residual(i, q, src, t):
        return dve(V.tensor_tensor, h[:, i, q * 512:(q + 1) * 512], h[:, i, q * 512:(q + 1) * 512], src, ALU.add,
                   after=[t])

    s_x = nc.alloc_semaphore("s_x")
    nc.sync.dma_start(h, d["x"]).then_inc(s_x, 16)
    loaded_x = Mark(s_x, 16)
    cols = sb("layer_cols", 2 * 96).rearrange("p (l n) -> p l n", l=2)
    mods = sb("modulation", 2 * 48 + 16 + KD).rearrange("p n -> p n")
    loaded_cols = fetch(cols, d["cols"])
    loaded_const = fetch(cst[:, 0:width1], d["const1"])
    posi = nc.alloc_sbuf_tensor("posi", [P, 2 * NT], I32)[:, :]
    most_i = nc.alloc_sbuf_tensor("most_tokens", [P, 1], I32)[:, :]
    route_mem = sb("routing", 3 * NT * NE + 2 * NT * (NE + 1))
    s_freed = nc.alloc_semaphore("s_freed")
    nc.sync.sem_inc(s_freed, NSLOT)
    freed = [NSLOT]
    work_done = [[]]
    loaded_pos = fetch(posi, d["pos"])
    loaded_c = fetch(mods[:, 112:112 + KD], d["c"])
    dve(V.memset, zero, 0.0)
    pe.wait(dve.now(), loaded_const)
    dve.wait(loaded_x, loaded_cols)
    cact = mods[:, 112:112 + KD]

    small1, n_small1 = spans(SMALL1)
    rows1b, _ = spans(ROWS1B, n_small1)
    rows1, _ = spans(ROWS1)
    small1.update(rows1b)

    def columns(buf, table):
        def get(name):
            at, n = table[name]
            return buf[:, at:at + n]
        return get

    def layer_tiles(l):
        out = []
        for c in range(-(-DIN1 // COLS)):
            n = min(COLS, DIN1 - c * COLS)
            out.append((f"win{c}", [(d["w_in"][l, c, :, 0:KD * n], 0)]))
        small = [("rows", [(d["rows1"][l:l + 1].to_broadcast([P, d["rows1"].shape[1]]), 0)]),
                 ("small", [(d["small1"][l], 0), (d["rows1b"][l:l + 1].to_broadcast([P, d["rows1b"].shape[1]]), n_small1)])]
        out[2:2] = small
        out += [("kc", [(d["kc_w1"][l], 0)]), ("vc", [(d["vc_w1"][l], 0)])]
        out += [(f"ada{c}", [(d["ada"][l, c], 0)]) for c in range(16)]
        out += [(f"wout{c}", [(d["w_out"][l, c], 0)]) for c in range(3)]
        return out

    def ple_tiles(l):
        return [("ple_up", [(d["ple_proj"][l], 0)])] + \
            [(f"pleg{c}", [(d["ple_gate"][l, c, :, 0:KD * min(COLS, D - c * COLS)], 0)]) for c in range(3)]

    def spatial_gating(z, small, tiles, ready):
        while 3 not in tiles:
            yield
        ready = ready + [tiles[3]]
        w, st = Carve(gates_flat), stats(0)
        u, v, tmp, wst = w(NT, 256), w(NT, 256), w(8, 64), w(4, P)
        yield
        act(S.activation, u, z[:, :, ZA:ZA + 256], ACT.Gelu_apprx_tanh, after=ready)
        yield
        m = act(S.activation, v, z[:, :, ZA + 256:ZA + 512], ACT.Gelu_apprx_tanh)
        yield
        dve(V.tensor_tensor, wst, small("wst").rearrange("p (h t) -> p h t", h=4), spread(C("tri"), 1, 4), ALU.mult,
            after=ready)
        yield
        yield from head_norm(v.rearrange("p i (h d) -> p (i h) d", h=4), 8, HD, 1e-5, tmp, st, after=[m])
        yield
        dve(V.tensor_tensor, v, v, spread(small("ln_g"), 1, NT), ALU.mult)
        yield
        m = dve(V.tensor_tensor, v, v, spread(small("ln_b"), 1, NT), ALU.add)
        yield
        pe.wait(m)
        while len(bank.order) < 1:
            yield
        b = bank.take()
        for i in range(NT):
            for hh in range(4):
                t = matmul(ps[:, b, (4 * i + hh) * HD:(4 * i + hh + 1) * HD], wst[:, hh, :],
                             v[:, i, hh * HD:(hh + 1) * HD], start=True, stop=True)
        t = pe.mark(t)
        bs = small("bs")
        mixed = v
        for i in range(NT):
            yield
            m = dve(V.tensor_tensor, mixed[:, i, :].rearrange("p (h d) -> p h d", h=4),
                    bank[b][:, i * 256:(i + 1) * 256].rearrange("p (h d) -> p h d", h=4), spread(bs, 2, HD), ALU.add,
                    after=[t])
        bank.give(b, m)
        yield
        marks["gating"] = dve(V.tensor_tensor, xn[:, :, 0:256], u, mixed, ALU.mult)

    def sparse_attention(z, small, tiles, ready, w):
        Z = 1536
        while 7 not in tiles:
            yield
        ready = ready + [tiles[c] for c in (4, 5, 6, 7)]
        st = stats(1)
        q = z[:, :, Z:Z + 512]
        tmp = w(512)
        qT, qrT, kT = w(NT, 4, P), w(NT, 4, P), w(2, SEQ)
        gt = w(NT, 24)
        mark1 = w.at
        oacc = xn[:, :, 512:1024]
        yield
        act(S.activation, gt, z[:, :, Z + 1280:Z + 1304], ACT.Sigmoid, after=ready)
        heads = lambda ap, n: ap.rearrange("p i (h d) -> p i h d", h=n)

        def turn_queries(dst, dep):
            pe.wait(*dep)
            for i in range(NT):
                while len(bank.order) < 1:
                    yield
                b = bank.take()
                for j in range(4):
                    t = transpose(b, j * P, q[:, i, j * P:(j + 1) * P])
                t = pe.mark(t)
                yield
                m = act(S.mul, dst[:, i], bank[b].rearrange("p (j t) -> p j t", j=4), HD ** -0.5, after=[t])
                bank.give(b, m)
            return t, m

        raw, _ = yield from turn_queries(qT, ready)
        yield
        for at in (Z + 768, Z + 1024):
            k2_ = heads(z[:, :, at:at + P], 2)
            r = yield from rotate(k2_, k2_, 2, 8, cos, sin, tmp, after=ready + [rope_ready])
            yield
        pe.wait(r)
        while len(bank.order) < 1:
            yield
        b = bank.take()
        for ty in range(2):
            for i in range(NT):
                t = transpose(b, (2 * ty + i) * P, z[:, i, Z + 768 + 256 * ty:Z + 896 + 256 * ty])
        t = pe.mark(t)
        yield
        m = act(S.copy, kT, bank[b].rearrange("p (a t) -> p a t", a=2), after=[t])
        bank.give(b, m)
        r = yield from rotate(heads(q, 8), heads(q, 8), 8, 8, cos, sin, tmp, after=[raw])
        yield
        _, turned = yield from turn_queries(qrT, [r])
        yield

        dup, x2 = w(NT, 4, 2, HD), w(4, SEQ)
        blk = w(4, 16, 15)
        hidden, hrep, kcT, vbd = w(2, 30), w(4, 32), w(16), w(4, HD)
        for i in range(NT):
            yield
            m = dve(V.tensor_copy, dup[:, i], spread(z[:, i, Z + 512:Z + 768].rearrange("p (a d) -> p a d", a=4), 2, 2))
        yield
        dve(V.memset, hrep, 0.0)
        yield
        dve(V.memset, vbd, 0.0)
        for i in range(NT):
            pe.wait(m)
            while len(bank.order) < 1:
                yield
            b = bank.take()
            for a in range(4):
                t = transpose(b, a * P, dup[:, i, a].rearrange("p b d -> p (b d)"))
            t = pe.mark(t)
            src = bank[b].rearrange("p (a t) -> p a t", a=4)
            yield
            act(S.copy, x2[0:64, :, i * P:(i + 1) * P], src[0:64], after=[t])
            lo = 1 if i == 0 else 0
            yield
            k = act(S.copy, x2[64:128, :, i * P + lo - 1:(i + 1) * P - 1], src[64:128, :, lo:P])
            bank.give(b, k)
            yield
        dve.wait(k)
        for a in range(4):
            for hh in range(2):
                yield
                m = dve(V.tensor_tensor, blk[:, a, 8 * hh:8 * hh + 8, :],
                        x2[:, a, 16 * hh:16 * hh + 240].rearrange("p (n l b) -> p b l n", l=8, b=2)[:, 0],
                        spread(small("pos")[:, 8 * hh:8 * hh + 8], 2, 15), ALU.add)
        while "kc" not in ring.held or "vc" not in ring.held:
            yield
        pe.wait(m)
        while len(bank.order) < 1:
            yield
        b = bank.take()
        for kv, tag in ((0, "kc"), (1, "vc")):
            w1, loaded = ring.get(tag)
            pe.wait(loaded)
            for l in range(16):
                t = matmul(ps[:, b, 32 * kv:32 * kv + 30], w1[:, l * P:(l + 1) * P], blk[:, 2 * kv:2 * kv + 2, l, :],
                             start=(l == 0), stop=(l == 15))
            t = pe.mark(t)
            ring.release(tag, t)
        yield
        m = act(S.activation, hidden, ps[:, b, 0:64].rearrange("p (v n) -> p v n", v=2)[:, :, 0:30], ACT.Gelu_apprx_tanh,
                after=[t])
        bank.give(b, m)
        yield
        m2 = dve(V.tensor_copy, hrep.rearrange("p (a g) n -> p a g n", g=2)[:, :, :, 0:15],
                 spread(hidden[:, 1, :].rearrange("p (g n) -> p g n", g=2), 1, 2), after=[m])
        pe.wait(m, m2)
        while len(bank.order) < 1:
            yield
        b = bank.take()
        for g in range(2):
            matmul(ps[64 * g:64 * g + 64, b, 0:15], small("kc_w2"), hidden[:, 0, 15 * g:15 * g + 15], start=True, stop=True)
        t = pe.mark(matmul(ps[:, b, 64:128], hrep.rearrange("p a n -> p (a n)"), small("vc_w2"), start=True, stop=True))
        yield
        act(S.copy, kcT[:, 0:15], ps[:, b, 0:15], after=[t])
        for a in range(4):
            yield
            k = act(S.copy, vbd[32 * a:32 * a + 32, a, :], ps[32 * a:32 * a + 32, b, 64:128])
        bank.give(b, k)
        yield
        sc, pct = w(NT * 8, 32), w(4, P)
        yield
        m = dve(V.memset, sc, 0.0)
        scv = sc.rearrange("p (i m) n -> p i m n", i=NT)
        neg = C("cmpneg").rearrange("p (i n) -> p i n", i=NT)
        pe.wait(k, turned)
        for i in range(NT):
            for g in range(2):
                while len(bank.order) < 1:
                    yield
                b = bank.take()
                for j in range(4):
                    t = matmul(ps[:, b, 16 * j:16 * j + 15], qT[64 * g:64 * g + 64, i, j, :],
                                 kcT[64 * g:64 * g + 64, 0:15], start=True, stop=True)
                t = pe.mark(t)
                yield
                m = dve(V.tensor_tensor, scv[:, i].rearrange("p (j g) n -> p j g n", g=2)[:, :, g, 0:15],
                        ps[:, b, 0:64].rearrange("p (j n) -> p j n", j=4)[:, :, 0:15], spread(neg[:, i], 1, 4), ALU.add,
                        after=[t])
                bank.give(b, m)
        yield
        rs, m = yield from softmax_rows(sc[:, :, 0:15], NT * 8, st)
        yield
        dve(V.tensor_tensor, sc[:, :, 0:15], sc[:, :, 0:15], spread(rs, 2, 15), ALU.mult)
        for i in range(NT):
            yield
            m = dve(V.tensor_tensor, scv[:, i, :, 0:15], scv[:, i, :, 0:15],
                    spread(C("cmp01").rearrange("p (i n) -> p i n", i=NT)[:, i], 1, 8), ALU.mult)
        yield
        pe.wait(m)
        while len(bank.order) < 1:
            yield
        b = bank.take()
        for e in range(4):
            t = transpose(b, e * P, sc[:, 4 * e:4 * e + 4, :].rearrange("p m n -> p (m n)"))
        t = pe.mark(t)
        yield
        m = act(S.copy, pct, bank[b].rearrange("p (a t) -> p a t", a=4), after=[t])
        bank.give(b, m)
        yield
        pe.wait(m)
        for i in range(NT):
            while len(bank.order) < 1:
                yield
            b = bank.take()
            for c in range(2):
                t = matmul(ps[:, b, 256 * c:256 * c + 256], pct[:, 2 * i + c, :], vbd.rearrange("p a d -> p (a d)"),
                             start=True, stop=True)
            t = pe.mark(t)
            yield
            m = dve(V.tensor_tensor, oacc[:, i, :].rearrange("p (m d) -> p m d", m=8),
                    bank[b].rearrange("p (m d) -> p m d", m=8), spread(gt[:, i, 0:8], 2, HD), ALU.mult, after=[t])
            bank.give(b, m)
        compressed = [m, act.now(), pe.now()]
        yield

        w.at = mark1
        sbuf, pt = w(8 * 256), w(16, P)
        for ty in range(2):
            vat = Z + 896 + 256 * ty
            for i in range(NT):
                n = P * (i + 1)
                s8 = sbuf[:, 0:8 * n].rearrange("p (m s) -> p m s", m=8)
                s8g = s8.rearrange("p (j g) s -> p j g s", g=2)
                mask = C("causal")[:, P * i:P * i + n]
                dve.wait(*compressed)
                act.wait(*compressed)
                per = 512 // n
                for g in range(2):
                    for j0 in range(0, 4, per):
                        while len(bank.order) < 1:
                            yield
                        b = bank.take()
                        for j in range(j0, j0 + per):
                            t = matmul(ps[:, b, (j - j0) * n:(j - j0 + 1) * n], qrT[64 * g:64 * g + 64, i, j, :],
                                         kT[64 * g:64 * g + 64, ty, 0:n], start=True, stop=True)
                        t = pe.mark(t)
                        yield
                        m = dve(V.tensor_tensor, s8g[:, j0:j0 + per, g, :],
                                bank[b].rearrange("p (j s) -> p j s", j=per), spread(mask, 1, per), ALU.add, after=[t])
                        bank.give(b, m)
                        yield
                rs, m = yield from softmax_rows(s8, 8, st)
                yield
                b, t = yield from weighted_values(s8, 8, i + 1, pt[:, 0:8 * (i + 1), :],
                                       lambda mm, st: z[:, st, vat + (mm % 2) * HD:vat + (mm % 2 + 1) * HD], m)
                yield
                dve(V.tensor_tensor, rs, rs, gt[:, i, 8 * (ty + 1):8 * (ty + 2)], ALU.mult)
                o = tmp[:, 0:512].rearrange("p (m d) -> p m d", m=8)
                yield
                m = dve(V.tensor_tensor, o, bank[b].rearrange("p (m d) -> p m d", m=8), spread(rs, 2, HD), ALU.mult,
                        after=[t])
                bank.give(b, m)
                dst = oacc[:, i, :]
                yield
                m = dve(V.tensor_tensor, dst, oacc[:, i, :], tmp[:, 0:512], ALU.add)
                compressed = [m]
                yield
        marks["attention"] = m

    def time_mix(z, small, rows, tiles, ready, w):
        st = stats(2)
        zb = z[:, :, 0:1024]
        zm, gg, k2 = w(NT, 1024), w(NT, 256), w(NT, 256)
        keep = w(NT, 4, 256)
        pr, qT, hT = w(2, NT, 2, P), w(2, SEQ), w(2, SEQ)
        wc, st_e = w(2, 4), w(2, 2, HD)
        state = w(4, 2, HD)
        y = w(NT, 256)
        gT, st_f = qT, hT.rearrange("p a t -> p (a t)").rearrange("p (a c d) -> p a c d", a=2, c=4)
        pr_flat = pr.rearrange("p a i e t -> p (a i e t)")
        lo, loT = (pr_flat[:, 512 * e:512 * e + 512].rearrange("p (a t) -> p a t", a=2) for e in range(2))
        gnat, t2 = lo, loT
        shared = w.at
        tmp = w(NT, 256)
        wa, kk, lw, wi, wx, wn = w(NT, 512), w(NT, 256), w(NT, 256), w(NT, 256), w(NT, 256), w(NT, 256)
        for i in range(NT):
            for c in range(2):
                cols = slice(512 * c, 512 * c + 512)
                pe.wait(*ready)
                while len(bank.order) < 1:
                    yield
                b = bank.take()
                t = matmul(bank[b], C("shift"), zb[:, i, cols], start=True, stop=(i == 0))
                if i:
                    t = matmul(bank[b], C("carry"), zb[:, i - 1, cols], start=False, stop=True)
                t = pe.mark(t)
                o = zm[:, i, cols]
                yield
                m = dve(V.tensor_tensor, o, bank[b], zb[:, i, cols], ALU.subtract, after=[t] + ready)
                bank.give(b, m)
                yield
                dve(V.tensor_tensor, o, o, rows("mu")[:, cols], ALU.mult)
                yield
                m = dve(V.tensor_tensor, o, o, zb[:, i, cols], ALU.add)
                yield
        r, k, v = zm[:, :, 0:256], zm[:, :, 256:512], zm[:, :, 512:768]
        yield
        act(S.activation, lo[:, :, 0:64], zm[:, :, 768:832], ACT.Tanh, after=[m])
        yield
        act(S.copy, lo[:, :, 64:128], zm[:, :, 832:896])
        yield
        m = act(S.activation, lo[:, :, 128:256], zm[:, :, 896:1024], ACT.Sigmoid)
        pe.wait(m)
        while len(bank.order) < 1:
            yield
        b = bank.take()
        for c in range(2):
            for i in range(NT):
                t = transpose(b, (2 * c + i) * P, lo[:, i, c * P:(c + 1) * P])
        t = pe.mark(t)
        yield
        m = act(S.copy, loT, bank[b].rearrange("p (c t) -> p c t", c=2), after=[t])
        bank.give(b, m)
        yield
        pe.wait(m)
        for i in range(NT):
            while len(bank.order) < 1:
                yield
            b = bank.take()
            t = pe.mark(matmul(bank[b], loT[:, 0, i * P:(i + 1) * P], small("lora"), start=True, stop=True))
            yield
            m = dve(V.tensor_tensor, wa[:, i, :], bank[b], rows("wa0"), ALU.add, after=[t])
            bank.give(b, m)
        while len(bank.order) < 1:
            yield
        b = bank.take()
        for i in range(NT):
            t = matmul(ps[:, b, 256 * i:256 * i + 256], loT[:, 1, i * P:(i + 1) * P], small("g_up"), start=True, stop=True)
        t = pe.mark(t)
        yield
        act(S.activation, wa, wa, ACT.Sigmoid, after=[m])
        yield
        m = act(S.copy, gg, bank[b].rearrange("p (i n) -> p i n", i=NT), after=[t])
        bank.give(b, m)
        yield
        a = wa[:, :, 256:512]
        yield
        lwr = dve(V.tensor_scalar, lw, wa[:, :, 0:256], -math.exp(-0.5), None, ALU.mult, after=[m])
        yield
        dve(V.tensor_tensor, kk, k, spread(rows("k_k"), 1, NT), ALU.mult)
        yield
        dve(V.tensor_tensor, tmp, kk, kk, ALU.mult)
        per_head = lambda ap: ap.rearrange("p i (h d) -> p (i h) d", h=4)
        ss = st[:, 16:24]
        yield
        dve(V.tensor_reduce, ss, per_head(tmp), AXX, ALU.add)
        yield
        m = dve(V.tensor_scalar, ss, ss, 1e-24, None, ALU.max)
        rsqrt(ss, after=[m])
        yield
        dve(V.tensor_tensor, per_head(kk), per_head(kk), spread(ss, 2, HD), ALU.mult)
        yield
        dve(V.tensor_scalar, tmp, a, -1.0, None, ALU.add)
        yield
        dve(V.tensor_tensor, tmp, tmp, spread(rows("k_a"), 1, NT), ALU.mult)
        yield
        dve(V.tensor_scalar, tmp, tmp, 1.0, None, ALU.add)
        yield
        dve(V.tensor_tensor, k2, k, tmp, ALU.mult)
        yield
        pe.wait(lwr)
        while len(bank.order) < 1:
            yield
        b = bank.take()
        for i in range(NT):
            t = matmul(ps[:, b, 256 * i:256 * i + 256], C("tri64"), lw[:, i, :], start=True, stop=True)
        t = pe.mark(t)
        cum = bank[b].rearrange("p (i n) -> p i n", i=NT)
        yield
        m = dve(V.tensor_tensor, wx, cum, lw, ALU.subtract, after=[t])
        yield
        act(S.activation, wi, cum, ACT.Exp, after=[m])
        yield
        k_ = act(S.activation, wn, cum, ACT.Exp, scale=-1.0)
        bank.give(b, m, k_)
        yield
        m = act(S.activation, wx, wx, ACT.Exp, after=[m])
        yield
        while len(bank.order) < 1:
            yield
        b = bank.take()
        for pair in range(2):
            for i in range(NT):
                t = matmul(ps[:, b, 4 * pair + 2 * i:4 * pair + 2 * i + 2], lw[:, i, pair * P:(pair + 1) * P], C("half"),
                             start=True, stop=True)
        t = pe.mark(t)
        yield
        k_ = act(S.activation, wc, ps[:, b, 0:8].rearrange("p (a c) -> p a c", a=2), ACT.Exp, after=[t])
        bank.give(b, k_)
        kp, kq, kh, kr = (keep[:, :, e, :] for e in range(4))
        yield
        dve(V.tensor_tensor, kp, wx, kk, ALU.mult, after=[m])
        yield
        dve(V.tensor_tensor, tmp, kk, a, ALU.mult)
        yield
        dve(V.tensor_tensor, kq, tmp, wn, ALU.mult)
        yield
        dve(V.tensor_tensor, kh, k2, wn, ALU.mult)
        yield
        m = dve(V.tensor_tensor, kr, r, wi, ALU.mult)
        ended = m
        yield
        pe.wait(m)
        for src, dst in ((kp, pr[:, :, :, 0, :]), (kr, pr[:, :, :, 1, :]), (kq, qT.rearrange("p a (i t) -> p a i t", i=NT)),
                         (kh, hT.rearrange("p a (i t) -> p a i t", i=NT))):
            while len(bank.order) < 1:
                yield
            b = bank.take()
            for pair in range(2):
                for i in range(NT):
                    t = transpose(b, (2 * pair + i) * P, src[:, i, pair * P:(pair + 1) * P])
            t = pe.mark(t)
            yield
            m = act(S.copy, dst, bank[b].rearrange("p (a i t) -> p a i t", a=2, i=NT), after=[t])
            bank.give(b, m)
            yield
        w.at = shared
        prod = w(8, 4, P)
        reused = [ended, pe.now(), act.now()]
        pe.wait(m)
        dve.wait(*reused)
        for i in range(NT):
            for hh in range(4):
                lo_p = 64 * (hh % 2)
                rhs = pr[lo_p:lo_p + 64, hh // 2, i].rearrange("p a t -> p (a t)")
                while len(bank.order) < 1:
                    yield
                b = bank.take()
                for e, src in enumerate((qT, hT)):
                    t = matmul(ps[:, b, 256 * e:256 * e + 256], src[lo_p:lo_p + 64, hh // 2, i * P:(i + 1) * P], rhs,
                                 start=True, stop=True)
                t = pe.mark(t)
                yield
                m = dve(V.tensor_tensor, prod[:, 4 * i + hh], bank[b].rearrange("p (e t) -> p e t", e=4),
                        C("mask4").rearrange("p (e t) -> p e t", e=4), ALU.mult, after=[t])
                bank.give(b, m)
                yield
        while len(tiles) < 8 or "gating" not in marks:
            yield
        xc, gc = Carve(xt_flat), Carve(gates_flat)
        xinv, xinvT, lev, cx = xc(8, P), xc(8, P), gc(8, P), gc(8, P)
        idb = spread(C("ident"), 1, 8)
        lvl = C("levels").rearrange("p (l t) -> p l t", l=6)
        yield
        dve(V.tensor_tensor, lev, prod[:, :, 0, :], spread(lvl[:, 0, :], 1, 8), ALU.mult,
            after=[tiles[7], marks["gating"], pe.now()])
        yield
        m = dve(V.tensor_tensor, xinvT, idb, lev, ALU.subtract)
        pe.wait(m)
        for g in range(2):
            while len(bank.order) < 1:
                yield
            b = bank.take()
            for e in range(4):
                t = transpose(b, e * P, xinvT[:, 4 * g + e, :])
            t = pe.mark(t)
            yield
            m = act(S.copy, xinv[:, 4 * g:4 * g + 4, :], bank[b].rearrange("p (e t) -> p e t", e=4), after=[t, m])
            bank.give(b, m)
        pe.wait(m)
        dve.wait(m)
        for l in range(1, 6):
            yield
            m = dve(V.tensor_tensor, lev, prod[:, :, 0, :], spread(lvl[:, l, :], 1, 8), ALU.mult)
            yield
            pe.wait(m)
            for g in range(2):
                while len(bank.order) < 1:
                    yield
                b = bank.take()
                for e in range(4):
                    t = matmul(ps[:, b, e * P:(e + 1) * P], lev[:, 4 * g + e, :], xinv[:, 4 * g + e, :], start=True, stop=True)
                t = pe.mark(t)
                yield
                k_ = act(S.copy, cx[:, 4 * g:4 * g + 4, :], bank[b].rearrange("p (e t) -> p e t", e=4), after=[t])
                bank.give(b, k_)
            yield
            pe.wait(k_)
            for g in range(2):
                while len(bank.order) < 2:
                    yield
                b1, b2 = bank.take(), bank.take()
                for e in range(4):
                    matmul(ps[:, b1, e * P:(e + 1) * P], xinvT[:, 4 * g + e, :], cx[:, 4 * g + e, :], start=True, stop=True)
                    t = matmul(ps[:, b2, e * P:(e + 1) * P], cx[:, 4 * g + e, :], xinvT[:, 4 * g + e, :], start=True, stop=True)
                t = pe.mark(t)
                for b, dst in ((b1, xinv), (b2, xinvT)):
                    yield
                    m = dve(V.tensor_tensor, dst[:, 4 * g:4 * g + 4, :], dst[:, 4 * g:4 * g + 4, :],
                            bank[b].rearrange("p (e t) -> p e t", e=4), ALU.subtract, after=[t])
                    bank.give(b, m)
                yield
        np_, utp, yg = xinv, lev, cx
        pe.wait(m)
        while len(bank.order) < 1:
            yield
        b = bank.take()
        for e in range(8):
            i, hh = divmod(e, 4)
            t = matmul(ps[:, b, e * HD:(e + 1) * HD], prod[:, e, 2, :], v[:, i, hh * HD:(hh + 1) * HD], start=True, stop=True)
        t = pe.mark(t)
        yield
        m = dve(V.tensor_copy, np_[:, :, 0:HD], bank[b].rearrange("p (e d) -> p e d", e=8), after=[t])
        bank.give(b, m)
        for i in range(NT):
            yield
            m = dve(V.tensor_copy, np_[:, 4 * i:4 * i + 4, HD:P], kp[:, i, :].rearrange("p (h d) -> p h d", h=4))
        yield
        pe.wait(m)
        for g in range(2):
            while len(bank.order) < 1:
                yield
            b = bank.take()
            for e in range(4):
                t = matmul(ps[:, b, e * P:(e + 1) * P], xinvT[:, 4 * g + e, :], np_[:, 4 * g + e, :], start=True, stop=True)
            t = pe.mark(t)
            yield
            m = dve(V.tensor_scalar, utp[:, 4 * g:4 * g + 4, :], bank[b].rearrange("p (e t) -> p e t", e=4), -1.0, None,
                    ALU.mult, after=[t])
            bank.give(b, m)
        yield
        pe.wait(m)
        for g in range(2):
            while len(bank.order) < 1:
                yield
            b = bank.take()
            for e in range(4):
                m3 = prod[:, 4 * g + e, 1, :]
                matmul(ps[:, b, e * P:e * P + HD], m3, utp[:, 4 * g + e, 0:HD], start=True, stop=False)
                matmul(ps[:, b, e * P:e * P + HD], prod[:, 4 * g + e, 3, :], v[:, g, e * HD:(e + 1) * HD],
                         start=False, stop=True)
                t = matmul(ps[:, b, e * P + HD:(e + 1) * P], m3, utp[:, 4 * g + e, HD:P], start=True, stop=True)
            t = pe.mark(t)
            src = bank[b].rearrange("p (e t) -> p e t", e=4)
            yield
            dve(V.tensor_copy, y[:, g, :].rearrange("p (h d) -> p h d", h=4), src[:, :, 0:HD], after=[t])
            yield
            m = dve(V.tensor_tensor, yg[:, 4 * g:4 * g + 4, 0:HD], src[:, :, HD:P],
                    kr[:, g, :].rearrange("p (h d) -> p h d", h=4), ALU.add)
            bank.give(b, m)
        pe.wait(m)
        yield
        for i in range(NT):
            yield
            m = dve(V.tensor_copy, gnat[:, i, :].rearrange("p (h d) -> p h d", h=4), yg[:, 4 * i:4 * i + 4, 0:HD])
        pe.wait(m)
        while len(bank.order) < 1:
            yield
        b = bank.take()
        for pair in range(2):
            for i in range(NT):
                t = transpose(b, (2 * pair + i) * P, gnat[:, i, pair * P:(pair + 1) * P])
        t = pe.mark(t)
        yield
        m = act(S.copy, gT, bank[b].rearrange("p (a t) -> p a t", a=2), after=[t])
        bank.give(b, m)
        yield
        while len(bank.order) < 2:
            yield
        fb = [bank.take(), bank.take()]
        while len(bank.order) < 2:
            yield
        eb = [bank.take(), bank.take()]
        for c in range(3):
            i, lo_t = c // 2, 64 * (c % 2)
            rows_c = slice(lo_t, lo_t + 64)
            for hh in range(4):
                e, lo_p = 4 * i + hh, 64 * (hh % 2)
                out = ps[lo_p:lo_p + 64, fb[c % 2], (2 * i + hh // 2) * HD:(2 * i + hh // 2 + 1) * HD]
                hc = slice(hh * HD, (hh + 1) * HD)
                matmul(out, kq[rows_c, i, hc], utp[rows_c, e, 0:HD], start=True, stop=False)
                t = matmul(out, kh[rows_c, i, hc], v[rows_c, i, hc], start=False, stop=True)
        for c in (1, 2):
            i, lo_t = c // 2, 64 * (c % 2)
            rows_c = slice(lo_t, lo_t + 64)
            for hh in range(4):
                e, lo_p = 4 * i + hh, 64 * (hh % 2)
                t = matmul(ps[lo_p:lo_p + 64, eb[c % 2], (hh // 2) * HD:(hh // 2 + 1) * HD],
                             utp[rows_c, e, HD:P], kq[rows_c, i, hh * HD:(hh + 1) * HD], start=True, stop=True)
        t = pe.mark(t)
        for c in range(3):
            yield
            m = dve(V.tensor_copy, st_f[:, :, c, :],
                    ps[:, fb[c % 2], 128 * (c // 2):128 * (c // 2) + 128].rearrange("p (a d) -> p a d", a=2), after=[t])
        for c in (1, 2):
            yield
            k_ = [dve(V.tensor_tensor, st_e[lo_p:lo_p + 64, c - 1], ps[lo_p:lo_p + 64, eb[c % 2], 0:128]
                      .rearrange("p (a d) -> p a d", a=2), spread(C("ident")[lo_p:lo_p + 64, lo_p:lo_p + 64], 1, 2), ALU.add)
                  for lo_p in (0, 64)][-1]
        for b in fb + eb:
            bank.give(b, k_)
        yield
        for pair in range(2):
            yield
            m = dve(V.tensor_scalar, state[:, 1, pair, :], st_f[:, pair, 0, :], wc[:, pair, 0:1], None, ALU.mult)
        for c in (1, 2):
            pe.wait(m)
            while len(bank.order) < 2:
                yield
            sbk = [bank.take(), bank.take()]
            for hh in range(4):
                lo_p = 64 * (hh % 2)
                t = matmul(ps[lo_p:lo_p + 64, sbk[hh % 2], (hh // 2) * HD:(hh // 2 + 1) * HD],
                             st_e[lo_p:lo_p + 64, c - 1, hh // 2, :], state[lo_p:lo_p + 64, c, hh // 2, :],
                             start=True, stop=True)
            t = pe.mark(t)
            for par in range(2):
                lo_p = 64 * par
                yield
                m = dve(V.tensor_tensor, state[lo_p:lo_p + 64, c + 1],
                        ps[lo_p:lo_p + 64, sbk[par], 0:128].rearrange("p (a d) -> p a d", a=2),
                        st_f[lo_p:lo_p + 64, :, c, :], ALU.add, after=[t])
                bank.give(sbk[par], m)
            for pair in range(2):
                yield
                m = dve(V.tensor_scalar, state[:, c + 1, pair, :], state[:, c + 1, pair, :], wc[:, pair, c:c + 1], None,
                        ALU.mult)
            yield
        pe.wait(m)
        while len(bank.order) < 2:
            yield
        yb = [bank.take(), bank.take()]
        for c in (1, 2, 3):
            lo_t = 64 * (c % 2)
            for hh in range(4):
                lo_p = 64 * (hh % 2)
                t = matmul(ps[lo_t:lo_t + 64, yb[hh % 2], (2 * (c // 2) + hh // 2) * HD:(2 * (c // 2) + hh // 2 + 1) * HD],
                             gT[lo_p:lo_p + 64, hh // 2, 64 * c:64 * c + 64], state[lo_p:lo_p + 64, c, hh // 2, :],
                             start=True, stop=True)
        t = pe.mark(t)
        yv = y.rearrange("p i (a b d) -> p i a b d", a=2, b=2)
        for par in range(2):
            src = ps[:, yb[par], 0:256].rearrange("p (i a d) -> p i a d", i=2, a=2)
            yield
            dve(V.tensor_tensor, yv[64:128, 0, :, par, :], yv[64:128, 0, :, par, :], src[64:128, 0], ALU.add, after=[t])
            yield
            m = dve(V.tensor_tensor, yv[:, 1, :, par, :], yv[:, 1, :, par, :], src[:, 1], ALU.add)
            bank.give(yb[par], m)
        yield
        t1 = gnat
        yield from head_norm(per_head(y), 8, HD, 64e-5, per_head(t1), st, after=[pe.now(), act.now()])
        yield
        dve(V.tensor_tensor, y, y, spread(rows("gn_g"), 1, NT), ALU.mult)
        yield
        dve(V.tensor_tensor, y, y, spread(rows("gn_b"), 1, NT), ALU.add)
        yield
        dve(V.tensor_tensor, t1, r, k2, ALU.mult)
        yield
        dve(V.tensor_tensor, t1, t1, spread(rows("r_k"), 1, NT), ALU.mult)
        yield
        dve(V.tensor_reduce, ss, per_head(t1), AXX, ALU.add)
        for i in range(NT):
            yield
            dve(V.tensor_tensor, t2[:, i, :].rearrange("p (h d) -> p h d", h=4),
                v[:, i, :].rearrange("p (h d) -> p h d", h=4), spread(ss[:, 4 * i:4 * i + 4], 2, HD), ALU.mult)
        yield
        dve(V.tensor_tensor, y, y, t2, ALU.add)
        yield
        dve(V.tensor_tensor, xn[:, :, 256:512], y, gg, ALU.mult)

    def route(small, ready):
        lw = Carve(route_mem)
        L, ex, sel, posx, gatx = lw(NT, NE), lw(NT, NE), lw(NT, NE), lw(NE + 1, NT), lw(NE + 1, NT)
        ww = Carve(zbuf)
        gt, eq = ww(NE, NE), ww(NE, NE)
        pe.wait(ready)
        b = bank.take()
        router = small("router").rearrange("p (k e) -> p k e", k=KD)
        for i in range(NT):
            for k in range(KD):
                t = matmul(ps[:, b, NE * i:NE * i + NE], xt[:, k, i * P:(i + 1) * P], router[:, k, :],
                             start=(k == 0), stop=(k == KD - 1))
        t = pe.mark(t)
        m = dve(V.tensor_tensor, L, ps[:, b, 0:NT * NE].rearrange("p (i e) -> p i e", i=NT), spread(small("rb"), 1, NT),
                ALU.add, after=[t])
        bank.give(b, m)
        for i in range(NT):
            other, own = spread(L[:, i, :], 1, NE), spread(L[:, i, :], 2, NE)
            dve(V.tensor_tensor, gt, other, own, ALU.is_gt)
            dve(V.tensor_tensor, eq, other, own, ALU.is_equal)
            dve(V.tensor_tensor, eq, eq, C("before").rearrange("p (e j) -> p e j", e=NE), ALU.mult)
            dve(V.tensor_tensor, gt, gt, eq, ALU.add)
            dve(V.tensor_reduce, sel[:, i, :], gt, AXX, ALU.add)
        selected = dve(V.tensor_scalar, sel, sel, 1.5, None, ALU.is_lt)
        sm = stat[:, 48:48 + NT]
        dve(V.tensor_reduce, sm, L, AXX, ALU.max)
        m = dve(V.tensor_tensor, ex, L, spread(sm, 2, NE), ALU.subtract)
        m = act(S.activation, ex, ex, ACT.Exp, after=[m])
        dve(V.tensor_tensor, ex, ex, sel, ALU.mult, after=[m])
        dve(V.tensor_reduce, sm, ex, AXX, ALU.add)
        dve(V.reciprocal, sm, sm)
        dve(V.tensor_tensor, ex, ex, spread(sm, 2, NE), ALU.mult)
        dve(V.memset, posx, -1.0)
        dve(V.memset, gatx, 0.0)
        pe.wait(selected)
        b = bank.take()
        matmul(ps[:, b, 0:NE], C("tri"), sel[:, 0, :], start=True, stop=True)
        matmul(ps[:, b, NE:2 * NE], C("tri"), sel[:, 1, :], start=True, stop=False)
        matmul(ps[:, b, NE:2 * NE], C("ones"), sel[:, 0, :], start=False, stop=True)
        matmul(ps[:, b, 2 * NE:3 * NE], C("ones"), sel[:, 0, :], start=True, stop=False)
        t = pe.mark(matmul(ps[:, b, 2 * NE:3 * NE], C("ones"), sel[:, 1, :], start=False, stop=True))
        counts = ps[:, b, 0:2 * NE].rearrange("p (i e) -> p i e", i=NT)
        dve(V.tensor_copy, gatx.rearrange("p e i -> p i e")[:, :, 0:NE], ex)
        pv = posx.rearrange("p e i -> p i e")[:, :, 0:NE]
        dve(V.tensor_tensor, pv, counts, sel, ALU.mult, after=[t])
        dve(V.tensor_scalar, pv, pv, -1.0, None, ALU.add)
        dve(V.tensor_reduce, sm[:, 0:1], ps[:, b, 2 * NE:3 * NE], AXX, ALU.max)
        m = dve(V.tensor_copy, most_i, sm[:, 0:1])
        bank.give(b, m)
        return ex, posx, gatx, most_i, m

    def spread_gates(ex):
        gate_all = zbuf[:, 0:NE * SEQ].rearrange("p (e t) -> p e t", e=NE)
        rep = xn.rearrange("p i n -> p (i n)").rearrange("p (i e t) -> p i e t", i=NT, e=NE)
        for i in range(NT):
            m = dve(V.tensor_copy, rep[:, i], spread(ex[:, i, :], 2, P))
        for n, (i, e0) in enumerate((i, e0) for i in range(NT) for e0 in (0, 4)):
            pe.wait(m)
            for e in range(4):
                t = matmul(ps[:, n, e * P:(e + 1) * P], rep[:, i, e0 + e, :], C("ident"), start=True, stop=True)
            t = pe.mark(t)
            k = dve(V.tensor_copy, gate_all[:, e0:e0 + 4, i * P:(i + 1) * P],
                    bank[n].rearrange("p (e t) -> p e t", e=4), after=[t])
        return gate_all, k

    def modulation(l, w):
        acc = w(2, COLS)
        while len(bank.order) < 1:
            yield
        bm = bank.take()
        read = [None, None]
        for c in range(16):
            while f"ada{c}" not in ring.held:
                yield
            wt, got = ring.get(f"ada{c}")
            wt = wt.rearrange("p (k n) -> p k n", k=KD)
            a = acc[:, c % 2, :]
            yield
            m = dve(V.tensor_scalar, a, wt[:, 0, :], cact[:, 0:1], None, ALU.mult, after=[got, read[c % 2]])
            for k in range(1, KD):
                if k == 4:
                    yield
                m = dve(V.scalar_tensor_tensor, out=a, in0=wt[:, k, :], scalar=cact[:, k:k + 1], in1=a, op0=ALU.mult,
                        op1=ALU.add)
            ring.release(f"ada{c}", m)
            pe.wait(m)
            for e in range(3):
                t = matmul(ps[:, bm, 3 * c + e:3 * c + e + 1], a[:, e * P:(e + 1) * P], C("ones")[:, 0:1], start=True, stop=True)
            read[c % 2] = pe.mark(t)
            yield
        m = act(S.copy, mods[:, 48 * l:48 * l + 48], ps[:, bm, 0:48], after=[read[1]])
        bank.give(bm, m)

    ZA = 1024
    gates_flat = gates2.rearrange("p g n -> p (g n)")
    xt_flat = xt.rearrange("p k t -> p (k t)")
    stats = lambda n: stat[:, 64 + 48 * n:112 + 48 * n]
    z1 = zbuf[:, 0:NT * DIN1].rearrange("p (i n) -> p i n", i=NT)
    col_at, _ = spans(COLS1)
    ring.schedule(layer_tiles(0))
    for l in range(2):
        kept = columns(cols[:, l, :], col_at)
        if l == 0:
            rms_rows([], xn)
        else:
            rms_rows(join(), xn)
        m = turn_xn([dve.now()], kept("g_mix"), after_w=[] if l else [loaded_cols])
        pe.wait(m)
        tiles, marks = {}, {}
        for _ in project(z1, DIN1, "win", (0, 1, 2), tiles):
            pass
        if l == 0:
            cos, sin, rope_ready = rope_tables(posi[:, 0:NT], C("inv1"), 8, Carve(work, 20000), [loaded_const, loaded_pos])
            act(S.activation, cact, cact, ACT.Silu, after=[loaded_c])
        buf, got = ring.get("small")
        small = columns(buf, small1)
        rbuf, got_rows = ring.get("rows")
        rows = columns(rbuf, rows1)
        ready = [tiles[0], tiles[1], tiles[2], got, got_rows, act.now()] + join()
        w = Carve(work)
        w_mix, w_att = Carve(work[:, 0:13100]), Carve(work[:, 13100:20736])
        alternate((pe, act, dve), time_mix(z1, small, rows, tiles, ready, w_mix), project(z1, DIN1, "win", range(3, 8), tiles),
                  spatial_gating(z1, small, tiles, ready), sparse_attention(z1, small, tiles, ready, w_att),
                  modulation(l, Carve(work[:, 20736:21504])))
        done = join()
        work_done[0] = done
        ring.release("small", *done)
        ring.release("rows", *done)
        turned = turn_xn(done)
        m = out_project("wout", turned, add_residual)
        m = rms_rows(join(), xn)
        m = turn_xn([m], kept("g_ffn"), after_w=join())
        if l == 0:
            feed_forward(d["ffn"], 0, m, add_residual)
        else:
            routed_feed_forward(kept, m)
        ring.schedule(ple_tiles(l) + (layer_tiles(1) if l == 0 else []))
        m = rms_rows(join(), xn)
        m = turn_xn([m], kept("g_ple"))
        up, got_up = ring.get("ple_up")
        pT = up[:, 2 * D:2 * D + 2 * SEQ].rearrange("p (k t) -> p k t", k=2)
        tb = Carve(zbuf)
        sg = tb(2, COLS)
        pe.wait(m)
        free_sg = [[], []]
        for c in range(3):
            n = min(COLS, D - c * COLS)
            wt, got_w = ring.get(f"pleg{c}")
            wt = wt[:, 0:KD * n].rearrange("p (k n) -> p k n", k=KD)
            pe.wait(got_w, got_up)
            for i in range(NT):
                b = bank.take()
                for k in range(KD):
                    t = matmul(ps[:, b, 0:n], xt[:, k, i * P:(i + 1) * P], wt[:, k, :], start=(k == 0), stop=(k == KD - 1))
                t = pe.mark(t)
                m = act(S.activation, sg[:, i, 0:n], ps[:, b, 0:n], ACT.Sigmoid, after=[t] + free_sg[i])
                bank.give(b, m)
                b = bank.take()
                for k in range(2):
                    u = matmul(ps[:, b, 0:n], pT[:, k, i * P:(i + 1) * P], up[:, k * D + c * COLS:k * D + c * COLS + n],
                                 start=(k == 0), stop=(k == 1))
                u = pe.mark(u)
                m = dve(V.tensor_tensor, sg[:, i, 0:n], sg[:, i, 0:n], ps[:, b, 0:n], ALU.mult, after=[m, u])
                bank.give(b, m)
                hs = h[:, i, c * COLS:c * COLS + n]
                m = dve(V.tensor_tensor, hs, hs, sg[:, i, 0:n], ALU.add)
                free_sg[i] = [m]
            ring.release(f"pleg{c}", u)
        ring.release("ple_up", u)

    ring.schedule([("final1", [(d["g_final"][0:1].to_broadcast([P, D]), 0)])])
    gf, got = ring.get("final1")
    rms_rows(join(), xn)
    m = dve(V.tensor_tensor, h, xn, spread(gf[:, 0:D], 1, NT), ALU.mult, after=[got])
    ring.release("final1", m)

    z2 = zbuf[:, 0:NT * DIN2].rearrange("p (i n) -> p i n", i=NT)
    loaded_const = fetch(cst[:, 0:width2], d["const2"], after=join())
    const[0] = tab2
    for e in (dve, act, pe):
        e.wait(loaded_const)
    cos2, sin2, rope2 = rope_tables(posi[:, NT:2 * NT], C("inv2"), 32, Carve(zbuf), join())
    small2, n_small2 = spans(SMALL2)
    rows2, n_rows2 = spans(ROWS2, n_small2)
    small2.update(rows2)

    def layer2_tiles(l):
        out = [("small", [(d["small2"][l], 0), (d["rows2"][l:l + 1].to_broadcast([P, d["rows2"].shape[1]]), n_small2)])]
        for c in range(-(-DIN2 // COLS)):
            n = min(COLS, DIN2 - c * COLS)
            out.append((f"win{c}", [(d["w_in2"][l, c, :, 0:KD * n], 0)]))
        out += [(f"wout{c}", [(d["w_out2"][l, c], 0)]) for c in range(3)]
        return out

    def adaptive(l, small, got):
        mod, gains = mods[:, 48 * l:48 * l + 48], mods[:, 96:112]
        m = dve(V.tensor_tensor, mod, mod, small("ada_b"), ALU.add, after=[got] + join())
        for e, (sc_at, name) in enumerate(((8, "g_mix"), (32, "g_ffn"))):
            o = gains[:, 8 * e:8 * e + 8]
            dve(V.tensor_scalar, o, mod[:, sc_at:sc_at + 8], 1.0, None, ALU.add)
            dve(V.tensor_tensor, o, o, small(name), ALU.mult)
        rep = Carve(zbuf)(16, P)
        for g, at in enumerate((16, 40)):
            m = dve(V.tensor_copy, rep[:, 8 * g:8 * g + 8, :], spread(mod[:, at:at + 8], 2, P))
        pe.wait(m)
        for q in range(4):
            b = bank.take()
            for e in range(4):
                t = matmul(ps[:, b, e * P:(e + 1) * P], rep[:, 4 * q + e, :], C("ident"), start=True, stop=True)
            t = pe.mark(t)
            m = act(S.copy, gates_flat[:, 512 * q:512 * q + 512], bank[b], after=[t])
            bank.give(b, m)
        return gains, mod, m

    def fox(z, small, tiles, ready, w):
        while 3 not in tiles:
            yield
        ready, st = ready + [tiles[c] for c in range(1, 4)], stats(0)
        qT, kT = w(NT, 2, P), w(2, SEQ)
        lf, e1, cq, rep = w(NT, 4), w(NT, 4), w(NT, 4), w(NT * 4, P)
        ck, cm, sbuf, pt, o = w(4, SEQ), w(4, SEQ), w(4 * SEQ), w(8, P), w(4, HD)
        yield
        dve(V.tensor_tensor, lf, z[:, :, 1280:1284], spread(small("fb"), 1, NT), ALU.add, after=ready)
        yield
        dve(V.tensor_scalar, cq, lf, -1.0, None, ALU.mult)
        yield
        m = dve(V.tensor_tensor, e1, lf, cq, ALU.max)
        yield
        m = act(S.activation, e1, e1, ACT.Exp, scale=-1.0, after=[m])
        yield
        m = dve(V.tensor_scalar, e1, e1, 1.0, None, ALU.add, after=[m])
        yield
        m = act(S.activation, e1, e1, ACT.Ln, after=[m])
        yield
        dve(V.tensor_scalar, lf, lf, 0.0, None, ALU.min, after=[m])
        yield
        dve(V.tensor_tensor, lf, lf, e1, ALU.subtract)
        yield
        m = dve(V.tensor_copy, rep, spread(lf.rearrange("p i h -> p (i h)"), 2, P))
        yield
        pe.wait(m, *ready)
        while len(bank.order) < 1:
            yield
        b = bank.take()
        matmul(ps[:, b, 0:4], C("tri"), lf[:, 0, :], start=True, stop=True)
        matmul(ps[:, b, 4:8], C("tri"), lf[:, 1, :], start=True, stop=False)
        t = pe.mark(matmul(ps[:, b, 4:8], C("ones"), lf[:, 0, :], start=False, stop=True))
        yield
        m = dve(V.tensor_copy, cq, ps[:, b, 0:8].rearrange("p (i h) -> p i h", i=NT), after=[t])
        bank.give(b, m)
        for pair in range(2):
            while len(bank.order) < 1:
                yield
            b = bank.take()
            for e in range(2):
                hh = 2 * pair + e
                matmul(ps[:, b, e * SEQ:e * SEQ + P], rep[:, hh, :], C("tri"), start=True, stop=True)
                matmul(ps[:, b, e * SEQ + P:(e + 1) * SEQ], rep[:, 4 + hh, :], C("tri"), start=True, stop=False)
                t = matmul(ps[:, b, e * SEQ + P:(e + 1) * SEQ], rep[:, hh, :], C("ones"), start=False, stop=True)
            t = pe.mark(t)
            yield
            m = dve(V.tensor_copy, ck[:, 2 * pair:2 * pair + 2, :], bank[b].rearrange("p (a s) -> p a s", a=2), after=[t])
            bank.give(b, m)
            yield
        for which in range(2):
            while len(bank.order) < 1:
                yield
            b = bank.take()
            for pair in range(2):
                for i in range(NT):
                    t = transpose(b, (2 * pair + i) * P, z[:, i, 512 + 256 * which + pair * P:512 + 256 * which + (pair + 1) * P])
            t = pe.mark(t)
            src = bank[b].rearrange("p (a i t) -> p a i t", a=2, i=NT)
            if which == 0:
                yield
                m = act(S.mul, qT.rearrange("p i a t -> p a i t"), src, HD ** -0.5, after=[t])
            else:
                yield
                m = act(S.copy, kT.rearrange("p a (i t) -> p a i t", i=NT), src, after=[t])
            bank.give(b, m)
            yield
        turned = m
        last = [dve.now()]
        for i in range(NT):
            n = P * (i + 1)
            pe.wait(turned, *last)
            yield
            dve(V.tensor_tensor, cm[:, :, 0:n], spread(C("causal")[:, P * i:P * i + n], 1, 4), ck[:, :, 0:n], ALU.subtract,
                after=last)
            s4 = sbuf[:, 0:4 * n].rearrange("p (h s) -> p h s", h=4)
            for par in range(2):
                while len(bank.order) < 1:
                    yield
                b = bank.take()
                for a in range(2):
                    t = matmul(ps[:, b, a * n:(a + 1) * n], qT[64 * par:64 * par + 64, i, a, :],
                                 kT[64 * par:64 * par + 64, a, 0:n], start=True, stop=True)
                t = pe.mark(t)
                for a in range(2):
                    hh = 2 * a + par
                    yield
                    m = dve(V.scalar_tensor_tensor, out=s4[:, hh, :], in0=ps[:, b, a * n:(a + 1) * n],
                            scalar=cq[:, i, hh:hh + 1], in1=cm[:, hh, 0:n], op0=ALU.add, op1=ALU.add, after=[t])
                bank.give(b, m)
            yield
            rs, m = yield from softmax_rows(s4, 4, st)
            yield
            b, t = yield from weighted_values(s4, 4, i + 1, pt[:, 0:4 * (i + 1), :],
                                   lambda mm, st: z[:, st, 1024 + mm * HD:1024 + (mm + 1) * HD], m)
            yield
            m = dve(V.tensor_tensor, xn[:, i, 0:256].rearrange("p (h d) -> p h d", h=4),
                    ps[:, b, 0:256].rearrange("p (h d) -> p h d", h=4), spread(rs, 2, HD), ALU.mult, after=[t])
            bank.give(b, m)
            last = [m]
            yield

    def pooling(z, small, tiles, ready, w):
        while 4 not in tiles:
            yield
        ready = ready + [tiles[3], tiles[4]]
        dT = w(2, SEQ)
        band = C("band").rearrange("p (g n) -> p g n", g=4)
        pe.wait(*ready)
        while len(bank.order) < 1:
            yield
        b = bank.take()
        for g in range(4):
            o = ps[64 * (g % 2):64 * (g % 2) + 64, b, (g // 2) * SEQ:(g // 2 + 1) * SEQ]
            u0, u1 = (z[:, i, 1284 + g * HD:1284 + (g + 1) * HD] for i in range(NT))
            matmul(o[:, 0:P], u0, band[:, g, 0:P], start=True, stop=True)
            matmul(o[:, P:SEQ], u0, band[:, g, P:SEQ], start=True, stop=False)
            t = matmul(o[:, P:SEQ], u1, band[:, g, SEQ:SEQ + P], start=False, stop=True)
        t = pe.mark(t)
        yield
        m = act(S.copy, dT, bank[b].rearrange("p (a t) -> p a t", a=2), after=[t] + ready)
        bank.give(b, m)
        yield
        pe.wait(m)
        pw = small("pool_w").rearrange("p (a d) -> p a d", a=2)
        for par in range(2):
            while len(bank.order) < 1:
                yield
            b = bank.take()
            for i in range(NT):
                for a in range(2):
                    t = matmul(ps[:, b, (2 * i + a) * HD:(2 * i + a + 1) * HD], dT[64 * par:64 * par + 64, a, i * P:(i + 1) * P],
                                 pw[64 * par:64 * par + 64, a, :], start=True, stop=True)
            t = pe.mark(t)
            for i in range(NT):
                yield
                m = dve(V.tensor_tensor, xn[:, i, 256:512].rearrange("p (a b d) -> p a b d", a=2, b=2)[:, :, par, :],
                        ps[:, b, i * P:(i + 1) * P].rearrange("p (a d) -> p a d", a=2),
                        small("pool_scale").rearrange("p (a b d) -> p a b d", a=2, b=2)[:, :, par, :], ALU.mult, after=[t])
            bank.give(b, m)
            yield

    def retention(z, small, tiles, ready, w):
        while 6 not in tiles:
            yield
        ready, st_ = ready + [tiles[c] for c in range(4, 7)], stats(1)
        qk, tmp = w(2, NT, 256), w(1024)
        qT, kT, st, o, t1 = w(2, SEQ), w(2, SEQ), w(4, 384), w(NT, 256), w(NT, 256)
        hv = lambda ap: ap.rearrange("p i (h d) -> p i h d", h=4)
        for which in range(2):
            src = z[:, :, 1540 + 256 * which:1796 + 256 * which]
            m = yield from rotate(hv(qk[:, which]), hv(src), 4, 32, cos2, sin2, tmp, after=ready + [rope2])
            yield
        pe.wait(m)
        for which, dst in ((0, qT), (1, kT)):
            while len(bank.order) < 1:
                yield
            b = bank.take()
            for pair in range(2):
                for i in range(NT):
                    t = transpose(b, (2 * pair + i) * P, qk[:, which, i, pair * P:(pair + 1) * P])
            t = pe.mark(t)
            yield
            m = act(S.copy, dst, bank[b].rearrange("p (a t) -> p a t", a=2), after=[t])
            bank.give(b, m)
            yield
        pe.wait(m)
        dec = C("decay").rearrange("p (h n) -> p h n", h=4)
        for hh in range(4):
            lo_p = 64 * (hh % 2)
            while len(bank.order) < 1:
                yield
            b = bank.take()
            qh, kh = qT[lo_p:lo_p + 64, hh // 2, :], kT[lo_p:lo_p + 64, hh // 2, :]
            matmul(ps[:, b, 0:SEQ], kh[:, 0:P], qh, start=True, stop=True)
            t = pe.mark(matmul(ps[:, b, SEQ:SEQ + P], kh[:, P:SEQ], qh[:, P:SEQ], start=True, stop=True))
            yield
            m = dve(V.tensor_tensor, st[:, hh, :], ps[:, b, 0:384], dec[:, hh, :], ALU.mult, after=[t])
            bank.give(b, m)
            yield
        pe.wait(m)
        while len(bank.order) < 1:
            yield
        b = bank.take()
        for hh in range(4):
            v = lambda i: z[:, i, 2052 + hh * HD:2052 + (hh + 1) * HD]
            matmul(ps[:, b, hh * HD:(hh + 1) * HD], st[:, hh, 0:P], v(0), start=True, stop=True)
            matmul(ps[:, b, 256 + hh * HD:256 + (hh + 1) * HD], st[:, hh, P:SEQ], v(0), start=True, stop=False)
            t = matmul(ps[:, b, 256 + hh * HD:256 + (hh + 1) * HD], st[:, hh, SEQ:SEQ + P], v(1), start=False, stop=True)
        t = pe.mark(t)
        yield
        m = dve(V.tensor_copy, o, bank[b].rearrange("p (i n) -> p i n", i=NT), after=[t])
        bank.give(b, m)
        yield
        g = act(S.activation, tmp[:, 0:512].rearrange("p (i n) -> p i n", i=NT), z[:, :, 2308:2564], ACT.Silu,
                after=ready + [dve.now()])
        per_head = lambda ap: ap.rearrange("p i (h d) -> p (i h) d", h=4)
        yield
        yield from head_norm(per_head(o), 8, HD, 1e-6, per_head(t1), st_)
        yield
        dve(V.tensor_tensor, o, o, spread(small("gn_g"), 1, NT), ALU.mult)
        yield
        dve(V.tensor_tensor, xn[:, :, 512:768], o, tmp[:, 0:512].rearrange("p (i n) -> p i n", i=NT), ALU.mult,
            after=[g])

    def conformer(z, small, tiles, ready, w):
        while 1 not in tiles:
            yield
        ready, st = ready + [tiles[0], tiles[1]], stats(2)
        gl, padded, acc, y, t1 = w(NT, 256), w(2, CONVW - 1 + SEQ), w(2, SEQ), w(NT, 256), w(NT, 256)
        yield
        m = act(S.activation, gl, z[:, :, 256:512], ACT.Sigmoid, after=ready)
        yield
        m = dve(V.tensor_tensor, gl, gl, z[:, :, 0:256], ALU.mult, after=[m])
        yield
        dve(V.memset, padded[:, :, 0:CONVW - 1], 0.0)
        pe.wait(m)
        while len(bank.order) < 1:
            yield
        b = bank.take()
        for a in range(2):
            for i in range(NT):
                t = transpose(b, (2 * a + i) * P, gl[:, i, a * P:(a + 1) * P])
        t = pe.mark(t)
        yield
        m = act(S.copy, padded[:, :, CONVW - 1:], bank[b].rearrange("p (a t) -> p a t", a=2), after=[t, dve.now()])
        bank.give(b, m)
        cw = small("conv_w").rearrange("p (a j) -> p a j", a=2)
        for a in range(2):
            yield
            dve(V.tensor_scalar, acc[:, a, :], padded[:, a, 0:SEQ], cw[:, a, 0:1], small("conv_b")[:, a:a + 1],
                ALU.mult, ALU.add, after=[m])
        for j in range(1, CONVW):
            for a in range(2):
                yield
                m = dve(V.scalar_tensor_tensor, out=acc[:, a, :], in0=padded[:, a, j:j + SEQ], scalar=cw[:, a, j:j + 1],
                        in1=acc[:, a, :], op0=ALU.mult, op1=ALU.add)
            yield
        pe.wait(m)
        while len(bank.order) < 1:
            yield
        b = bank.take()
        for i in range(NT):
            for a in range(2):
                t = transpose(b, (2 * i + a) * P, acc[:, a, i * P:(i + 1) * P])
        t = pe.mark(t)
        yield
        m = dve(V.tensor_copy, y, bank[b].rearrange("p (i n) -> p i n", i=NT), after=[t])
        bank.give(b, m)
        yield
        yield from head_norm(y, NT, 256, 1e-6, t1, st)
        yield
        dve(V.tensor_tensor, y, y, spread(small("ln_g"), 1, NT), ALU.mult)
        yield
        m = dve(V.tensor_tensor, y, y, spread(small("ln_b"), 1, NT), ALU.add)
        yield
        act(S.activation, xn[:, :, 768:1024], y, ACT.Silu, after=[m])

    def gated_add(which):
        def add(i, q, src, t):
            tmp = xn[:, i, q * 512:(q + 1) * 512]
            dve(V.tensor_tensor, tmp, src, gates2[:, which, q * 512:(q + 1) * 512], ALU.mult, after=[t])
            hs = h[:, i, q * 512:(q + 1) * 512]
            return dve(V.tensor_tensor, hs, hs, tmp, ALU.add)
        return add

    for l in range(2):
        ring.schedule(layer2_tiles(l))
        buf, got = ring.get("small")
        small = columns(buf, small2)
        gains, mod, m = adaptive(l, small, got)
        rms_rows(join(), xn)
        m = turn_xn([dve.now()], gains[:, 0:8], mod[:, 0:8])
        pe.wait(m)
        tiles, marks = {}, {}
        ready = [m, got] + join()
        w = Carve(work)
        alternate((pe, act, dve), project(z2, DIN2, "win", range(7), tiles),
                  conformer(z2, small, tiles, ready, Carve(work[:, 0:2800])),
                  fox(z2, small, tiles, ready, Carve(work[:, 2800:9500])),
                  pooling(z2, small, tiles, ready, Carve(work[:, 9500:10100])),
                  retention(z2, small, tiles, ready, Carve(work[:, 10100:16000])))
        done = join()
        work_done[0] = done
        ring.release("small", *done)
        turned = turn_xn(done)
        m = out_project("wout", turned, gated_add(0))
        m = rms_rows(join(), xn)
        m = turn_xn([m], gains[:, 8:16], mod[:, 24:32], after_w=join())
        m = feed_forward(d["ffn2"], l * FB, m, gated_add(1))

    ring.schedule([("final2", [(d["g_final"][1:2].to_broadcast([P, D]), 0)])])
    gf, got = ring.get("final2")
    rms_rows(join(), xn)
    m = dve(V.tensor_tensor, xn, xn, spread(gf[:, 0:D], 1, NT), ALU.mult, after=[got])
    sp.wait(m)
    s_out = nc.alloc_semaphore("s_out")
    nc.sync.dma_start(d["out"], xn).then_inc(s_out, 16)
    nc.sync.wait_ge(s_out, 16)


def column_tiles(w, cols=COLS):
    L, _, n = w.shape
    t = -(-n // cols)
    out = np.zeros((L, t, P, KD * cols), np.float32)
    for c in range(t):
        m = min(cols, n - c * cols)
        out[:, c, :, 0:KD * m] = w[:, :, c * cols:c * cols + m].reshape(L, KD, P, m).transpose(0, 2, 1, 3).reshape(L, P, KD * m)
    return out


def row_tiles(w):
    L = w.shape[0]
    out = np.zeros((L, 3, P, 3, D), np.float32)
    blocks = w.reshape(L, KD, P, D)
    for k in range(KD):
        out[:, k // 3, :, k % 3] = blocks[:, k]
    return out.reshape(L, 3, P, 3 * D)


def ffn_tiles(w1, w3, w2):
    E = w1.shape[0]
    out = np.empty((E, FB, P, 3, D), np.float32)
    for e, w in enumerate((w1, w3)):
        out[:, :, :, e] = w.reshape(E, KD, P, FB, P).transpose(0, 3, 2, 1, 4).reshape(E, FB, P, D)
    out[:, :, :, 2] = w2.reshape(E, FB, P, D)
    return out.reshape(E * FB, P, 3 * D)


def by_partition(v):
    return v.reshape(v.shape[0], -1, P).transpose(0, 2, 1)


def pack(fields, values):
    return np.concatenate([np.asarray(values[n], np.float32).reshape(2, P, w) for n, w in fields], axis=2)


def pack_rows(fields, values):
    return np.concatenate([values[n].reshape(2, w) for n, w in fields], axis=1)


def lay_out(a):
    one, two = const_arrays()
    w_in = a["w_in"]
    zc = 1536
    q = w_in[:, :, zc:zc + 512].reshape(2, D, 2, 4, HD).transpose(0, 1, 3, 2, 4).reshape(2, D, 512)
    gates = w_in[:, :, zc + 1280:].reshape(2, D, 2, 4, 3).transpose(0, 1, 4, 3, 2).reshape(2, D, 24)
    w_in = np.concatenate([w_in[:, :, 512:zc], w_in[:, :, :512], q, w_in[:, :, zc + 512:zc + 1280], gates], axis=2)
    w_out = a["w_out"]
    tail = w_out[:, 512:].reshape(2, 2, 4, HD, D).transpose(0, 2, 1, 3, 4).reshape(2, 512, D)
    w_out = np.concatenate([w_out[:, :512], tail], axis=1)
    lora = np.zeros((2, P, 512), np.float32)
    lora[:, :64, :256] = a["rw_w_up"]
    lora[:, 64:, 256:] = a["rw_a_up"]
    pos = a["nsa_cmp_pos"].reshape(2, 16, 2, HD).transpose(0, 2, 3, 1).reshape(2, P, 16)
    router = a["router_w"].reshape(1, KD, P, NE).transpose(0, 2, 1, 3).reshape(1, P, KD * NE)
    small1 = pack(SMALL1, {
        "kc_w2": a["nsa_kc_w2"], "vc_w2": a["nsa_vc_w2"], "pos": pos, "lora": lora, "g_up": a["rw_g_up"],
        "wst": a["gm_ws"].transpose(0, 3, 1, 2).reshape(2, P, 512), "bs": a["gm_bs"].transpose(0, 2, 1)})
    rb = np.broadcast_to(a["router_b"][:, None, :], (1, P, NE))
    cols = pack(COLS1, {
        "g_mix": by_partition(a["g_mix"]), "g_ffn": by_partition(a["g_ffn"]), "g_ple": by_partition(a["g_ple"]),
        "router": np.concatenate([router, router]), "rb": np.concatenate([rb, rb])})
    rows1 = pack_rows(ROWS1, {"mu": a["rw_mu"], "wa0": np.concatenate([a["rw_w0"], a["rw_a0"]], 1), "k_k": a["rw_k_k"],
                              "k_a": a["rw_k_a"], "r_k": a["rw_r_k"], "gn_g": a["rw_gn_g"], "gn_b": a["rw_gn_b"]})
    rows1b = pack_rows(ROWS1B, {"ln_g": a["gm_ln_g"], "ln_b": a["gm_ln_b"]})
    cmp_w1 = lambda w: w.reshape(2, 16, P, P).transpose(0, 2, 1, 3).reshape(2, P, 2048)
    ple = np.concatenate([a["ple_proj_w"].reshape(2, 2, P, D).transpose(0, 2, 1, 3).reshape(2, P, 2 * D),
                          a["p"].reshape(2, SEQ, 2, P).transpose(0, 3, 2, 1).reshape(2, P, 2 * SEQ)], axis=2)
    ada_b = a["ada_b_2"]
    c = by_partition(a["c_2"])
    pool_w = a["pool_w_2"].reshape(2, 2, 2, HD, HD).transpose(0, 2, 3, 1, 4).reshape(2, P, 128)
    conv_w = a["conv_w_2"].reshape(2, CONVW, 2, P).transpose(0, 3, 2, 1).reshape(2, P, 62)
    small2 = pack(SMALL2, {
        "g_mix": by_partition(a["norm_mix_g_2"]), "g_ffn": by_partition(a["norm_ffn_g_2"]), "pool_w": pool_w,
        "conv_w": conv_w, "conv_b": by_partition(a["conv_b_2"]), "ada_b": by_partition(ada_b)})
    w_in2 = np.concatenate([a["w_in_2"][:, :, 2052:], a["w_in_2"][:, :, :2052]], axis=2)
    rows2 = pack_rows(ROWS2, {"pool_scale": a["pool_scale_2"], "gn_g": a["ret_gn_g_2"], "ln_g": a["conv_ln_g_2"],
                              "ln_b": a["conv_ln_b_2"], "fb": a["fox_fb_2"]})
    tokens = lambda v: v.reshape(NT, P).transpose(1, 0)
    return {
        "const1": np.concatenate(list(one.values()), 1), "const2": np.concatenate(list(two.values()), 1),
        "x": a["x"].reshape(NT, P, D).transpose(1, 0, 2),
        "pos": np.concatenate([tokens(a["positions"]), tokens(a["positions_2"])], 1),
        "small1": small1, "rows1": rows1, "rows1b": rows1b, "w_in": column_tiles(w_in), "w_out": row_tiles(w_out),
        "kc_w1": cmp_w1(a["nsa_kc_w1"]), "vc_w1": cmp_w1(a["nsa_vc_w1"]), "ple_proj": ple,
        "ple_gate": column_tiles(a["ple_gate_w"]), "ffn": ffn_tiles(a["ffn_w1"], a["ffn_w3"], a["ffn_w2"]),
        "moe": ffn_tiles(a["moe_w1"][0], a["moe_w3"][0], a["moe_w2"][0]),
        "g_final": np.concatenate([a["g_final"], a["final_g_2"]]).reshape(2, D),
        "small2": small2, "rows2": rows2, "cols": cols.transpose(1, 0, 2), "c": c[0], "ada": column_tiles(a["ada_w_2"]),
        "w_in2": column_tiles(w_in2), "w_out2": row_tiles(a["w_out_2"]),
        "ffn2": ffn_tiles(a["ffn_w1_2"], a["ffn_w3_2"], a["ffn_w2_2"]),
    }


def kernel(**inputs):
    import concourse.bacc as bacc
    from concourse.bass_utils import run_bass_kernel_spmd

    arrays = lay_out({k: np.asarray(v) for k, v in inputs.items()})
    nc = bacc.Bacc("TRN2", target_bir_lowering=False, num_devices=1)
    ins, d = {}, {}
    for name, v in arrays.items():
        v = np.ascontiguousarray(v)
        ins["in_" + name] = v
        d[name] = nc.dram_tensor("in_" + name, v.shape, mybir.dt.from_np(v.dtype), kind="ExternalInput").ap()
    d["out"] = nc.dram_tensor("out", (P, NT, D), F32, kind="ExternalOutput").ap()
    build(nc, d)
    r = run_bass_kernel_spmd(nc, [ins], core_ids=[0])
    out = r.results[0]["out"]
    return np.ascontiguousarray(out.transpose(1, 0, 2).reshape(1, SEQ, D))
```
